# Optimizing a Trainium2 kernel written in Bass

```python
import jax, jax.numpy as jnp
from jax import lax
import numpy as np

D_MODEL = 2048
BATCH = 1
SEQ = 256
DEPTH = 1

D_MIX = D_MODEL
D_LRU = D_MIX // 2
D_RET = D_MIX - D_LRU
LRU_BLOCKS = 8
LRU_BLOCK_W = D_LRU // LRU_BLOCKS
CONV_W = 4
LRU_C = 8.0
RET_HEADS = 8
RET_HD = D_RET // RET_HEADS
CHUNK = 128
ROPE_BASE = 10000.0
D_FF = ((8 * D_MODEL + 3 * 256 - 1) // (3 * 256)) * 256
EPS = 1e-6
SPLITS = (D_LRU, 2 * D_LRU, 2 * D_LRU + D_RET, 2 * D_LRU + 2 * D_RET, 2 * D_LRU + 3 * D_RET)
D_IN = 2 * D_LRU + 4 * D_RET


def rmsnorm(x, w):
    xf = x.astype(jnp.float32)
    y = xf * lax.rsqrt(jnp.mean(xf * xf, axis=-1, keepdims=True) + EPS)
    return (y * w.astype(jnp.float32)).astype(x.dtype)

def causal_depthwise_conv(x, w, b):
    S = x.shape[1]
    xp = jnp.pad(x, ((0, 0), (CONV_W - 1, 0), (0, 0)))
    y = b
    for tap in range(CONV_W):
        y = y + xp[:, tap:tap + S, :] * w[tap]
    return y

def rg_lru(u, wa, ba, wx, bx, lam):
    B, S, _ = u.shape
    uf = u.astype(jnp.float32)
    ub = uf.reshape(B, S, LRU_BLOCKS, LRU_BLOCK_W)
    r = jax.nn.sigmoid(jnp.einsum('bsnc,ncd->bsnd', ub, wa.astype(jnp.float32)).reshape(B, S, D_LRU) + ba)
    i = jax.nn.sigmoid(jnp.einsum('bsnc,ncd->bsnd', ub, wx.astype(jnp.float32)).reshape(B, S, D_LRU) + bx)
    log_a = LRU_C * r * jax.nn.log_sigmoid(lam.astype(jnp.float32))
    a = jnp.exp(log_a)
    b = jnp.sqrt(-jnp.expm1(2.0 * log_a)) * (i * uf)

    def combine(left, right):
        a1, b1 = left
        a2, b2 = right
        return a1 * a2, a2 * b1 + b2

    _, h = lax.associative_scan(combine, (a, b), axis=1)
    return h.astype(u.dtype)

def rope(t, cos, sin):
    half = t.shape[-1] // 2
    t1, t2 = t[..., :half], t[..., half:]
    c = cos[None, :, None, :]
    s = sin[None, :, None, :]
    return jnp.concatenate([t1 * c - t2 * s, t1 * s + t2 * c], axis=-1)

def retention(q, k, v, g, gn_w):
    B, S, _ = q.shape
    H, Dh, C = RET_HEADS, RET_HD, CHUNK
    N = S // C
    f32 = jnp.float32
    pos = jnp.arange(S, dtype=f32)
    inv_freq = ROPE_BASE ** (-jnp.arange(0, Dh, 2, dtype=f32) / Dh)
    ang = pos[:, None] * inv_freq[None, :]
    cos, sin = jnp.cos(ang), jnp.sin(ang)
    qh = rope(q.astype(f32).reshape(B, S, H, Dh), cos, sin)
    kh = rope(k.astype(f32).reshape(B, S, H, Dh), cos, sin) * (Dh ** -0.5)
    vh = v.astype(f32).reshape(B, S, H, Dh)
    qc = qh.reshape(B, N, C, H, Dh)
    kc = kh.reshape(B, N, C, H, Dh)
    vc = vh.reshape(B, N, C, H, Dh)

    log_gamma = jnp.log1p(-jnp.exp2(-5.0 - jnp.arange(H, dtype=f32)))
    idx = jnp.arange(C)
    diff = idx[:, None] - idx[None, :]
    causal = diff >= 0
    decay = jnp.where(causal[None], jnp.exp(log_gamma[:, None, None] * jnp.where(causal, diff, 0)[None].astype(f32)), 0.0)

    scores = jnp.einsum('bnqhd,bnkhd->bnhqk', qc, kc) * decay[None, None]
    inner = jnp.einsum('bnhqk,bnkhe->bnqhe', scores, vc)

    zeta = jnp.exp(log_gamma[None, :] * (C - 1 - idx).astype(f32)[:, None])
    kv = jnp.einsum('bnkhd,bnkhe->bnhde', kc * zeta[:, :, None], vc)
    chunk_decay = jnp.exp(log_gamma * C)[:, None, None]

    def step(R, kv_n):
        return R * chunk_decay + kv_n, R

    _, R_prev = lax.scan(step, jnp.zeros((B, H, Dh, Dh), f32), jnp.moveaxis(kv, 1, 0))
    R_prev = jnp.moveaxis(R_prev, 0, 1)

    xi = jnp.exp(log_gamma[None, :] * (idx + 1).astype(f32)[:, None])
    cross = jnp.einsum('bnqhd,bnhde->bnqhe', qc * xi[:, :, None], R_prev)
    o = (inner + cross).reshape(B, S, H, Dh)

    mu = jnp.mean(o, axis=-1, keepdims=True)
    var = jnp.mean(jnp.square(o - mu), axis=-1, keepdims=True)
    on = ((o - mu) * lax.rsqrt(var + EPS)).reshape(B, S, D_RET) * gn_w.astype(f32)
    return (jax.nn.silu(g.astype(f32)) * on).astype(q.dtype)

def first_inputs(seed: int = 0) -> dict:
    key = jax.random.key(seed)
    ks = jax.random.split(key, 20)
    f32 = jnp.float32

    def nrm(k, shape, scale):
        return jax.random.normal(k, shape, f32) * scale

    u = jax.random.uniform(ks[8], (DEPTH, D_LRU), f32, 0.9, 0.999)
    s = u ** (1.0 / LRU_C)
    lru_lambda = jnp.log(s) - jnp.log1p(-s)
    return {
        "x": nrm(ks[0], (BATCH, SEQ, D_MODEL), 1.0),
        "ln1_w": 1.0 + nrm(ks[1], (DEPTH, D_MODEL), 0.02),
        "w_in": nrm(ks[2], (DEPTH, D_MODEL, D_IN), D_MODEL ** -0.5),
        "conv_w": nrm(ks[3], (DEPTH, CONV_W, D_LRU), CONV_W ** -0.5),
        "conv_b": nrm(ks[4], (DEPTH, D_LRU), 0.01),
        "gate_a_w": nrm(ks[5], (DEPTH, LRU_BLOCKS, LRU_BLOCK_W, LRU_BLOCK_W), LRU_BLOCK_W ** -0.5),
        "gate_a_b": nrm(ks[6], (DEPTH, D_LRU), 0.01),
        "gate_x_w": nrm(ks[7], (DEPTH, LRU_BLOCKS, LRU_BLOCK_W, LRU_BLOCK_W), LRU_BLOCK_W ** -0.5),
        "gate_x_b": nrm(ks[9], (DEPTH, D_LRU), 0.01),
        "lru_lambda": lru_lambda,
        "ret_gn_w": 1.0 + nrm(ks[10], (DEPTH, D_RET), 0.02),
        "w_out": nrm(ks[11], (DEPTH, D_MIX, D_MODEL), D_MIX ** -0.5),
        "ln2_w": 1.0 + nrm(ks[12], (DEPTH, D_MODEL), 0.02),
        "w_ffn_gate": nrm(ks[13], (DEPTH, D_MODEL, D_FF), D_MODEL ** -0.5),
        "w_ffn_up": nrm(ks[14], (DEPTH, D_MODEL, D_FF), D_MODEL ** -0.5),
        "w_ffn_down": nrm(ks[15], (DEPTH, D_FF, D_MODEL), D_FF ** -0.5),
        "final_norm_w": 1.0 + nrm(ks[16], (D_MODEL,), 0.02),
    }

def first_block(x, ln1_w, w_in, conv_w, conv_b, gate_a_w, gate_a_b, gate_x_w, gate_x_b,
              lru_lambda, ret_gn_w, w_out, ln2_w, w_ffn_gate, w_ffn_up, w_ffn_down, final_norm_w):
    h = x
    for l in range(DEPTH):
        u = rmsnorm(h, ln1_w[l])
        proj = jnp.einsum('bsd,de->bse', u, w_in[l])
        lru_x, lru_g, q, k, v, ret_g = jnp.split(proj, SPLITS, axis=-1)
        lru_x = causal_depthwise_conv(lru_x, conv_w[l], conv_b[l])
        y_lru = rg_lru(lru_x, gate_a_w[l], gate_a_b[l], gate_x_w[l], gate_x_b[l], lru_lambda[l])
        y_lru = y_lru * jax.nn.gelu(lru_g)
        y_ret = retention(q, k, v, ret_g, ret_gn_w[l])
        y = jnp.concatenate([y_lru, y_ret], axis=-1)
        h = h + jnp.einsum('bse,ed->bsd', y, w_out[l])
        u = rmsnorm(h, ln2_w[l])
        ff = jax.nn.silu(jnp.einsum('bsd,df->bsf', u, w_ffn_gate[l])) * jnp.einsum('bsd,df->bsf', u, w_ffn_up[l])
        h = h + jnp.einsum('bsf,fd->bsd', ff, w_ffn_down[l])
    return rmsnorm(h, final_norm_w)


GRID_W = 64
CTX_LEN = 256

D_SGU = D_MODEL // 4
SGU_HEADS = 4
SGU_HD = D_SGU // SGU_HEADS
SGU_CHUNK = 128
D_MLSTM = D_MODEL // 2
MLSTM_HEADS = 4
MLSTM_HD = D_MLSTM // MLSTM_HEADS
MLSTM_CHUNK = 128
QK_CONV = 3
D_POOL = D_MODEL // 4
POOL_WINDOWS = (2, 4, 8, 16)
POOL_GC = D_POOL // len(POOL_WINDOWS)
N_GATES = 2 * 2 * MLSTM_HEADS

OFF_U = 0
OFF_V = OFF_U + D_SGU
OFF_P = OFF_V + D_SGU
OFF_Q = OFF_P + D_POOL
OFF_O = OFF_Q + D_MLSTM
OFF_K = OFF_O + D_MLSTM
OFF_VM = OFF_K + D_MLSTM
OFF_G = OFF_VM + D_MLSTM
D_IN_2 = OFF_G + N_GATES

N_KEYS = 128
N_EXPERTS = N_KEYS * N_KEYS
PEER_HEADS = 8
PEER_TOPK = 16
PEER_DK = 256
PEER_BLOCK = 128


def rmsnorm_2(x, g):
    xf = x.astype(jnp.float32)
    y = xf * lax.rsqrt(jnp.mean(xf * xf, axis=-1, keepdims=True) + EPS)
    return (y * g.astype(jnp.float32)).astype(x.dtype)

def ada_modulation(cond, w, b):
    m = jax.nn.silu(cond) @ w + b
    return jnp.split(m[:, None, :], 6, axis=-1)

def modulate(h, shift, scale):
    return h * (1 + scale) + shift

def chunk_sgu(u, v, g, w_s, b_s):
    B, T, _ = u.shape
    v = rmsnorm_2(v, g).reshape(B, T // SGU_CHUNK, SGU_CHUNK, SGU_HEADS, SGU_HD)
    mixed = jnp.einsum('hts,bcshd->bcthd', w_s, v) + b_s.T[None, None, :, :, None]
    return u * mixed.reshape(B, T, D_SGU)

def centred_dwconv(x, w):
    K, ch = w.shape
    pad = K // 2
    return lax.conv_general_dilated(x, w.astype(x.dtype)[:, None, :], window_strides=(1,),
                                    padding=[(pad, K - 1 - pad)],
                                    dimension_numbers=('NWC', 'WIO', 'NWC'), feature_group_count=ch)

def to_heads(a):
    B, T, _ = a.shape
    return a.reshape(B, T, MLSTM_HEADS, MLSTM_HD).transpose(0, 2, 1, 3)

def mlstm_inputs(q_raw, k_raw, v_raw, g_raw, conv_w, b_gate):
    k = to_heads(jax.nn.silu(centred_dwconv(k_raw, conv_w[:, D_MLSTM:])))
    v = to_heads(v_raw)
    B, T, _ = g_raw.shape
    g = (g_raw + b_gate).astype(jnp.float32).reshape(B, T, 2, 2, MLSTM_HEADS)
    g = g.transpose(2, 3, 0, 4, 1)
    q = None if q_raw is None else to_heads(jax.nn.silu(centred_dwconv(q_raw, conv_w[:, :D_MLSTM])))
    return q, k, v, g

def to_chunks(a):
    B, H, T = a.shape[:3]
    a = a.reshape((B, H, T // MLSTM_CHUNK, MLSTM_CHUNK) + a.shape[3:])
    return jnp.moveaxis(a, 2, 0)

def zero_state(batch):
    return (jnp.zeros((batch, MLSTM_HEADS, MLSTM_HD, MLSTM_HD), jnp.float32),
            jnp.zeros((batch, MLSTM_HEADS, MLSTM_HD), jnp.float32),
            jnp.zeros((batch, MLSTM_HEADS), jnp.float32))

def mlstm_scan(q, k, v, ig, fg, state, with_outputs):
    L = MLSTM_CHUNK
    causal = jnp.tril(jnp.ones((L, L), bool))
    kf = k.astype(jnp.float32) * (MLSTM_HD ** -0.5)
    xs = [to_chunks(a) for a in (kf, v.astype(jnp.float32), ig, fg)]
    if with_outputs:
        xs.append(to_chunks(q.astype(jnp.float32)))

    def step(carry, inp):
        C, n, m = carry
        kc, vc, ic, fc = inp[:4]
        b = jnp.cumsum(jax.nn.log_sigmoid(fc), axis=-1)
        b_last = b[..., -1]
        g = b_last[..., None] - b + ic
        m_new = jnp.maximum(b_last + m, g.max(-1))
        wk = jnp.exp(g - m_new[..., None])
        decay = jnp.exp(b_last + m - m_new)
        C_new = decay[..., None, None] * C + jnp.einsum('bhsv,bhsk->bhvk', vc * wk[..., None], kc)
        n_new = decay[..., None] * n + jnp.einsum('bhs,bhsk->bhk', wk, kc)
        if not with_outputs:
            return (C_new, n_new, m_new), None
        qc = inp[4]
        log_w = jnp.where(causal, b[..., :, None] - b[..., None, :] + ic[..., None, :], -jnp.inf)
        inter = b + m[..., None]
        m_t = jnp.maximum(inter, log_w.max(-1))
        w_prev = jnp.exp(inter - m_t)
        s = jnp.einsum('bhtd,bhsd->bhts', qc, kc) * jnp.exp(log_w - m_t[..., None])
        num = jnp.einsum('bhts,bhsv->bhtv', s, vc) + w_prev[..., None] * jnp.einsum('bhvk,bhtk->bhtv', C, qc)
        den = s.sum(-1) + w_prev * jnp.einsum('bhk,bhtk->bht', n, qc)
        h = num / jnp.maximum(jnp.abs(den), jnp.exp(-m_t))[..., None]
        return (C_new, n_new, m_new), h

    state, hs = lax.scan(step, state, tuple(xs))
    if not with_outputs:
        return None, state
    B, H, T, Dh = v.shape
    return jnp.moveaxis(hs, 0, 2).reshape(B, H, T, Dh), state

def mlstm_bidir(q, k, v, g, states, with_outputs):
    flip = lambda a: None if a is None else jnp.flip(a, axis=2)
    h_f, st_f = mlstm_scan(q, k, v, g[0, 0], g[0, 1], states[0], with_outputs)
    h_b, st_b = mlstm_scan(flip(q), flip(k), flip(v), flip(g[1, 0]), flip(g[1, 1]), states[1], with_outputs)
    h = h_f + jnp.flip(h_b, axis=2) if with_outputs else None
    return h, (st_f, st_b)

def mlstm_out(h, o_raw, g_norm, dtype):
    B, H, T, Dh = h.shape
    hn = h * lax.rsqrt(jnp.mean(h * h, axis=-1, keepdims=True) + EPS)
    hn = hn.transpose(0, 2, 1, 3).reshape(B, T, D_MLSTM) * g_norm.astype(jnp.float32)
    return (jax.nn.sigmoid(o_raw.astype(jnp.float32)) * hn).astype(dtype)

def window_bounds(n, w):
    idx = jnp.arange(n)
    return jnp.clip(idx - w // 2, 0, n), jnp.clip(idx - w // 2 + w, 0, n)

def grid_window_mean(x, rows, cols, w):
    B, T, ch = x.shape
    s = jnp.cumsum(jnp.cumsum(x.astype(jnp.float32).reshape(B, rows, cols, ch), axis=1), axis=2)
    s = jnp.pad(s, ((0, 0), (1, 0), (1, 0), (0, 0)))
    rlo, rhi = window_bounds(rows, w)
    clo, chi = window_bounds(cols, w)
    box = lambda r, c: jnp.take(jnp.take(s, r, axis=1), c, axis=2)
    tot = box(rhi, chi) - box(rlo, chi) - box(rhi, clo) + box(rlo, clo)
    cnt = ((rhi - rlo)[:, None] * (chi - clo)[None, :]).astype(jnp.float32)
    return (tot / cnt[None, :, :, None]).reshape(B, T, ch)

def pool_mixer(x, rows, cols, w_g, scale):
    B, T, _ = x.shape
    xg = x.reshape(B, T, len(POOL_WINDOWS), POOL_GC)
    means = jnp.stack([grid_window_mean(xg[:, :, i], rows, cols, w) for i, w in enumerate(POOL_WINDOWS)], axis=2)
    d = (means - xg.astype(jnp.float32)).astype(x.dtype)
    y = jnp.einsum('btgc,gcd->btgd', d, w_g)
    return y.reshape(B, T, D_POOL) * scale

def stream_mixers(p, h_mlstm, rows, cols, sgu_norm, sgu_w, sgu_b, mlstm_norm, pool_w, pool_scale):
    u = jax.nn.gelu(p[..., OFF_U:OFF_V])
    v = jax.nn.gelu(p[..., OFF_V:OFF_P])
    y_a = chunk_sgu(u, v, sgu_norm, sgu_w, sgu_b)
    y_b = mlstm_out(h_mlstm, p[..., OFF_O:OFF_K], mlstm_norm, p.dtype)
    y_c = pool_mixer(p[..., OFF_P:OFF_Q], rows, cols, pool_w, pool_scale)
    return jnp.concatenate([y_a, y_b, y_c], axis=-1)

def peer_ffn(h, wq, keys, u_tab, v_tab):
    B, T, D = h.shape
    ht = h.reshape(B * T, D)
    n = B * T
    q = (ht @ wq).astype(jnp.float32).reshape(n, PEER_HEADS, 2, PEER_DK // 2)
    s = jnp.einsum('nhpc,pkc->nhpk', q, keys.astype(jnp.float32))
    s1, i1 = lax.top_k(s[:, :, 0], PEER_TOPK)
    s2, i2 = lax.top_k(s[:, :, 1], PEER_TOPK)
    cand = (s1[..., :, None] + s2[..., None, :]).reshape(n, PEER_HEADS, PEER_TOPK * PEER_TOPK)
    sc, ci = lax.top_k(cand, PEER_TOPK)
    e = (jnp.take_along_axis(i1, ci // PEER_TOPK, axis=-1) * N_KEYS
         + jnp.take_along_axis(i2, ci % PEER_TOPK, axis=-1))
    gate = jax.nn.softmax(sc, axis=-1)
    nb = n // PEER_BLOCK

    def block(args):
        xb, eb, gb = args
        a = jnp.einsum('nd,nhkd->nhk', xb, jnp.take(u_tab, eb, axis=0))
        w = (gb * jax.nn.gelu(a.astype(jnp.float32))).astype(xb.dtype)
        return jnp.einsum('nhk,nhkd->nd', w, jnp.take(v_tab, eb, axis=0))

    out = lax.map(block, (ht.reshape(nb, PEER_BLOCK, D),
                          e.reshape(nb, PEER_BLOCK, PEER_HEADS, PEER_TOPK),
                          gate.reshape(nb, PEER_BLOCK, PEER_HEADS, PEER_TOPK)))
    return out.reshape(B, T, D)

def second_inputs(seed: int = 0) -> dict:
    key = jax.random.key(seed)
    ks = jax.random.split(key, 24)
    L, D = DEPTH, D_MODEL
    nrm = lambda k, shape, s: jax.random.normal(k, shape, jnp.float32) * s
    gate_base = jnp.array([0.0, 3.0], jnp.float32)[None, None, :, None]
    return {
        'x': nrm(ks[0], (BATCH, SEQ, D), 1.0),
        'c': nrm(ks[1], (BATCH, D), 1.0),
        'ctx': nrm(ks[2], (BATCH, CTX_LEN, D), 1.0),
        'c_ctx': nrm(ks[3], (D,), 1.0),
        'ada_w': nrm(ks[4], (L, D, 6 * D), 0.5 * D ** -0.5),
        'ada_b': nrm(ks[5], (L, 6 * D), 0.02),
        'norm_mix': 1.0 + nrm(ks[6], (L, D), 0.05),
        'norm_ffn': 1.0 + nrm(ks[7], (L, D), 0.05),
        'w_in': nrm(ks[8], (L, D, D_IN_2), D ** -0.5),
        'b_gate': (gate_base + nrm(ks[9], (L, 2, 2, MLSTM_HEADS), 0.1)).reshape(L, N_GATES),
        'sgu_norm': 1.0 + nrm(ks[10], (L, D_SGU), 0.05),
        'sgu_w': nrm(ks[11], (L, SGU_HEADS, SGU_CHUNK, SGU_CHUNK), SGU_CHUNK ** -0.5),
        'sgu_b': 1.0 + nrm(ks[12], (L, SGU_HEADS, SGU_CHUNK), 0.1),
        'qk_conv': nrm(ks[13], (L, QK_CONV, 2 * D_MLSTM), QK_CONV ** -0.5),
        'mlstm_norm': 1.0 + nrm(ks[14], (L, D_MLSTM), 0.05),
        'pool_w': nrm(ks[15], (L, len(POOL_WINDOWS), POOL_GC, POOL_GC), POOL_GC ** -0.5),
        'pool_scale': 1.0 + nrm(ks[16], (L, D_POOL), 0.1),
        'w_out': nrm(ks[17], (L, D, D), D ** -0.5),
        'peer_wq': nrm(ks[18], (L, D, PEER_HEADS * PEER_DK), D ** -0.5),
        'peer_keys': nrm(ks[19], (L, 2, N_KEYS, PEER_DK // 2), (PEER_DK // 2) ** -0.5),
        'peer_u': nrm(ks[20], (L, N_EXPERTS, D), D ** -0.5),
        'peer_v': nrm(ks[21], (L, N_EXPERTS, D), 0.25),
        'norm_final': 1.0 + nrm(ks[22], (D,), 0.05),
    }

def second_block(x, c, ctx, c_ctx, ada_w, ada_b, norm_mix, norm_ffn, w_in, b_gate, sgu_norm, sgu_w, sgu_b,
              qk_conv, mlstm_norm, pool_w, pool_scale, w_out, peer_wq, peer_keys, peer_u, peer_v, norm_final):
    rows = x.shape[1] // GRID_W
    ctx_len = ctx.shape[1]
    x_lat, x_ctx = x, ctx
    for l in range(DEPTH):
        last = l == DEPTH - 1
        m_lat = ada_modulation(c, ada_w[l], ada_b[l])
        m_ctx = ada_modulation(c_ctx[None, :], ada_w[l], ada_b[l])
        mix_args = (sgu_norm[l], sgu_w[l], sgu_b[l], mlstm_norm[l], pool_w[l], pool_scale[l])

        hc = modulate(rmsnorm_2(x_ctx, norm_mix[l]), m_ctx[0], m_ctx[1])
        if last:
            pk = hc @ w_in[l][:, OFF_K:]
            _, kc, vc, gc = mlstm_inputs(None, pk[..., :D_MLSTM], pk[..., D_MLSTM:2 * D_MLSTM],
                                          pk[..., 2 * D_MLSTM:], qk_conv[l], b_gate[l])
            _, ctx_states = mlstm_bidir(None, kc, vc, gc, (zero_state(x.shape[0]), zero_state(x.shape[0])), False)
        else:
            pc = hc @ w_in[l]
            qc, kc, vc, gc = mlstm_inputs(pc[..., OFF_Q:OFF_O], pc[..., OFF_K:OFF_VM], pc[..., OFF_VM:OFF_G],
                                          pc[..., OFF_G:], qk_conv[l], b_gate[l])
            h_c, ctx_states = mlstm_bidir(qc, kc, vc, gc, (zero_state(x.shape[0]), zero_state(x.shape[0])), True)
            y_c = stream_mixers(pc, h_c, 1, ctx_len, *mix_args)
            x_ctx_new = x_ctx + m_ctx[2] * (y_c @ w_out[l])
            hf = modulate(rmsnorm_2(x_ctx_new, norm_ffn[l]), m_ctx[3], m_ctx[4])
            x_ctx_new = x_ctx_new + m_ctx[5] * peer_ffn(hf, peer_wq[l], peer_keys[l], peer_u[l], peer_v[l])

        hl = modulate(rmsnorm_2(x_lat, norm_mix[l]), m_lat[0], m_lat[1])
        pl = hl @ w_in[l]
        ql, kl, vl, gl = mlstm_inputs(pl[..., OFF_Q:OFF_O], pl[..., OFF_K:OFF_VM], pl[..., OFF_VM:OFF_G],
                                      pl[..., OFF_G:], qk_conv[l], b_gate[l])
        h_l, _ = mlstm_bidir(ql, kl, vl, gl, ctx_states, True)
        y_l = stream_mixers(pl, h_l, rows, GRID_W, *mix_args)
        x_lat = x_lat + m_lat[2] * (y_l @ w_out[l])
        hf = modulate(rmsnorm_2(x_lat, norm_ffn[l]), m_lat[3], m_lat[4])
        x_lat = x_lat + m_lat[5] * peer_ffn(hf, peer_wq[l], peer_keys[l], peer_u[l], peer_v[l])

        if not last:
            x_ctx = x_ctx_new
    return rmsnorm_2(x_lat, norm_final)


def setup_inputs(seed=0):
    out = dict(first_inputs(seed))
    for name, value in second_inputs(seed + 1).items():
        if name != "x":
            out[name + "_2"] = value
    return out


def reference(
    x, ln1_w, w_in, conv_w, conv_b, gate_a_w, gate_a_b, gate_x_w, gate_x_b, lru_lambda,
    ret_gn_w, w_out, ln2_w, w_ffn_gate, w_ffn_up, w_ffn_down, final_norm_w, c_2, ctx_2, c_ctx_2,
    ada_w_2, ada_b_2, norm_mix_2, norm_ffn_2, w_in_2, b_gate_2, sgu_norm_2, sgu_w_2, sgu_b_2,
    qk_conv_2, mlstm_norm_2, pool_w_2, pool_scale_2, w_out_2, peer_wq_2, peer_keys_2, peer_u_2,
    peer_v_2, norm_final_2,
):
    x = first_block(
        x, ln1_w, w_in, conv_w, conv_b, gate_a_w, gate_a_b, gate_x_w, gate_x_b, lru_lambda,
        ret_gn_w, w_out, ln2_w, w_ffn_gate, w_ffn_up, w_ffn_down, final_norm_w,
    )
    return second_block(
        x, c_2, ctx_2, c_ctx_2, ada_w_2, ada_b_2, norm_mix_2, norm_ffn_2, w_in_2, b_gate_2,
        sgu_norm_2, sgu_w_2, sgu_b_2, qk_conv_2, mlstm_norm_2, pool_w_2, pool_scale_2, w_out_2,
        peer_wq_2, peer_keys_2, peer_u_2, peer_v_2, norm_final_2,
    )


_drawn_inputs = setup_inputs


def setup_inputs(seed=0):
    import zlib

    import numpy as np

    out = dict(_drawn_inputs(seed))
    spreads = {}
    factors = {'ln1_w': 2.794,
     'conv_b': 3.105,
     'gate_a_b': 64.0,
     'gate_x_b': 55.733,
     'ret_gn_w': 6.287,
     'ln2_w': 3.99,
     'final_norm_w': 2.784,
     'ctx_2': 4.078,
     'c_ctx_2': 4.571,
     'ada_b_2': 2.953,
     'norm_mix_2': 4.089,
     'norm_ffn_2': 18.908,
     'sgu_norm_2': 8.0,
     'sgu_b_2': 4.675,
     'mlstm_norm_2': 42.419,
     'pool_scale_2': 3.384,
     'qk_conv_2': 3.285}
    for name, (base, spread) in spreads.items():
        noise = np.random.default_rng([zlib.crc32(name.encode()), seed]).standard_normal(out[name].shape)
        drawn = base * np.exp(spread * noise) if base else spread * noise
        out[name] = __import__('jax').numpy.asarray(drawn.astype(out[name].dtype))
    for name, factor in factors.items():
        out[name] = (out[name] * factor).astype(out[name].dtype)
    return out
```

```python
from contextlib import ExitStack

import numpy as np
import concourse.bass as bass
from concourse import mybir

ALU = mybir.AluOpType
ACT = mybir.ActivationFunctionType
AX = mybir.AxisListType
F32 = mybir.dt.float32
F32R = mybir.dt.float32r
U32 = mybir.dt.uint32
I32 = mybir.dt.int32

P = 128
NB = 2
T = NB * P
D = 2048
KT = D // P
EPS = 1e-6
CW = 512
CK = 4
CPT = KT // CK
SLOTS_W = 4
LEAD = 2

D_LRU = 1024
LB = D_LRU // P
CONV_W = 4
LRU_C = 8.0
HEADS = 8
W_IN_TILES = 6144 // CW
D_FF = 5632
FT = D_FF // CW
C_Q, C_V, C_G = 2048, 4096, 5120

D_SGU = 512
SH = 4
PW = (2, 4, 8, 16)
GRID_W = 64
MH = 4
MD = 256
MKT = MD // P
D_ML = MH * MD
MB = D_ML // P
O_U, O_V, O_P, O_Q, O_O, O_K, O_VM, O_G = 0, 512, 1024, 1536, 2560, 3584, 4608, 5632
W2_TILES = O_G // CW
CTX_TILES = 2 * D_ML // CW
NG = 16
VA = MD + 1
NKEY = 128
PH = 8
TOPK = 16
SLOTS = PH * TOPK
GATH = 8
GSTEP = 2 * GATH
LOWEST = -3.0e38
ADA_TILES = 6 * D // CW
ADA_STEP = 2
OUT_TILES = D // CW
FF_FIRST = "gggg" + "uauauaua" + "aaaa"
FF_STEP = "gggg" + "uauauaua" + "dadadaad"
FF_LAST = "aad" * 4

S_IN = 0
S_OUT = S_IN + W_IN_TILES * CPT
S_FFN = S_OUT + OUT_TILES * CPT
S_STEP = S_FFN + len(FF_FIRST)
S_LAST = S_STEP + (FT - 1) * len(FF_STEP)
S_CTX = S_LAST + len(FF_LAST)
S_IN2 = S_CTX + CTX_TILES * CPT
S_OUT2 = S_IN2 + W2_TILES * CPT
S_WQ = S_OUT2 + OUT_TILES * CPT
NCH = S_WQ + OUT_TILES * CPT

Q_IN = 0
Q_OUT = Q_IN + W_IN_TILES
Q_FFN = Q_OUT + OUT_TILES
Q_CTX = Q_FFN + 2 * FT
Q_IN2 = Q_CTX + CTX_TILES
Q_OUT2 = Q_IN2 + W2_TILES
Q_WQ = Q_OUT2 + OUT_TILES

COL, NCOL = {}, 0
for _name, _w in (("ln1", KT), ("ln2", KT), ("ba", LB), ("bx", LB), ("conv", CONV_W * LB), ("convb", LB), ("lam", LB),
                  ("gnw", HEADS), ("nmix", KT), ("nffn", KT), ("ada_b", 6 * KT), ("qkconv", 3 * 2 * MB), ("mlnorm", MB),
                  ("pscale", len(PW)), ("c", KT), ("cctx", KT), ("sgub", SH), ("bgate", 4), ("xi", HEADS),
                  ("zeta", HEADS), ("sel", 2), ("iota", TOPK)):
    COL[_name] = (NCOL, _w)
    NCOL += _w

C1 = {"wa": 0, "wx": 1024, "decay": 2048, "rope": 3072, "_": 3584}
C2 = {"pool": 0, "sguw": 2048, "poolw": 2560, "keys": 3072, "mask": 3328, "_": 3584}


def lin(const, i=None, step=0):
    return const if i is None else i * step + const


def build(nc, a, out, until=99):
    with ExitStack() as ctx:
        sems = {}

        def sem(name):
            if name not in sems:
                sems[name] = ctx.enter_context(nc.semaphore(name))
            return sems[name]

        class Chain:

            def __init__(self, eng, name):
                self.eng, self.sem, self.n = eng, sem(name), 0

            def mark(self, ins):
                self.n += 1
                ins.then_inc(self.sem, 1)

            def sync(self):
                self.eng.wait_ge(self.sem, self.n)

            def __call__(self, ins):
                self.mark(ins)
                self.sync()

        region, words = {}, 0
        for name, n in (("ident", P), ("cols", 512), ("modt", 12 * KT), ("small", 512), ("X", NB * D), ("UH", KT * T),
                        ("UL", KT * T), ("RAW", SLOTS_W * D), ("WH", SLOTS_W * D), ("P", 12288),
                        ("TMP", 6176), ("C", 3584), ("MISC", 1120)):
            region[name] = words
            words += n
        arena = ctx.enter_context(nc.sbuf_tensor("arena", [P, words], F32))
        arena_at = nc.lookup_mloc(arena).addr

        def view(name, where, off, shape, dt=F32):
            return nc.alloc_sbuf_tensor_at(name, [P] + shape, dt, offset=arena_at + 4 * (region[where] + off))

        ident = view("ident", "ident", 0, [P])
        cols = view("cols", "cols", 0, [512])
        modt = view("modt", "modt", 0, [6 * KT, 2])
        X = view("X", "X", 0, [NB, D])
        UH = view("UH", "UH", 0, [KT, T], F32R)
        UL = view("UL", "UL", 0, [KT, T], F32R)
        raw = view("raw", "RAW", 0, [SLOTS_W, CK * CW])
        WH = view("WH", "WH", 0, [SLOTS_W, CK * CW], F32R)
        WL = view("WL", "RAW", 0, [SLOTS_W, CK * CW], F32R)
        bank = [ctx.enter_context(nc.psum_tensor(f"bank{i}", [P, CW], F32)) for i in range(8)]
        ACC = [bank[0:2], bank[2:4]]
        DB = bank[4:8]
        ALLB = DB + bank[0:4]

        small_at = [0]

        def tiny(name, shape, dt=F32):
            n = int(np.prod(shape))
            v = view(name, "small", small_at[0], shape, dt)
            small_at[0] += -(-n // 8) * 8
            assert small_at[0] <= 512
            return v

        def col(name, j=0, n=1, rows=P):
            o, w = COL[name]
            assert j + n <= w
            return cols[0:rows, o + j:o + j + n]

        ss = tiny("ss", [NB])
        ms = tiny("ms", [NB])
        rms = tiny("rms", [NB])
        rinv = tiny("rinv", [NB])
        sc_mix = tiny("sc_mix", [2, KT])
        sc_ffn = tiny("sc_ffn", [KT])
        csil = tiny("csil", [KT, 2])
        lam_t = [tiny(f"lam_t{i}", [LB]) for i in range(5)]
        p_col = tiny("p_col", [LB])
        n_col = tiny("n_col", [LB])
        gn = [tiny(f"gn{i}", [NB * HEADS]) for i in range(3)]

        raw_landed = [sem(f"raw_landed{s}") for s in range(SLOTS_W)]
        hi_ready, lo_ready, split_used = sem("hi_ready"), sem("lo_ready"), sem("split_used")
        acc_free_act, acc_free_dve = sem("acc_free_act"), sem("acc_free_dve")

        Pin = view("Pin", "P", 0, [NB, 6144])
        XN = view("XN", "TMP", 0, [NB, D])
        mod_tmp = view("mod_tmp", "MISC", 0, [2, T])
        wa = view("wa", "C", C1["wa"], [LB, P])
        wx = view("wx", "C", C1["wx"], [LB, P])
        decay = view("decay", "C", C1["decay"], [HEADS, P])
        rope = view("rope", "C", C1["rope"], [NB, 2, P // 2])
        lru_x = view("lru_x", "TMP", 0, [LB, T + CONV_W - 1])
        lru_b = view("lru_b", "TMP", 0, [LB, T])
        lru_u = view("lru_u", "TMP", LB * (T + CONV_W - 1), [LB, T])
        lru_g = view("lru_g", "TMP", LB * (2 * T + CONV_W - 1), [LB, T])
        rt = [view(f"rt{i}", "TMP", 1024 * i, [KT, P // 2]) for i in range(4)]
        ret_s = view("ret_s", "TMP", 0, [HEADS, NB, P])
        ret_kz = view("ret_kz", "TMP", 2048, [HEADS, P])
        ret_r = view("ret_r", "TMP", 3072, [HEADS, P])
        ret_o = view("ret_o", "TMP", 4096, [NB, HEADS, P])
        ret_sq = view("ret_sq", "TMP", 0, [NB, HEADS, P])
        FH = view("FH", "P", 0, [CK, T], F32R)
        FL = view("FL", "P", 1024, [CK, T], F32R)
        ff_g = view("ff_g", "P", 2048, [NB, CW])
        ff = view("ff", "P", 3072, [NB, CW])
        fnw = view("fnw", "P", 4096, [D])
        cond = view("cond", "P", 8192, [KT, P], F32R)
        ada_rows = view("ada_rows", "P", 10240, [ADA_STEP, CW])

        def half(j):
            return lambda b: Pin[:, b // 4, 1024 * j + (b % 4) * T:1024 * j + (b % 4 + 1) * T]

        def wide(j):
            return Pin[:, :, 1024 * j:1024 * (j + 1)]

        pool_t = view("pool_t", "C", C2["pool"], [len(PW), NB, T])
        sgu_w = view("sgu_w", "C", C2["sguw"], [SH, P])
        pool_w = view("pool_w", "C", C2["poolw"], [len(PW), P])
        keys = view("keys", "C", C2["keys"], [2, NKEY])
        mask = view("mask", "C", C2["mask"], [2, P])
        wg = view("wg", "MISC", 776, [KT, NG])
        ctx_x = view("ctx_x", "P", 0, [NB, D])
        ctx_n = view("ctx_n", "P", D * NB, [NB, D])
        kv = view("kv", "P", 0, [NB, 2 * D_ML])
        c_pad = view("c_pad", "P", 4096, [MB, T + 2])
        c_k = view("c_k", "P", 6160, [MB, T])
        c_ktok = view("c_ktok", "P", 8208, [NB, D_ML])
        c_v1 = view("c_v1", "P", 4096, [NB, MH, VA])
        c_rows = [view(f"c_rows{i}", "TMP", 4112 + 512 * i, [2, T]) for i in range(4)] + [view("c_rows4", "P", 10256, [2, T])]
        st = view("st", "TMP", 0, [2, MH, MKT, VA])
        P2 = view("P2", "P", 0, [NB, O_G])
        XN2 = view("XN2", "P", 0, [NB, D])
        l_pad = view("l_pad", "TMP", 4112, [MB, T + 2])
        l_v1 = view("l_v1", "TMP", 4112, [NB, MH, VA])
        pool_d = view("pool_d", "TMP", 4112, [len(PW), T])
        sc_t = view("sc_t", "P", NB * O_G, [MH, NB, P])
        sgu_n = view("sgu_n", "P", NB * O_G, [D_SGU])
        sgu_sq = view("sgu_sq", "P", NB * O_G + D_SGU, [D_SGU])
        ml_t = view("ml_t", "MISC", 0, [2, VA])
        vw = view("vw", "MISC", 0, [2, VA])
        wb = view("wb", "MISC", 520, [2, P])
        gb1 = view("gb1", "TMP", 0, [D])
        gb2 = view("gb2", "TMP", D, [D])
        g_tmp = view("g_tmp", "MISC", 0, [NB, CW])
        sc_row = view("sc_row", "P", 4096, [D])
        sh_row = view("sh_row", "P", 6144, [D])
        q_tok = view("q_tok", "P", 8192, [NB, D])
        q_t = view("q_t", "P", 4096, [2 * PH, T])
        key_s = view("key_s", "P", 8192, [NB, 2 * PH, NKEY])
        cand = view("cand", "TMP", 0, [PH, TOPK, TOPK])
        hot = view("hot", "TMP", 4096, [PH, TOPK, TOPK])
        top_v = view("top_v", "MISC", 0, [2 * PH, TOPK])
        top_i = view("top_i", "MISC", 256, [2 * PH, TOPK], U32)
        top_f = view("top_f", "MISC", 512, [2 * PH, TOPK])
        best_v = view("best_v", "MISC", 768, [PH, TOPK])
        best_i = view("best_i", "MISC", 896, [PH, TOPK], U32)
        pick_i = view("pick_i", "P", 4096, [SLOTS], U32)
        pick_f = view("pick_f", "P", 4096 + SLOTS, [SLOTS])
        exp_f = [view(f"exp_f{i}", "P", 4096 + SLOTS * (2 + i), [SLOTS]) for i in range(2)]
        soft = view("soft", "P", 4096 + SLOTS * 4, [PH])
        idx = view("idx", "P", 4096 + SLOTS * 5, [NB, SLOTS], U32)
        gate_w = view("gate_w", "P", 4096 + SLOTS * 7, [NB, SLOTS])
        dots = view("dots", "P", 4096 + SLOTS * 9, [NB, SLOTS])
        step_dots = view("step_dots", "P", 4096 + SLOTS * 11, [GSTEP])
        step_idx = view("step_idx", "P", 4096 + SLOTS * 12, [2, GATH], U32)
        v_sum = view("v_sum", "P", 8192, [2, D])
        nfin = view("nfin", "TMP", 0, [D])
        rows_g = view("rows_g", "RAW", 0, [GATH, D])
        gtok = tiny("gtok", [NB, NG])
        m_st = tiny("m_st", [2, 2 * NB + 1])
        n_ml = tiny("n_ml", [2, NB])
        dcy = tiny("dcy", [2, NB])
        co = tiny("co", [5, 2, NB, MH])
        den = tiny("den", [2])
        l_ms = [tiny(f"l_ms{i}", [NB * MH]) for i in range(3)]

        def lat_half(o):
            return lambda b: P2[:, b // 4, o + (b % 4) * T:o + (b % 4 + 1) * T]

        l_rows = [P2[0:MH, 0, 512 * i:512 * (i + 1)].rearrange("p (d t) -> p d t", d=2) for i in range(3)] + \
                 [P2[0:MH, 1, 512 * i:512 * (i + 1)].rearrange("p (d t) -> p d t", d=2) for i in range(3)]

        class Stream:

            def __init__(self, s):
                self.s, self.lat = s, s == 1
                v = (c_pad, c_k, c_ktok, c_v1)
                if not self.lat:
                    self.pad, self.v1 = c_pad, c_v1
                    self.kT = lambda b: c_k[:, b, :]
                    self.k_raw = lambda n, b: kv[:, n, b * P:(b + 1) * P]
                    self.k_tok = lambda n, o, w: c_ktok[:, n, o:o + w]
                    self.v = lambda n: kv[:, n, D_ML:2 * D_ML]
                    r = [x[0:MH, :, :] for x in c_rows]
                    self.A, self.lf, self.b, self.M, self.wk = r
                else:
                    self.pad, self.v1 = l_pad, l_v1
                    self.kT = lat_half(O_K)
                    self.k_raw = lambda n, b: P2[:, n, O_K + b * P:O_K + (b + 1) * P]
                    self.k_tok = lambda n, o, w: P2[:, n, O_VM + o:O_VM + o + w]
                    self.v = lambda n: P2[:, n, O_VM:O_VM + D_ML]
                    self.A, self.lf, self.b, self.M, self.wk, self.ex = l_rows
                self.steps = [(step, d, step if d == 0 else NB - 1 - step) for step in range(NB) for d in range(2)]

        streams = [Stream(0), Stream(1)]

        def span(n):
            return slice(n * P, (n + 1) * P)

        def scan_ap(x, d, n):
            r = x[:, d, n * P:(n + 1) * P]
            return r if d == 0 else r[:, ::-1]

        def last_of(x, d, n):
            t = (n + 1) * P - 1 if d == 0 else n * P
            return x[:, d, t:t + 1]

        def hdim(x):
            return x[:, :].unsqueeze(2)

        block = ctx.enter_context(nc.Block())

        @block.sync
        def _(sp):
            sp.dma_start(cols[:, 0:NCOL], a["cols"]).then_inc(sem("cols_landed"), 16)
            sp.dma_start(ident[:, :], a["ident"]).then_inc(sem("ident_landed"), 16)

            def load_chunk(c, s):
                sp.dma_start(raw[:, s, :], a["wstream"][c]).then_inc(raw_landed[s], 16)

            for s in range(SLOTS_W):
                load_chunk(s, s)
            loads = [S_OUT, S_OUT, S_FFN, S_CTX, S_IN2, S_IN2, S_OUT2, S_OUT2, NCH, NCH]
            with sp.Fori(1, min(loads[min(until, 9)] + SLOTS_W, NCH) // SLOTS_W) as i:
                for s in range(SLOTS_W):
                    sp.wait_ge(split_used, lin(s + 1 - SLOTS_W, i, SLOTS_W))
                    load_chunk(lin(s, i, SLOTS_W), s)

            if until < 9:
                for s in range(SLOTS_W):
                    sp.wait_ge(raw_landed[s], 16 * (min(loads[until] + SLOTS_W, NCH) // SLOTS_W))
                sp.wait_ge(sem("cols_landed"), 16)
                return
            sp.wait_ge(sem("out_ready"), NB)
            sp.dma_start(out.rearrange("o (b p) d -> p (o b) d", p=P), X[:, :, :]).then_inc(sem("out_stored"), 16)
            sp.wait_ge(sem("out_stored"), 16)

        @block.gpsimd
        def _(pool):
            pool.dma_start(X[:, :, :], a["x"].rearrange("o (b p) d -> p (o b) d", p=P)).then_inc(sem("x_landed"), 16)
            pool.dma_start(wa[:, :, :], a["wa"]).then_inc(sem("gates_landed"), 16)
            pool.dma_start(wx[:, :, :], a["wx"]).then_inc(sem("gates_landed"), 16)
            pool.dma_start(decay[:, :, :], a["decay"]).then_inc(sem("decay_landed"), 16)
            pool.dma_start(rope[:, :, :, :], a["rope"]).then_inc(sem("rope_landed"), 16)
            if until < 3:
                return
            pool.wait_ge(sem("y1_ready"), 2 * LB)
            for dst, name in ((pool_t, "pool_t"), (sgu_w, "sgu_w"), (pool_w, "pool_w"), (keys, "keys"), (mask, "mask"),
                              (wg, "wg")):
                pool.dma_start(dst[tuple(slice(None) for _ in dst.shape)], a[name]).then_inc(sem("tables_landed"), 16)
            pool.dma_start(fnw[:, :], a["fnw"].partition_broadcast(P)).then_inc(sem("fnw_landed"), 16)
            if until < 4:
                return
            pool.wait_ge(sem("x2_ready"), 1)
            pool.dma_start(ctx_x[:, :, :], a["ctx"].rearrange("o (b p) d -> p (o b) d", p=P)).then_inc(
                sem("ctx_landed"), 16)
            if until < 6:
                return
            pool.wait_ge(sem("ctx_done"), 1)
            pool.dma_start(sgu_n[:, :], a["sgu_n"].partition_broadcast(P)).then_inc(sem("sgu_n_landed"), 16)
            if until < 9:
                return
            for table, g0, b in (("u_tab", 0, 0), ("u_tab", SLOTS, 1), ("v_tab", 2 * SLOTS, 0), ("v_tab", 3 * SLOTS, 1)):
                if g0 < 2 * SLOTS:
                    pool.wait_ge(sem("idx_ready"), b + 1)
                with pool.Fori(0, SLOTS // GSTEP) as i:
                    for s in range(GSTEP):
                        if s % GATH == 0:
                            pool.tensor_copy(step_idx[:, s // GATH, :], idx[:, b, bass.ds(lin(s, i, GSTEP), GATH)]).then_inc(
                                sem("step_idx_ready"), 1)
                            pool.wait_ge(sem("step_idx_ready"), lin(g0 // GATH + s // GATH + 1, i, GSTEP // GATH))
                        pool.wait_ge(sem("row_used"), lin(g0 + s + 1, i, GSTEP))
                        pool.sem_inc(sem("gathers"), 1)
                        pool.indirect_dma_start(
                            out=rows_g[:, s % GATH, :], out_offset=None, in_=a[table],
                            in_offset=bass.IndirectOffsetOnAxis(ap=step_idx[:, s // GATH, s % GATH:s % GATH + 1], axis=0),
                        ).then_inc(sem(f"row_landed{s % GATH}"), 16)

        @block.tensor
        def _(pe):
            def products(n, banks, k0, nk, i, per, ah, al, blocks=NB, first=True, last=True):
                pe.wait_ge(lo_ready, lin(n + 1, i, per))
                wh, wl = WH[:, n % SLOTS_W, :], WL[:, n % SLOTS_W, :]
                for k in range(nk):
                    w = slice(k * CW, (k + 1) * CW)
                    for b in range(blocks):
                        t = slice(b * P, (b + 1) * P)
                        o = banks[b][:, :]
                        pe.matmul(o, ah[:, k0 + k, t], wh[:, w], start=first and k == 0, stop=False)
                        mm = pe.matmul(o, ah[:, k0 + k, t], wl[:, w], start=False,
                                       stop=al is None and last and k == nk - 1)
                        if al is not None:
                            mm = pe.matmul(o, al[:, k0 + k, t], wh[:, w], start=False, stop=last and k == nk - 1)
                mm.then_inc(split_used, 1)

            def tile(n, q, par, i=None, per=0, qper=0):
                pe.wait_ge(acc_free_act, lin(q + 1, i, qper))
                pe.wait_ge(acc_free_dve, lin(q + 1, i, qper))
                for m in range(CPT):
                    products(n + m, ACC[par], m * CK, CK, i, per, UH, UL, first=m == 0, last=m == CPT - 1)

            def linear(n0, q0, tiles):
                with pe.Fori(0, tiles // 2) as i:
                    for par in range(2):
                        tile(n0 + CPT * par, q0 + par, (q0 + par) % 2, i, 2 * CPT, 2)
                if tiles % 2:
                    tile(n0 + CPT * (tiles - 1), q0 + tiles - 1, (q0 + tiles - 1) % 2)

            def turn(src, banks, name, wait=None, per_bank=4):
                for j, bk in enumerate(banks):
                    if wait:
                        wait(j)
                    for m in range(per_bank):
                        mm = pe.transpose(bk[:, m * P:(m + 1) * P], src(j, m), ident[:, :])
                    mm.then_inc(sem(name), 1)

            def norm_turned(rows, call, xn):
                pe.wait_ge(sem("xn_ready"), NB * (rows + 1))
                turn(lambda j, m: xn[:, m % 2, (2 * j + m // 2) * P:(2 * j + m // 2 + 1) * P], ALLB, "xn_turned")

            def u_ready(call):
                pe.wait_ge(sem("u_ready"), KT * (call + 1))

            pe.wait_ge(sem("ident_landed"), 16)
            norm_turned(0, 0, XN)
            u_ready(0)
            linear(S_IN, Q_IN, W_IN_TILES)
            if until < 2:
                return

            pe.wait_ge(acc_free_act, Q_OUT + 2)
            pe.wait_ge(acc_free_dve, Q_OUT + 2)
            turn(lambda j, m: Pin[:, m % 2, (2 * j + m // 2) * P:(2 * j + m // 2 + 1) * P], DB, "lru_x_turned")
            turn(lambda j, m: Pin[:, m % 2, 1024 + (2 * j + m // 2) * P:1024 + (2 * j + m // 2 + 1) * P], bank[0:4],
                 "lru_g_turned")
            pe.wait_ge(sem("gates_landed"), 32)
            pe.wait_ge(sem("lru_g_ready"), 4)
            pe.wait_ge(sem("lru_x_ready"), 4)
            pe.wait_ge(sem("lru_u_ready"), 1)
            for w, banks in ((wa, DB), (wx, bank[0:4])):
                for b in range(LB):
                    mm = pe.matmul(banks[b // 2][:, (b % 2) * T:(b % 2 + 1) * T], w[:, b, :], lru_u[:, b, :],
                                   start=True, stop=True)
                    mm.then_inc(sem("lru_gate_ps"), 1)

            pe.wait_ge(sem("lru_gates_ready"), 2 * LB)
            pe.wait_ge(sem("rope_ready"), NB)
            for t0, banks in ((C_Q, DB), (C_Q + 1024, bank[0:4])):
                turn(lambda j, m: Pin[:, m % 2, t0 + (2 * j + m // 2) * P:t0 + (2 * j + m // 2 + 1) * P], banks,
                     "qk_turned")
            pe.wait_ge(sem("qk_ready"), 8)
            qT, kT = half(0), half(1)
            for h in range(HEADS):
                for n in range(NB):
                    t = slice(n * P, (n + 1) * P)
                    mm = pe.matmul(DB[h // 2][:, ((h % 2) * 2 + n) * P:((h % 2) * 2 + n + 1) * P], kT(h)[:, t], qT(h)[:, t],
                                   start=True, stop=True)
                if h % 2:
                    mm.then_inc(sem("ret_scores"), 1)
            for h in range(HEADS):
                pe.wait_ge(sem("ret_s_ready"), h // 2 + 1)
                for n in range(NB):
                    mm = pe.matmul(bank[2 * n + h // 4][:, (h % 4) * P:(h % 4 + 1) * P], ret_s[:, h, n, :],
                                   Pin[:, n, C_V + h * P:C_V + (h + 1) * P], start=True, stop=True)
            mm.then_inc(sem("ret_inner"), 1)
            pe.wait_ge(sem("ret_kz_ready"), 1)
            for h in range(HEADS):
                mm = pe.matmul(DB[h // 4][:, (h % 4) * P:(h % 4 + 1) * P], ret_kz[:, h, :],
                               Pin[:, 0, C_V + h * P:C_V + (h + 1) * P], start=True, stop=True)
            mm.then_inc(sem("ret_kv"), 1)
            pe.wait_ge(sem("ret_r_ready"), 2)
            for h in range(HEADS):
                mm = pe.matmul(DB[2 + h // 4][:, (h % 4) * P:(h % 4 + 1) * P], qT(h)[:, P:T], ret_r[:, h, :],
                               start=True, stop=True)
            mm.then_inc(sem("ret_cross"), 1)
            pe.wait_ge(sem("ret_o_ready"), 1)
            turn(lambda j, m: ret_o[:, m % 2, 2 * j + m // 2, :], bank[0:4], "ret_turned")
            pe.wait_ge(sem("y1_ready"), 2 * LB)
            linear(S_OUT, Q_OUT, OUT_TILES)
            if until < 3:
                return

            norm_turned(1, 1, XN)
            u_ready(1)

            def step(kinds, n, i=None, tile=0, down=0):
                m = dict.fromkeys(kinds, 0)
                for p, kind in enumerate(kinds):
                    at, k = n + p, m[kind]
                    m[kind] += 1
                    if k == 0 and kind in "gu":
                        q = Q_FFN + 2 * tile + "gu".index(kind)
                        pe.wait_ge(acc_free_act, lin(q + 1, i, 2))
                        pe.wait_ge(acc_free_dve, lin(q + 1, i, 2))
                    if kind == "g":
                        if k == 0 and tile:
                            pe.wait_ge(sem("mod_ready"), lin(ADA_STEP * tile, i, ADA_STEP))
                        products(at, ACC[0], k * CK, CK, i, len(FF_STEP), UH, UL, first=k == 0, last=k == CPT - 1)
                    elif kind == "u":
                        if k == 0 and tile:
                            pe.wait_ge(sem("ffT_ready"), lin(CK * tile, i, CK))
                        products(at, ACC[1], k * CK, CK, i, len(FF_STEP), UH, UL, first=k == 0, last=k == CPT - 1)
                    elif kind == "a":
                        if k == 0:
                            pe.wait_ge(acc_free_act, lin(Q_FFN + 4 + 2 * min(tile, FT - 1), i, 2))
                            if tile == FT:
                                pe.wait_ge(sem("mod_ready"), ADA_STEP * FT)
                        r = k % CPT
                        products(at, [ACC[0][k // CPT]], r * CK, CK, i, len(FF_STEP), cond, None, blocks=1, first=r == 0,
                                 last=r == CPT - 1)
                    else:
                        if k == 0:
                            pe.wait_ge(sem("ffT_ready"), lin(CK * (down + 1), i, CK))
                        pe.wait_ge(sem("down_added"), lin(2 + OUT_TILES * down + k - 1, i, OUT_TILES))
                        products(at, DB[2 * (k % 2):2 * (k % 2) + 2], 0, CK, i, len(FF_STEP), FH, FL)

            def turn_ff(i=None, nth=0):
                pe.wait_ge(sem("ff_ready"), lin(nth + 1, i, 1))
                for j in range(2):
                    for m in range(4):
                        k = 2 * j + m // 2
                        mm = pe.transpose(bank[2 + j][:, m * P:(m + 1) * P], ff[:, m % 2, k * P:(k + 1) * P], ident[:, :])
                mm.then_inc(sem("ff_turned"), 1)

            def ada_turned(i=None, nth=0):
                for t in range(ADA_STEP):
                    pe.wait_ge(sem("ada_rows_ready"), lin(ADA_STEP * nth + t + 1, i, ADA_STEP))
                    for j in range(CW // P):
                        mm = pe.matmul(ACC[0][t][:, 2 * j:2 * j + 2], ada_rows[0:4, t, j * P:(j + 1) * P],
                                       col("sel", 0, 2, rows=4), start=True, stop=True)
                    mm.then_inc(sem("ada_cols"), 1)

            pe.wait_ge(sem("cond_ready"), 1)
            step(FF_FIRST, S_FFN)
            turn_ff()
            ada_turned()
            with pe.Fori(0, FT - 1) as i:
                step(FF_STEP, S_STEP, i, tile=1)
                ada_turned(i, 1)
                turn_ff(i, 1)
            step(FF_LAST, S_LAST, tile=FT, down=FT - 1)
            ada_turned(nth=FT)
            if until < 4:
                return

            def gates(s):
                g = DB[2]
                for b in range(NB):
                    for k in range(KT):
                        for part in (UH, UL):
                            mm = pe.matmul(g[:, b * NG:(b + 1) * NG], part[:, k, span(b)].bitcast(F32), wg[:, k, :],
                                           start=part is UH and k == 0, stop=part is UL and k == KT - 1)
                mm.then_inc(sem("gate_ps"), 1)

            def gate_rows(s):
                pe.wait_ge(sem("gtok_ready"), s + 1)
                for typ in range(2):
                    for d in range(2):
                        for b in range(NB):
                            mm = pe.matmul(DB[2 + typ][0:MH, d * T + b * P:d * T + (b + 1) * P],
                                           gtok[:, b, (2 * d + typ) * MH:(2 * d + typ + 1) * MH], ident[:, :], start=True,
                                           stop=True)
                mm.then_inc(sem("gate_rows_ps"), 1)

            def keys_turned(S):
                turn(lambda j, m: S.k_raw(m % 2, 2 * j + m // 2), bank[0:4], "k_turned")
                pe.wait_ge(sem("k_silu"), S.s + 1)
                for j in range(4):
                    for m in range(4):
                        mm = pe.transpose(bank[j][:, m * P:(m + 1) * P], S.kT(4 * (j % 2) + m)[:, span(j // 2)], ident[:, :])
                    mm.then_inc(sem("k_back"), 1)

            def columns(S):
                pe.wait_ge(sem("rows_ready"), S.s + 1)
                kinds = [S.A, S.wk, S.lf, S.ex] if S.lat else [None, S.wk]
                for kind, row in enumerate(kinds):
                    for d in range(2):
                        for n in range(NB):
                            o = ((kind * 2 + d) * NB + n) * MH
                            if row is not None:
                                pe.matmul(DB[2][:, o:o + MH], row[:, d, span(n)], ident[0:MH, 0:MH], start=True, stop=True)
                for d in range(2):
                    for n in range(NB):
                        o = ((4 * 2 + d) * NB + n) * MH
                        mm = pe.matmul(DB[2][:, o:o + MH], dcy[0:MH, d, n:n + 1].to_broadcast([MH, P]), ident[0:MH, 0:MH],
                                       start=True, stop=True)
                mm.then_inc(sem("cols_ps"), 1)

            upd = [0]

            def update(S, n):
                for h in range(MH):
                    pe.wait_ge(sem("vw_ready"), upd[0] * MH + h + 1)
                    for kt in range(MKT):
                        mm = pe.matmul(ALLB[2 * h + kt][:, 0:VA], S.k_tok(n, h * MD + kt * P, P), vw[:, h % 2, :], start=True,
                                       stop=True)
                    mm.then_inc(sem("state_ps"), 1)
                upd[0] += 1
                pe.wait_ge(sem("state_ready"), upd[0])

            pe.wait_ge(sem("down_added"), 2 + FT * OUT_TILES)
            norm_turned(3, 2, ctx_n)
            u_ready(2)
            linear(S_CTX, Q_CTX, CTX_TILES)
            if until < 5:
                return
            pe.wait_ge(sem("tables_landed"), 16 * 6)
            gates(0)
            gate_rows(0)
            pe.wait_ge(acc_free_act, Q_IN2 + 2)
            pe.wait_ge(acc_free_dve, Q_IN2 + 2)
            keys_turned(streams[0])
            columns(streams[0])
            pe.wait_ge(sem("k_tok_ready"), 4)
            pe.wait_ge(sem("co_ready"), 1)
            for step, d, n in streams[0].steps:
                update(streams[0], n)
            if until < 6:
                return

            norm_turned(4, 3, XN2)
            u_ready(3)
            linear(S_IN2, Q_IN2, W2_TILES)
            gates(1)
            pe.wait_ge(acc_free_act, Q_OUT2 + 2)
            pe.wait_ge(acc_free_dve, Q_OUT2 + 2)
            if until < 7:
                return

            for g in range(len(PW)):
                for b in range(NB):
                    mm = pe.matmul(DB[g // 2][:, (g % 2) * T:(g % 2 + 1) * T], P2[:, b, O_P + g * P:O_P + (g + 1) * P],
                                   pool_t[:, g, b, :], start=b == 0, stop=b == NB - 1)
                mm.then_inc(sem("pool_ps"), 1)
            for g in range(len(PW)):
                pe.wait_ge(sem("pool_d_ready"), g + 1)
                mm = pe.matmul(bank[g // 2][:, (g % 2) * T:(g % 2 + 1) * T], pool_w[:, g, :], pool_d[:, g, :], start=True,
                               stop=True)
                mm.then_inc(sem("pool_y_ps"), 1)
            pe.wait_ge(sem("sgu_v_ready"), 1)
            for n in range(NB):
                for h in range(SH):
                    mm = pe.matmul(DB[n][:, h * P:(h + 1) * P], sgu_w[:, h, :], P2[:, n, O_V + h * P:O_V + (h + 1) * P],
                                   start=True, stop=True)
            mm.then_inc(sem("sgu_ps"), 1)
            pe.wait_ge(sem("sgu_y_ready"), 1)
            turn(lambda j, m: P2[:, m % 2, O_U + (2 * j + m // 2) * P:O_U + (2 * j + m // 2 + 1) * P], DB[0:2], "sgu_turned")
            L = streams[1]
            pe.wait_ge(sem("y2_ready"), 8)
            turn(lambda j, m: P2[:, m % 2, O_Q + (2 * j + m // 2) * P:O_Q + (2 * j + m // 2 + 1) * P], DB, "q_turned")
            pe.wait_ge(sem("q_pad_ready"), 4)
            gate_rows(1)
            keys_turned(L)
            pe.wait_ge(sem("q_silu"), 1)
            for h in range(MH):
                for n in range(NB):
                    for kt in range(MKT):
                        mm = pe.matmul(DB[h // 2][:, ((h % 2) * NB + n) * P:((h % 2) * NB + n + 1) * P],
                                       L.kT(MKT * h + kt)[:, span(n)], lat_half(O_Q)(MKT * h + kt)[:, span(n)],
                                       start=kt == 0, stop=kt == MKT - 1)
            mm.then_inc(sem("ml_scores"), 1)
            pe.wait_ge(sem("k_tok_ready"), 8)
            columns(L)
            pe.wait_ge(sem("co_ready"), 2)
            pe.wait_ge(sem("sc_t_ready"), 1)
            x = 0
            for step, d, n in L.steps:
                def weights(h):
                    pe.matmul(DB[h % 2][:, 0:P], ident[0:MH, h:h + 1].to_broadcast([MH, P]), L.b[:, d, span(n)], start=True,
                              stop=False)
                    pe.matmul(DB[h % 2][:, 0:P], ident[:, :], mask[:, d, :], start=False, stop=True).then_inc(
                        sem("arg_ps"), 1)
                weights(0)
                for h in range(MH):
                    if h + 1 < MH:
                        if h >= 1:
                            pe.wait_ge(sem("w_exp"), x + h)
                        weights(h + 1)
                    if x + h >= 2:
                        pe.wait_ge(sem("h_ready"), x + h - 1)
                    for kt in range(MKT):
                        pe.matmul(ACC[h % 2][1][:, 0:VA], lat_half(O_Q)(MKT * h + kt)[:, span(n)], st[:, d, h, kt, :],
                                  start=kt == 0, stop=kt == MKT - 1)
                    pe.wait_ge(sem("w_ready"), x + h + 1)
                    pe.matmul(ACC[h % 2][0][:, 0:VA], wb[:, h % 2, :], L.v1[:, n, h, :], start=True, stop=True).then_inc(
                        sem("num_ps"), 1)
                x += MH
                pe.wait_ge(sem("w_exp"), x)
                if step == 0:
                    pe.wait_ge(sem("h_ready"), x)
                    update(L, n)
            pe.wait_ge(sem("ml_y_ready"), 1)
            turn(lambda j, m: P2[:, m % 2, O_K + (2 * j + m // 2) * P:O_K + (2 * j + m // 2 + 1) * P], DB, "ml_turned")
            if until < 8:
                return
            def spread(column):
                for j in range(4):
                    for m in range(4):
                        mm = pe.matmul(DB[j][:, m * P:(m + 1) * P], column(4 * j + m).to_broadcast([P, P]), ident[:, :],
                                       start=True, stop=True)
                    mm.then_inc(sem("spread_ps"), 1)

            pe.wait_ge(sem("y2_ready"), KT)
            spread(lambda k: modt[:, 2 * KT + k, 0:1])
            pe.wait_ge(sem("spread_ready"), 4)
            spread(lambda k: modt[:, 5 * KT + k, 0:1])
            linear(S_OUT2, Q_OUT2, OUT_TILES)

            pe.wait_ge(sem("spread_ready"), 8)
            norm_turned(5, 4, XN2)
            u_ready(4)
            spread(lambda k: sc_ffn[:, k:k + 1])
            pe.wait_ge(sem("spread_ready"), 12)
            spread(lambda k: modt[:, 3 * KT + k, 0:1])
            linear(S_WQ, Q_WQ, OUT_TILES)
            pe.wait_ge(sem("spread_ready"), 16)
            pe.wait_ge(acc_free_act, Q_WQ + OUT_TILES + 2)
            pe.wait_ge(acc_free_dve, Q_WQ + OUT_TILES + 2)
            pe.wait_ge(sem("hf_ready"), NB)
            turn(lambda j, m: q_tok[:, m % 2, (2 * j + m // 2) * P:(2 * j + m // 2 + 1) * P], ALLB, "pq_turned")
            pe.wait_ge(sem("q_t_ready"), 8)
            for b in range(NB):
                for hp in range(2 * PH):
                    mm = pe.matmul(ALLB[4 * b + hp // 4][:, (hp % 4) * NKEY:(hp % 4 + 1) * NKEY], q_t[:, hp, span(b)],
                                   keys[:, hp % 2, :], start=True, stop=True)
                    if hp % 4 == 3:
                        mm.then_inc(sem("key_ps"), 1)

        @block.scalar
        def _(act):
            chain = Chain(act, "act_chain")

            def hi(n, i=None, per=0):
                if i is None and n >= NCH:
                    return
                act.wait_ge(raw_landed[n % SLOTS_W], lin(16 * (n // SLOTS_W + 1), i, 16 * per // SLOTS_W))
                act.activation(WH[:, n % SLOTS_W, :], raw[:, n % SLOTS_W, :], ACT.Copy).then_inc(hi_ready, 1)

            def tile(n, evacuate, i=None, per=0):
                for m in range(CPT):
                    hi(n + LEAD + m, i, per)
                act.wait_ge(split_used, lin(n + CPT, i, per))
                evacuate()

            def linear(n0, q0, tiles, evacuate):
                pairs = tiles // 2
                last = n0 + tiles * CPT == NCH
                with act.Fori(0, pairs - last) as i:
                    for par in range(2):
                        tile(n0 + CPT * par, lambda: evacuate((q0 + par) % 2, lin(par, i, 2)), i, 2 * CPT)
                for t in range(2 * (pairs - last), tiles):
                    tile(n0 + CPT * t, lambda: evacuate((q0 + t) % 2, t))

            def to(dst, width):
                def evacuate(par, t):
                    act.activation(dst(t), ACC[par][0][:, 0:width], ACT.Copy).then_inc(acc_free_act, 1)
                return evacuate

            def nothing(par, t):
                act.sem_inc(acc_free_act, 1)

            def root(call):
                act.wait_ge(sem("ms_ready"), call + 1)
                act.activation(rms[:, :], ms[:, :], ACT.Sqrt).then_inc(sem("rms_ready"), 1)

            def norm_turned(rows, call, scale, bias=None):
                root(rows)
                for j in range(8):
                    act.wait_ge(sem("xn_turned"), 8 * call + j + 1)
                    for m in range(2):
                        k = 2 * j + m
                        src = ALLB[j][:, m * T:(m + 1) * T]
                        if bias is None:
                            ins = act.activation(UH[:, k, :], src, ACT.Copy, scale=scale(k))
                        else:
                            ins = act.activation(UH[:, k, :], src, ACT.Identity, scale=scale(k), bias=bias(k))
                        ins.then_inc(sem("uh_ready"), 1)

            act.wait_ge(sem("cols_landed"), 16)
            for r, name in enumerate(("c", "cctx")):
                chain.mark(act.activation(csil[:, :, r], col(name, 0, KT), ACT.Silu))
            chain.sync()
            act.wait_ge(sem("lam_abs"), 1)
            act.activation(lam_t[1][:, :], lam_t[0][:, :], ACT.Exp, scale=-1.0).then_inc(sem("lam_exp"), 1)
            for m in range(LEAD):
                hi(m)
            act.sem_inc(acc_free_act, 2)

            norm_turned(0, 0, lambda k: col("ln1", k))
            linear(S_IN, Q_IN, W_IN_TILES, to(lambda t: Pin[:, 0, bass.ds(t * CW, CW)], CW))
            if until < 2:
                return

            for j in range(4):
                act.wait_ge(sem("lru_x_turned"), j + 1)
                act.activation(lru_x[:, 2 * j:2 * j + 2, CONV_W - 1:],
                               DB[j][:, :].rearrange("p (b t) -> p b t", t=T), ACT.Copy).then_inc(sem("lru_x_ready"), 1)
            for j in range(4):
                act.wait_ge(sem("lru_g_turned"), j + 1)
                act.activation(lru_g[:, 2 * j:2 * j + 2, :], bank[j][:, :].rearrange("p (b t) -> p b t", t=T),
                               ACT.Gelu_apprx_tanh).then_inc(sem("lru_g_ready"), 1)
            rg, ig = half(0), half(1)
            act.wait_ge(sem("lru_g_turned"), 4)
            for name, dst, banks, w in (("ba", rg, DB, 0), ("bx", ig, bank[0:4], LB)):
                for b in range(LB):
                    act.wait_ge(sem("lru_gate_ps"), w + b // 2 * 2 + 2)
                    act.activation(dst(b), banks[b // 2][:, (b % 2) * T:(b % 2 + 1) * T], ACT.Sigmoid,
                                   bias=col(name, b)).then_inc(sem("lru_gates_ready"), 1)
            act.wait_ge(sem("lru_gates_ready"), 2 * LB)
            act.wait_ge(sem("lam_ready"), 1)
            for b in range(LB):
                act.activation(lru_b[:, b, :], rg(b), ACT.Tanh, scale=p_col[:, b:b + 1]).then_inc(sem("lru_tanh"), 1)
            for b in range(LB):
                act.activation(rg(b), rg(b), ACT.Exp, scale=n_col[:, b:b + 1]).then_inc(sem("lru_a_ready"), 1)
            act.wait_ge(sem("lru_sq_ready"), 1)
            act.activation(lru_b[:, :, :], lru_b[:, :, :], ACT.Sqrt).then_inc(sem("lru_root"), 1)
            act.wait_ge(sem("lru_y_ready"), 1)
            act.activation(UH[:, 0:LB, :], lru_g[:, :, :], ACT.Copy).then_inc(sem("lru_yh_ready"), 1)

            for j in range(8):
                act.wait_ge(sem("qk_turned"), j + 1)
                qk = half(j // 4)
                for m in range(2):
                    ins = act.activation(qk(2 * (j % 4) + m), (DB if j < 4 else bank[0:4])[j % 4][:, m * T:(m + 1) * T],
                                         ACT.Copy)
                ins.then_inc(sem("qk_ready"), 1)
            act.wait_ge(sem("ret_kv"), 1)
            for j in range(2):
                act.activation(ret_r[:, 4 * j:4 * j + 4, :], DB[j][:, :].rearrange("p (h e) -> p h e", e=P),
                               ACT.Copy).then_inc(sem("ret_r_ready"), 1)
            act.activation(Pin[:, :, C_G:C_G + 1024], Pin[:, :, C_G:C_G + 1024], ACT.Silu).then_inc(sem("ret_gate"), 1)
            act.wait_ge(sem("gn_var"), 1)
            act.activation(gn[1][:, :], gn[0][:, :], ACT.Sqrt).then_inc(sem("gn_root"), 1)
            for j in range(4):
                act.wait_ge(sem("ret_turned"), j + 1)
                for m in range(2):
                    h = 2 * j + m
                    act.activation(UH[:, LB + h, :], bank[j][:, m * T:(m + 1) * T], ACT.Copy,
                                   scale=col("gnw", h)).then_inc(sem("ret_yh_ready"), 1)
            linear(S_OUT, Q_OUT, OUT_TILES, nothing)
            if until < 3:
                return

            act.activation(cond[:, :, 0:2], csil[:, :, :], ACT.Copy).then_inc(sem("cond_hi"), 1)
            norm_turned(1, 1, lambda k: col("ln2", k))

            def step(kinds, n, i=None, tile=0):
                m = dict.fromkeys(kinds, 0)
                for p, kind in enumerate(kinds):
                    hi(n + LEAD + p, i, len(FF_STEP))
                    m[kind] += 1
                    if kind == "g" and m[kind] == CPT:
                        act.wait_ge(split_used, lin(n + p + 1, i, len(FF_STEP)))
                        if tile:
                            act.wait_ge(sem("ff_ready"), lin(tile, i, 1))
                        for b in range(NB):
                            ins = act.activation(ff_g[:, b, :], ACC[0][b][:, :], ACT.Silu)
                        ins.then_inc(acc_free_act, 2)
                    if kind == "a" and m[kind] % CPT == 0:
                        t = m[kind] // CPT - 1
                        act.wait_ge(split_used, lin(n + p + 1, i, len(FF_STEP)))
                        if tile:
                            act.wait_ge(sem("ada_cols"), lin(ADA_STEP * (tile - 1) + t + 1, i, ADA_STEP))
                        act.activation(ada_rows[0:4, t, :], ACC[0][t][0:4, :], ACT.Copy).then_inc(sem("ada_rows_ready"), 1)

            def turned(i=None, nth=0):
                act.wait_ge(sem("ff_turned"), lin(nth + 1, i, 1))
                for k in range(CK):
                    act.activation(FH[:, k, :], bank[2 + k // 2][:, (k % 2) * T:(k % 2 + 1) * T], ACT.Copy).then_inc(
                        sem("ffh_ready"), 1)

            step(FF_FIRST, S_FFN)
            turned()
            with act.Fori(0, FT - 1) as i:
                step(FF_STEP, S_STEP, i, tile=1)
                turned(i, 1)
            step(FF_LAST, S_LAST, tile=FT)
            if until < 4:
                return

            root(2)

            def pads(name, base, banks, pad, done):
                for j in range(4):
                    act.wait_ge(sem(name), base + j + 1)
                    act.activation(pad[:, 2 * j:2 * j + 2, 1:T + 1], banks[j][:, :].rearrange("p (b t) -> p b t", t=T),
                                   ACT.Copy).then_inc(sem(done), 1)

            def keys_turned(S):
                pads("k_turned", 4 * S.s, bank[0:4], S.pad, "k_pad_ready")
                act.wait_ge(sem("k_conv"), S.s + 1)
                for b in range(MB):
                    chain.mark(act.activation(S.kT(b), S.kT(b), ACT.Silu))
                chain.sync()
                for b in range(MB):
                    ins = act.activation(S.kT(b), S.kT(b), ACT.Copy, scale=float(MD) ** -0.5)
                ins.then_inc(sem("k_silu"), 1)
                if S.lat:
                    act.wait_ge(sem("v1_ready"), 1)
                for j in range(4):
                    act.wait_ge(sem("k_back"), 4 * S.s + j + 1)
                    act.activation(S.k_tok(j // 2, (j % 2) * CW, CW), bank[j][:, :], ACT.Copy).then_inc(sem("k_tok_ready"), 1)

            def gate_rows(S):
                act.wait_ge(sem("fg_abs"), S.s + 1)
                chain(act.activation(S.b, S.b, ACT.Exp, scale=-1.0))
                act.activation(S.b, S.b, ACT.Ln, bias=1.0).then_inc(sem("fg_log"), 1)
                act.wait_ge(sem("row_max"), S.s + 1)
                for d in range(2):
                    for n in range(NB):
                        chain.mark(act.activation(S.wk[:, d, span(n)], S.A[:, d, span(n)], ACT.Exp,
                                                  bias=n_ml[0:MH, d, n:n + 1]))
                chain.mark(act.activation(dcy[0:MH, :, :], dcy[0:MH, :, :], ACT.Exp))
                if S.lat:
                    for step, d, n in S.steps:
                        chain.mark(act.activation(S.lf[:, d, span(n)], S.M[:, d, span(n)], ACT.Exp, scale=-1.0,
                                                  bias=m_st[0:MH, d, NB + step:NB + step + 1]))
                    chain.mark(act.activation(S.ex, S.ex, ACT.Exp, scale=-1.0))
                chain.sync()
                act.sem_inc(sem("rows_exp"), 1)

            norm_turned(3, 2, lambda k: sc_mix[:, 1, k:k + 1], lambda k: modt[:, k, 1:2])
            linear(S_CTX, Q_CTX, CTX_TILES, to(lambda t: kv[:, 0, bass.ds(t * CW, CW)], CW))
            if until < 5:
                return
            keys_turned(streams[0])
            gate_rows(streams[0])
            if until < 6:
                return

            norm_turned(4, 3, lambda k: sc_mix[:, 0, k:k + 1], lambda k: modt[:, k, 0:1])
            linear(S_IN2, Q_IN2, W2_TILES, to(lambda t: P2[:, 0, bass.ds(t * CW, CW)], CW))
            if until < 7:
                return
            act.wait_ge(acc_free_dve, Q_OUT2 + 2)
            act.activation(P2[:, :, O_U:O_P], P2[:, :, O_U:O_P], ACT.Gelu_apprx_tanh).then_inc(sem("sgu_gelu"), 1)
            for g in range(len(PW)):
                act.wait_ge(sem("pool_ps"), g // 2 * 2 + 2)
                act.activation(pool_d[:, g, :], DB[g // 2][:, (g % 2) * T:(g % 2 + 1) * T], ACT.Copy).then_inc(
                    sem("pool_d_ready"), 1)
            for g in range(len(PW)):
                act.wait_ge(sem("pool_y_ps"), g // 2 * 2 + 2)
                act.activation(UH[:, 12 + g, :], bank[g // 2][:, (g % 2) * T:(g % 2 + 1) * T], ACT.Copy,
                               scale=col("pscale", g)).then_inc(sem("yh2_ready"), 1)
            act.wait_ge(sem("sgu_ms"), 1)
            act.activation(rms[:, :], ms[:, :], ACT.Sqrt).then_inc(sem("sgu_root"), 1)
            for k in range(4):
                act.wait_ge(sem("sgu_turned"), k // 2 + 1)
                act.activation(UH[:, k, :], DB[k // 2][:, (k % 2) * T:(k % 2 + 1) * T], ACT.Copy).then_inc(
                    sem("yh2_ready"), 1)
            L = streams[1]
            act.wait_ge(sem("y2_ready"), 8)
            pads("q_turned", 0, DB, L.pad, "q_pad_ready")
            act.wait_ge(sem("q_conv"), 1)
            qT = lat_half(O_Q)
            for b in range(MB):
                ins = act.activation(qT(b), qT(b), ACT.Silu)
            ins.then_inc(sem("q_silu"), 1)
            keys_turned(L)
            gate_rows(L)
            act.wait_ge(sem("co_ready"), 2)
            x = 0
            for step, d, n in L.steps:
                def weights(h):
                    act.wait_ge(sem("arg_ps"), x + h + 1)
                    if x + h >= 2:
                        act.wait_ge(sem("num_ps"), x + h - 1)
                    act.activation(wb[:, h % 2, :], DB[h % 2][:, 0:P], ACT.Exp, bias=co[:, 0, d, n, h:h + 1]).then_inc(
                        sem("w_exp"), 1)
                weights(0)
                for h in range(MH):
                    if h + 1 < MH:
                        weights(h + 1)
                    act.wait_ge(sem("num_ps"), x + h + 1)
                    if x + h >= 2:
                        act.wait_ge(sem("h_ready"), x + h - 1)
                    act.activation(ml_t[:, h % 2, :], ACC[h % 2][1][:, 0:VA], ACT.Copy,
                                   scale=co[:, 2, d, n, h:h + 1]).then_inc(sem("inter_ready"), 1)
                x += MH
            act.activation(P2[:, :, O_O:O_O + D_ML], P2[:, :, O_O:O_O + D_ML], ACT.Sigmoid).then_inc(sem("ml_gate"), 1)
            act.wait_ge(sem("ml_ms"), 1)
            act.activation(l_ms[1][:, :], l_ms[0][:, :], ACT.Sqrt).then_inc(sem("ml_root"), 1)
            for j in range(4):
                act.wait_ge(sem("ml_turned"), j + 1)
                for m in range(2):
                    b = 2 * j + m
                    act.activation(UH[:, 4 + b, :], DB[j][:, m * T:(m + 1) * T], ACT.Copy, scale=col("mlnorm", b)).then_inc(
                        sem("yh2_ready"), 1)
            if until < 8:
                return

            def spread(q, dst):
                for j in range(4):
                    act.wait_ge(sem("spread_ps"), 4 * q + j + 1)
                    act.activation(dst[:, j * CW:(j + 1) * CW], DB[j][:, :], ACT.Copy).then_inc(sem("spread_ready"), 1)

            spread(0, gb1)
            spread(1, gb2)
            linear(S_OUT2, Q_OUT2, OUT_TILES, nothing)
            norm_turned(5, 4, lambda k: sc_ffn[:, k:k + 1], lambda k: modt[:, 3 * KT + k, 0:1])
            act.wait_ge(sem("u_ready"), KT * 5)
            spread(2, sc_row)
            spread(3, sh_row)
            linear(S_WQ, Q_WQ, OUT_TILES, to(lambda t: q_tok[:, 0, bass.ds(t * CW, CW)], CW))
            act.wait_ge(sem("hf_ready"), NB)
            for j in range(8):
                act.wait_ge(sem("pq_turned"), j + 1)
                act.activation(q_t[:, 2 * j:2 * j + 2, :], ALLB[j][:, :].rearrange("p (b t) -> p b t", t=T),
                               ACT.Copy).then_inc(sem("q_t_ready"), 1)
            for j in range(8):
                act.wait_ge(sem("key_ps"), j + 1)
                act.activation(key_s[:, j // 4, 4 * (j % 4):4 * (j % 4) + 4, :],
                               ALLB[j][:, :].rearrange("p (b t) -> p b t", t=NKEY), ACT.Copy).then_inc(sem("key_s_ready"), 1)
            if until < 9:
                return
            for b in range(NB):
                act.wait_ge(sem("best_ready"), b + 1)
                act.activation(gate_w[:, b, :], gate_w[:, b, :], ACT.Exp).then_inc(sem("soft_exp"), 1)
            act.wait_ge(sem("dots_done"), 1)
            act.activation(dots[:, :, :], dots[:, :, :], ACT.Gelu_apprx_tanh).then_inc(sem("dots_gelu"), 1)
            act.dma_start(nfin[:, :], a["nfin"].partition_broadcast(P)).then_inc(sem("nfin_landed"), 16)
            for b in range(NB):
                act.wait_ge(sem("fin_ms"), b + 1)
                act.activation(rms[:, b:b + 1], ms[:, b:b + 1], ACT.Sqrt).then_inc(sem("fin_root"), 1)

        @block.vector
        def _(dve):
            link = Chain(dve, "dve_chain")

            def lo(n, i=None, per=0):
                if i is None and n >= NCH:
                    return
                dve.wait_ge(hi_ready, lin(n + 1, i, per))
                dve.tensor_tensor(WL[:, n % SLOTS_W, :], raw[:, n % SLOTS_W, :], WH[:, n % SLOTS_W, :].bitcast(F32),
                                  ALU.subtract).then_inc(lo_ready, 1)

            def tile(n, evacuate, i=None, per=0):
                for m in range(CPT):
                    lo(n + LEAD + m, i, per)
                dve.wait_ge(split_used, lin(n + CPT, i, per))
                evacuate()

            def linear(n0, q0, tiles, evacuate):
                pairs = tiles // 2
                last = n0 + tiles * CPT == NCH
                with dve.Fori(0, pairs - last) as i:
                    for par in range(2):
                        tile(n0 + CPT * par, lambda: evacuate((q0 + par) % 2, lin(par, i, 2)), i, 2 * CPT)
                for t in range(2 * (pairs - last), tiles):
                    tile(n0 + CPT * t, lambda: evacuate((q0 + t) % 2, t))

            def to(dst, width):
                def evacuate(par, t):
                    dve.tensor_copy(dst(t), ACC[par][1][:, 0:width]).then_inc(acc_free_dve, 1)
                return evacuate

            def add_to_x(par, t):
                for b in range(NB):
                    x = X[:, b, bass.ds(t * CW, CW)]
                    ins = dve.tensor_tensor(x, ACC[par][b][:, :], x, ALU.add)
                ins.then_inc(acc_free_dve, 1)

            def norm_rows(call, x, xn):
                for b in range(NB):
                    link(dve.tensor_tensor_reduce(xn[:, b, :], x[:, b, :], x[:, b, :], 1.0, 0.0, ALU.mult, ALU.add,
                                                  ss[:, b:b + 1]))
                dve.tensor_scalar(ms[:, :], ss[:, :], 1.0 / D, EPS, ALU.mult, ALU.add).then_inc(sem("ms_ready"), 1)
                dve.wait_ge(sem("rms_ready"), call + 1)
                link(dve.reciprocal(rinv[:, :], rms[:, :]))
                for b in range(NB):
                    dve.tensor_scalar(xn[:, b, :], x[:, b, :], rinv[:, b:b + 1], None, ALU.mult).then_inc(
                        sem("xn_ready"), 1)

            def norm_turned(rows, call, x, xn, scale, bias=None):
                norm_rows(rows, x, xn)
                for k in range(KT):
                    src = ALLB[k // 2][:, (k % 2) * T:(k % 2 + 1) * T]
                    dve.wait_ge(sem("uh_ready"), KT * call + k // 2 * 2 + 2)
                    if bias is None:
                        ins = dve.scalar_tensor_tensor(UL[:, k, :], src, scale(k), UH[:, k, :].bitcast(F32), ALU.mult,
                                                       ALU.subtract)
                    else:
                        link(dve.tensor_scalar(mod_tmp[:, k % 2, :], src, scale(k), bias(k), ALU.mult, ALU.add))
                        ins = dve.tensor_tensor(UL[:, k, :], mod_tmp[:, k % 2, :], UH[:, k, :].bitcast(F32), ALU.subtract)
                    ins.then_inc(sem("u_ready"), 1)

            dve.wait_ge(sem("cols_landed"), 16)
            o = COL["ada_b"][0]
            link(dve.tensor_copy(modt[:, :, :], cols[:, o:o + 6 * KT].unsqueeze(2).to_broadcast([P, 6 * KT, 2])))
            z, s, s2, acc, e = lam_t[1], lam_t[2], lam_t[3], lam_t[4], lam_t[0]
            dve.scalar_tensor_tensor(lam_t[0][:, :], col("lam", 0, LB), -1.0, col("lam", 0, LB), ALU.mult, ALU.max).then_inc(sem("lam_abs"), 1)
            dve.wait_ge(sem("lam_exp"), 1)
            link(dve.tensor_scalar(s[:, :], z[:, :], 2.0, None, ALU.add))
            link(dve.reciprocal(s[:, :], s[:, :]))
            link(dve.tensor_tensor(s[:, :], s[:, :], z[:, :], ALU.mult))
            link(dve.tensor_tensor(s2[:, :], s[:, :], s[:, :], ALU.mult))
            link(dve.memset(acc[:, :], 1.0 / 19))
            for n in range(17, 0, -2):
                link(dve.tensor_tensor(acc[:, :], acc[:, :], s2[:, :], ALU.mult))
                link(dve.tensor_scalar(acc[:, :], acc[:, :], 1.0 / n, None, ALU.add))
            link(dve.tensor_tensor(acc[:, :], acc[:, :], s[:, :], ALU.mult))
            link(dve.tensor_scalar(e[:, :], col("lam", 0, LB), -1.0, 0.0, ALU.mult, ALU.max))
            link(dve.scalar_tensor_tensor(acc[:, :], acc[:, :], 2.0, e[:, :], ALU.mult, ALU.add))
            link.mark(dve.tensor_scalar(p_col[:, :], acc[:, :], LRU_C, None, ALU.mult))
            dve.tensor_scalar(n_col[:, :], acc[:, :], -LRU_C, None, ALU.mult).then_inc(sem("lam_ready"), 1)
            for m in range(LEAD):
                lo(m)
            dve.sem_inc(acc_free_dve, 2)
            dve.wait_ge(sem("x_landed"), 16)
            norm_turned(0, 0, X, XN, lambda k: col("ln1", k))
            linear(S_IN, Q_IN, W_IN_TILES, to(lambda t: Pin[:, 1, bass.ds(t * CW, CW)], CW))
            if until < 2:
                return

            link(dve.memset(lru_x[:, :, 0:CONV_W - 1], 0.0))
            for j in range(4):
                dve.wait_ge(sem("lru_x_ready"), j + 1)
                for tap in range(CONV_W):
                    for b in (2 * j, 2 * j + 1):
                        w, x = col("conv", tap * LB + b), lru_x[:, b, tap:tap + T]
                        if tap == 0:
                            link.mark(dve.tensor_scalar(lru_u[:, b, :], x, w, col("convb", b), ALU.mult, ALU.add))
                        else:
                            link.mark(dve.scalar_tensor_tensor(lru_u[:, b, :], x, w, lru_u[:, b, :], ALU.mult, ALU.add))
                    link.sync()
            dve.sem_inc(sem("lru_u_ready"), 1)
            dve.wait_ge(sem("lru_gates_ready"), 2 * LB)
            link(dve.tensor_tensor(wide(1), wide(1), lru_u[:, :, :].rearrange("p (n b) t -> p n (b t)", n=NB), ALU.mult))
            dve.wait_ge(sem("lru_tanh"), LB)
            link(dve.tensor_scalar(lru_u[:, :, :], lru_b[:, :, :], 1.0, None, ALU.add))
            link(dve.reciprocal(lru_u[:, :, :], lru_u[:, :, :]))
            dve.scalar_tensor_tensor(lru_b[:, :, :], lru_b[:, :, :], 2.0, lru_u[:, :, :], ALU.mult, ALU.mult).then_inc(
                sem("lru_sq_ready"), 1)
            dve.wait_ge(sem("lru_root"), 1)
            link(dve.tensor_tensor(lru_b[:, :, :].rearrange("p (n b) t -> p n (b t)", n=NB),
                                   lru_b[:, :, :].rearrange("p (n b) t -> p n (b t)", n=NB), wide(1), ALU.mult))
            dve.wait_ge(sem("lru_a_ready"), LB)
            for b in range(LB):
                link.mark(dve.tensor_tensor_scan(lru_u[:, b, :], half(0)(b), lru_b[:, b, :], 0.0, ALU.mult, ALU.add))
            link.sync()
            dve.tensor_tensor(lru_g[:, :, :], lru_g[:, :, :], lru_u[:, :, :], ALU.mult).then_inc(sem("lru_y_ready"), 1)
            dve.wait_ge(sem("lru_yh_ready"), 1)
            dve.tensor_tensor(UL[:, 0:LB, :], lru_g[:, :, :], UH[:, 0:LB, :].bitcast(F32), ALU.subtract).then_inc(
                sem("y1_ready"), LB)
            dve.wait_ge(sem("y1_ready"), LB)

            dve.wait_ge(sem("rope_landed"), 16)
            dve.wait_ge(acc_free_act, Q_OUT + 2)
            dve.wait_ge(acc_free_dve, Q_OUT + 2)
            for b in range(NB):
                qk = Pin[:, b, C_Q:C_V].rearrange("p (h u e) -> p h u e", u=2, e=P // 2)
                t1, t2 = qk[:, :, 0, :], qk[:, :, 1, :]
                c, s = (rope[:, b, j:j + 1, :].to_broadcast([P, KT, P // 2]) for j in range(2))
                for dst, t, w in ((rt[0], t1, c), (rt[1], t2, s), (rt[2], t1, s), (rt[3], t2, c)):
                    link.mark(dve.tensor_tensor(dst[:, :, :], t, w, ALU.mult))
                link.sync()
                link.mark(dve.tensor_tensor(t1, rt[0][:, :, :], rt[1][:, :, :], ALU.subtract))
                link(dve.tensor_tensor(t2, rt[2][:, :, :], rt[3][:, :, :], ALU.add))
                dve.sem_inc(sem("rope_ready"), 1)
            o = COL["zeta"][0]
            dve.tensor_tensor(ret_kz[:, :, :], Pin[:, 0, C_Q + 1024:C_V].rearrange("p (h e) -> p h e", e=P),
                              cols[:, o:o + HEADS].unsqueeze(2).to_broadcast([P, HEADS, P]), ALU.mult).then_inc(
                sem("ret_kz_ready"), 1)
            dve.wait_ge(sem("decay_landed"), 16)
            for j in range(4):
                dve.wait_ge(sem("ret_scores"), j + 1)
                for m in range(2):
                    h = 2 * j + m
                    ins = dve.tensor_tensor(ret_s[:, h, :, :], DB[j][:, m * T:(m + 1) * T].rearrange("p (n q) -> p n q", q=P),
                                            decay[:, h:h + 1, :].to_broadcast([P, NB, P]), ALU.mult)
                ins.then_inc(sem("ret_s_ready"), 1)
            dve.wait_ge(sem("ret_inner"), 1)
            for j in range(2):
                link.mark(dve.tensor_copy(ret_o[:, 0, 4 * j:4 * j + 4, :], bank[j][:, :].rearrange("p (h e) -> p h e", e=P)))
            dve.wait_ge(sem("ret_cross"), 1)
            o = COL["xi"][0]
            for j in range(2):
                link(dve.tensor_tensor(ret_o[:, 1, 4 * j:4 * j + 4, :], DB[2 + j][:, :].rearrange("p (h e) -> p h e", e=P),
                                       cols[:, o + 4 * j:o + 4 * j + 4].unsqueeze(2).to_broadcast([P, 4, P]), ALU.mult))
                link(dve.tensor_tensor(ret_o[:, 1, 4 * j:4 * j + 4, :], ret_o[:, 1, 4 * j:4 * j + 4, :],
                                       bank[2 + j][:, :].rearrange("p (h e) -> p h e", e=P), ALU.add))
            heads = ret_o[:, :, :, :].rearrange("p n h e -> p (n h) e")
            sq = ret_sq[:, :, :, :].rearrange("p n h e -> p (n h) e")
            nh = [P, NB * HEADS, P]
            link(dve.tensor_reduce(gn[0][:, :], heads, AX.X, ALU.add))
            link(dve.tensor_scalar(gn[0][:, :], gn[0][:, :], 1.0 / P, None, ALU.mult))
            link(dve.tensor_tensor(heads, heads, gn[0][:, :].unsqueeze(2).to_broadcast(nh), ALU.subtract))
            link(dve.tensor_tensor(sq, heads, heads, ALU.mult))
            link(dve.tensor_reduce(gn[0][:, :], sq, AX.X, ALU.add))
            dve.tensor_scalar(gn[0][:, :], gn[0][:, :], 1.0 / P, EPS, ALU.mult, ALU.add).then_inc(sem("gn_var"), 1)
            dve.wait_ge(sem("gn_root"), 1)
            link(dve.reciprocal(gn[2][:, :], gn[1][:, :]))
            link(dve.tensor_tensor(heads, heads, gn[2][:, :].unsqueeze(2).to_broadcast(nh), ALU.mult))
            dve.wait_ge(sem("ret_gate"), 1)
            dve.tensor_tensor(ret_o[:, :, :, :].rearrange("p n h e -> p n (h e)"),
                              ret_o[:, :, :, :].rearrange("p n h e -> p n (h e)"), Pin[:, :, C_G:C_G + 1024],
                              ALU.mult).then_inc(sem("ret_o_ready"), 1)
            for h in range(HEADS):
                dve.wait_ge(sem("ret_yh_ready"), h // 2 * 2 + 2)
                dve.scalar_tensor_tensor(UL[:, LB + h, :], bank[h // 2][:, (h % 2) * T:(h % 2 + 1) * T], col("gnw", h),
                                         UH[:, LB + h, :].bitcast(F32), ALU.mult, ALU.subtract).then_inc(
                    sem("y1_ready"), 1)
            linear(S_OUT, Q_OUT, OUT_TILES, add_to_x)
            dve.wait_ge(acc_free_dve, Q_FFN + 2)
            if until < 3:
                return

            link.mark(dve.memset(cond[:, :, 4:P].bitcast(F32), 0.0))
            dve.wait_ge(sem("cond_hi"), 1)
            link.mark(dve.tensor_tensor(cond[:, :, 2:4], csil[:, :, :], cond[:, :, 0:2].bitcast(F32), ALU.subtract))
            link.sync()
            dve.sem_inc(sem("cond_ready"), 1)
            norm_turned(1, 1, X, XN, lambda k: col("ln2", k))
            dve.sem_inc(sem("down_added"), 2)

            def up(i=None, nth=0):
                dve.wait_ge(acc_free_act, lin(Q_FFN + 2 + 2 * (nth + 1), i, 2))
                if i is not None:
                    dve.wait_ge(sem("ff_turned"), lin(nth, i, 1))
                for b in range(NB):
                    ins = dve.tensor_tensor(ff[:, b, :], ACC[1][b][:, :], ff_g[:, b, :], ALU.mult)
                ins.then_inc(sem("ff_ready"), 1)
                dve.sem_inc(acc_free_dve, 2)

            def turned(i=None, nth=0):
                for k in range(CK):
                    dve.wait_ge(sem("ffh_ready"), lin(CK * nth + k // 2 * 2 + 2, i, CK))
                    dve.tensor_tensor(FL[:, k, :], bank[2 + k // 2][:, (k % 2) * T:(k % 2 + 1) * T],
                                      FH[:, k, :].bitcast(F32), ALU.subtract).then_inc(sem("ffT_ready"), 1)

            def add_down(n, j, i=None, per=0):
                dve.wait_ge(split_used, lin(n + 1, i, per))
                for b in range(NB):
                    x = X[:, b, j * CW:(j + 1) * CW]
                    ins = dve.tensor_tensor(x, DB[2 * (j % 2) + b][:, :], x, ALU.add)
                ins.then_inc(sem("down_added"), 1)

            def step(kinds, n, i=None, tile=0):
                m = dict.fromkeys(kinds, 0)
                for p, kind in enumerate(kinds):
                    lo(n + LEAD + p, i, len(FF_STEP))
                    m[kind] += 1
                    if kind == "u" and m[kind] == CPT:
                        dve.wait_ge(split_used, lin(n + p + 1, i, len(FF_STEP)))
                        up(i, tile)
                    if kind == "d":
                        add_down(n + p, m[kind] - 1, i, len(FF_STEP))

            def modulation(i=None, nth=0):
                for t in range(ADA_STEP):
                    dve.wait_ge(sem("ada_cols"), lin(ADA_STEP * nth + t + 1, i, ADA_STEP))
                    w = CW // P
                    m = modt[:, bass.ds(lin(w * (ADA_STEP * nth + t), i, w * ADA_STEP), w), :]
                    dve.tensor_tensor(m, ACC[0][t][:, 0:2 * w].rearrange("p (j r) -> p j r", r=2), m, ALU.add).then_inc(
                        sem("mod_ready"), 1)

            step(FF_FIRST, S_FFN)
            turned()
            modulation()
            with dve.Fori(0, FT - 1) as i:
                step(FF_STEP, S_STEP, i, tile=1)
                modulation(i, 1)
                turned(i, 1)
            step(FF_LAST, S_LAST)
            modulation(nth=FT)
            dve.wait_ge(sem("down_added"), 2 + FT * OUT_TILES)
            if until < 4:
                return

            dve.wait_ge(sem("mod_ready"), ADA_TILES)
            for r in range(2):
                link(dve.scalar_tensor_tensor(sc_mix[:, r, :], modt[:, KT:2 * KT, r], 1.0, col("nmix", 0, KT), ALU.add,
                                              ALU.mult))
            link(dve.scalar_tensor_tensor(sc_ffn[:, :], modt[:, 4 * KT:5 * KT, 0], 1.0, col("nffn", 0, KT), ALU.add,
                                          ALU.mult))

            norm_rows(2, X, XN)
            dve.wait_ge(sem("xn_ready"), 2 * 3)
            dve.wait_ge(sem("fnw_landed"), 16)
            for b in range(NB):
                link.mark(dve.tensor_tensor(X[:, b, :], XN[:, b, :], fnw[:, :], ALU.mult))
            link.sync()
            dve.sem_inc(sem("x2_ready"), 1)

            def conv(S, dst, taps, padded, base):
                for j in range(4):
                    dve.wait_ge(sem(padded), base + (4 if S.lat else j + 1))
                    for tap in range(3):
                        for b in (2 * j, 2 * j + 1):
                            w, x = col("qkconv", tap * 2 * MB + taps + b), S.pad[:, b, tap:tap + T]
                            if tap == 0:
                                link.mark(dve.tensor_scalar(dst(b), x, w, None, ALU.mult))
                            else:
                                link.mark(dve.scalar_tensor_tensor(dst(b), x, w, dst(b), ALU.mult, ALU.add))
                        link.sync()

            def edges(S):
                for t in (0, T + 1):
                    link.mark(dve.memset(S.pad[:, :, t:t + 1], 0.0))
                link.sync()

            def gates(s):
                dve.wait_ge(sem("gate_ps"), s + 1)
                dve.tensor_copy(gtok[:, :, :], DB[2][:, 0:NB * NG].rearrange("p (b g) -> p b g", g=NG)).then_inc(
                    sem("gtok_ready"), 1)

            def gate_rows(S):
                dve.wait_ge(sem("gate_rows_ps"), S.s + 1)
                for typ, dst in ((0, S.A), (1, S.lf)):
                    for d in range(2):
                        link.mark(dve.tensor_scalar(dst[:, d, :], DB[2 + typ][0:MH, d * T:(d + 1) * T],
                                                    col("bgate", 2 * d + typ, rows=MH), None, ALU.add))
                link.sync()
                dve.scalar_tensor_tensor(S.b, S.lf, -1.0, S.lf, ALU.mult, ALU.max).then_inc(sem("fg_abs"), 1)
                link(dve.memset(S.M, 0.0))
                dve.wait_ge(sem("fg_log"), S.s + 1)
                link(dve.scalar_tensor_tensor(S.lf, S.lf, 0.0, S.b, ALU.min, ALU.subtract))
                for d in range(2):
                    for n in range(NB):
                        link.mark(dve.tensor_tensor_scan(scan_ap(S.b, d, n), scan_ap(S.lf, d, n), scan_ap(S.M, d, n), 0.0,
                                                         ALU.add, ALU.add))
                link.sync()
                link(dve.tensor_tensor(S.A, S.A, S.b, ALU.subtract))
                for step, d, n in S.steps:
                    m0 = NB * S.s + step
                    link(dve.tensor_tensor_scan(scan_ap(S.M, d, n), scan_ap(S.A, d, n), scan_ap(S.A, d, n),
                                                m_st[0:MH, d, m0:m0 + 1], ALU.max, ALU.max))
                    last = last_of(S.M, d, n)
                    link.mark(dve.tensor_tensor(m_st[0:MH, d, m0 + 1:m0 + 2], last_of(S.b, d, n), last, ALU.add))
                    link.mark(dve.tensor_scalar(n_ml[0:MH, d, n:n + 1], last, -1.0, None, ALU.mult))
                    link(dve.tensor_tensor(dcy[0:MH, d, n:n + 1], m_st[0:MH, d, m0:m0 + 1], last, ALU.subtract))
                if S.lat:
                    link(dve.tensor_tensor(S.ex, S.b, S.M, ALU.add))
                dve.sem_inc(sem("row_max"), 1)
                if S.lat:
                    link(dve.tensor_scalar(S.b, S.M, -1.0, None, ALU.mult))
                dve.wait_ge(sem("rows_exp"), S.s + 1)
                dve.sem_inc(sem("rows_ready"), 1)

            def columns(S):
                dve.wait_ge(sem("cols_ps"), S.s + 1)
                for k in range(5) if S.lat else (1, 4):
                    w = 2 * NB * MH
                    link.mark(dve.tensor_copy(co[:, k, :, :, :].rearrange("p d n h -> p (d n h)"), DB[2][:, k * w:(k + 1) * w]))
                link.sync()
                dve.sem_inc(sem("co_ready"), 1)

            def ones(S):
                link.mark(dve.memset(S.v1[:, :, :, MD:VA], 1.0))
                for n in range(NB):
                    link.mark(dve.tensor_copy(S.v1[:, n, :, 0:MD], S.v(n).rearrange("p (h e) -> p h e", e=MD)))
                link.sync()

            upd = [0]

            def update(S, d, n):
                u = upd[0]
                for h in range(MH):
                    if u * MH + h >= 2:
                        dve.wait_ge(sem("state_ps"), u * MH + h - 1)
                    dve.tensor_scalar(vw[:, h % 2, :], S.v1[:, n, h, :], co[:, 1, d, n, h:h + 1], None, ALU.mult).then_inc(
                        sem("vw_ready"), 1)
                for h in range(MH):
                    dve.wait_ge(sem("state_ps"), u * MH + h + 1)
                    for kt in range(MKT):
                        s = st[:, d, h, kt, :]
                        link.mark(dve.scalar_tensor_tensor(s, s, co[:, 4, d, n, h:h + 1], ALLB[2 * h + kt][:, 0:VA], ALU.mult,
                                                           ALU.add))
                link.sync()
                dve.sem_inc(sem("state_ready"), 1)
                upd[0] += 1

            dve.wait_ge(sem("ctx_landed"), 16)
            norm_turned(3, 2, ctx_x, ctx_n, lambda k: sc_mix[:, 1, k:k + 1], lambda k: modt[:, k, 1:2])
            linear(S_CTX, Q_CTX, CTX_TILES, to(lambda t: kv[:, 1, bass.ds(t * CW, CW)], CW))
            if until < 5:
                return
            C = streams[0]
            gates(0)
            edges(C)
            link.mark(dve.memset(m_st[0:MH, :, :], 0.0))
            link.mark(dve.memset(st[:, :, :, :, :], 0.0))
            conv(C, C.kT, MB, "k_pad_ready", 0)
            dve.sem_inc(sem("k_conv"), 1)
            gate_rows(C)
            dve.wait_ge(sem("k_silu"), 1)
            dve.wait_ge(acc_free_act, Q_IN2 + 2)
            dve.wait_ge(acc_free_dve, Q_IN2 + 2)
            ones(C)
            columns(C)
            for step, d, n in C.steps:
                update(C, d, n)
            dve.sem_inc(sem("ctx_done"), 1)
            if until < 6:
                return

            norm_turned(4, 3, X, XN2, lambda k: sc_mix[:, 0, k:k + 1], lambda k: modt[:, k, 0:1])
            linear(S_IN2, Q_IN2, W2_TILES, to(lambda t: P2[:, 1, bass.ds(t * CW, CW)], CW))
            gates(1)
            if until < 7:
                return
            for g in range(len(PW)):
                dve.wait_ge(sem("yh2_ready"), g // 2 * 2 + 2)
                dve.scalar_tensor_tensor(UL[:, 12 + g, :], bank[g // 2][:, (g % 2) * T:(g % 2 + 1) * T], col("pscale", g),
                                         UH[:, 12 + g, :].bitcast(F32), ALU.mult, ALU.subtract).then_inc(sem("y2_ready"), 1)
            dve.wait_ge(sem("sgu_gelu"), 1)
            dve.wait_ge(sem("sgu_n_landed"), 16)
            for b in range(NB):
                v = P2[:, b, O_V:O_P]
                link(dve.tensor_tensor_reduce(sgu_sq[:, :], v, v, 1.0, 0.0, ALU.mult, ALU.add, ss[:, b:b + 1]))
            dve.tensor_scalar(ms[:, :], ss[:, :], 1.0 / D_SGU, EPS, ALU.mult, ALU.add).then_inc(sem("sgu_ms"), 1)
            dve.wait_ge(sem("sgu_root"), 1)
            link(dve.reciprocal(rinv[:, :], rms[:, :]))
            for b in range(NB):
                v = P2[:, b, O_V:O_P]
                ins = dve.scalar_tensor_tensor(v, v, rinv[:, b:b + 1], sgu_n[:, :], ALU.mult, ALU.mult)
            ins.then_inc(sem("sgu_v_ready"), 1)
            dve.wait_ge(sem("sgu_ps"), 1)
            for n in range(NB):
                for h in range(SH):
                    u = P2[:, n, O_U + h * P:O_U + (h + 1) * P]
                    ins = dve.scalar_tensor_tensor(u, DB[n][:, h * P:(h + 1) * P], col("sgub", h), u, ALU.add, ALU.mult)
            ins.then_inc(sem("sgu_y_ready"), 1)
            for k in range(4):
                dve.wait_ge(sem("yh2_ready"), 4 + k // 2 * 2 + 2)
                dve.tensor_tensor(UL[:, k, :], DB[k // 2][:, (k % 2) * T:(k % 2 + 1) * T], UH[:, k, :].bitcast(F32),
                                  ALU.subtract).then_inc(sem("y2_ready"), 1)
            L = streams[1]
            dve.wait_ge(sem("pool_y_ps"), len(PW))
            edges(L)
            qT = lat_half(O_Q)
            conv(L, qT, 0, "q_pad_ready", 0)
            dve.sem_inc(sem("q_conv"), 1)
            conv(L, L.kT, MB, "k_pad_ready", 4)
            dve.sem_inc(sem("k_conv"), 1)
            dve.wait_ge(acc_free_act, Q_OUT2 + 2)
            dve.wait_ge(acc_free_dve, Q_OUT2 + 2)
            ones(L)
            dve.sem_inc(sem("v1_ready"), 1)
            gate_rows(L)
            dve.wait_ge(sem("ml_scores"), 1)
            for j in range(2):
                link.mark(dve.tensor_copy(sc_t[:, 2 * j:2 * j + 2, :, :].rearrange("p h n t -> p (h n t)"), DB[j][:, :]))
            link.sync()
            dve.sem_inc(sem("sc_t_ready"), 1)
            columns(L)
            x = 0
            for step, d, n in L.steps:
                def weights(h):
                    dve.wait_ge(sem("w_exp"), x + h + 1)
                    dve.tensor_tensor(wb[:, h % 2, :], wb[:, h % 2, :], sc_t[:, h, n, :], ALU.mult).then_inc(sem("w_ready"), 1)
                weights(0)
                for h in range(MH):
                    if h + 1 < MH:
                        weights(h + 1)
                    dve.wait_ge(sem("inter_ready"), x + h + 1)
                    t = ml_t[:, h % 2, :]
                    link(dve.tensor_tensor(t, t, ACC[h % 2][0][:, 0:VA], ALU.add))
                    link(dve.scalar_tensor_tensor(den[:, 0:1], t[:, MD:VA], -1.0, t[:, MD:VA], ALU.mult, ALU.max))
                    link(dve.tensor_scalar(den[:, 0:1], den[:, 0:1], co[:, 3, d, n, h:h + 1], None, ALU.max))
                    link(dve.reciprocal(den[:, 1:2], den[:, 0:1]))
                    y = P2[:, n, O_K + h * MD:O_K + (h + 1) * MD]
                    if step == 0:
                        ins = dve.tensor_scalar(y, t[:, 0:MD], den[:, 1:2], None, ALU.mult)
                    else:
                        ins = dve.scalar_tensor_tensor(y, t[:, 0:MD], den[:, 1:2], y, ALU.mult, ALU.add)
                    ins.then_inc(sem("h_ready"), 1)
                x += MH
                dve.wait_ge(sem("h_ready"), x)
                if step == 0:
                    update(L, d, n)
            nh = [P, MH, MD]
            for n in range(NB):
                y = P2[:, n, O_K:O_K + D_ML]
                sq = P2[:, n, O_Q:O_Q + D_ML]
                link(dve.tensor_tensor(sq, y, y, ALU.mult))
                link(dve.tensor_reduce(l_ms[2][:, n * MH:(n + 1) * MH], sq.rearrange("p (h e) -> p h e", e=MD), AX.X, ALU.add))
            dve.tensor_scalar(l_ms[0][:, :], l_ms[2][:, :], 1.0 / MD, EPS, ALU.mult, ALU.add).then_inc(sem("ml_ms"), 1)
            dve.wait_ge(sem("ml_root"), 1)
            link(dve.reciprocal(l_ms[2][:, :], l_ms[1][:, :]))
            dve.wait_ge(sem("ml_gate"), 1)
            for n in range(NB):
                y = P2[:, n, O_K:O_K + D_ML]
                yh = y.rearrange("p (h e) -> p h e", e=MD)
                link(dve.tensor_tensor(yh, yh, l_ms[2][:, n * MH:(n + 1) * MH].unsqueeze(2).to_broadcast(nh), ALU.mult))
                link(dve.tensor_tensor(y, y, P2[:, n, O_O:O_O + D_ML], ALU.mult))
            dve.sem_inc(sem("ml_y_ready"), 1)
            for b in range(MB):
                dve.wait_ge(sem("yh2_ready"), 8 + b // 2 * 2 + 2)
                dve.scalar_tensor_tensor(UL[:, 4 + b, :], DB[b // 2][:, (b % 2) * T:(b % 2 + 1) * T], col("mlnorm", b),
                                         UH[:, 4 + b, :].bitcast(F32), ALU.mult, ALU.subtract).then_inc(sem("y2_ready"), 1)
            if until < 8:
                return

            def add_gated(par, t):
                for b in range(NB):
                    ins = dve.tensor_tensor(g_tmp[:, b, :], ACC[par][b][:, :], gb1[:, bass.ds(t * CW, CW)], ALU.mult)
                ins.then_inc(sem("gated"), 1)
                dve.wait_ge(sem("gated"), t + 1)
                for b in range(NB):
                    x = X[:, b, bass.ds(t * CW, CW)]
                    ins = dve.tensor_tensor(x, g_tmp[:, b, :], x, ALU.add)
                ins.then_inc(acc_free_dve, 1)

            dve.wait_ge(sem("spread_ready"), 8)
            linear(S_OUT2, Q_OUT2, OUT_TILES, add_gated)
            dve.wait_ge(acc_free_dve, Q_WQ + 2)
            norm_turned(5, 4, X, XN2, lambda k: sc_ffn[:, k:k + 1], lambda k: modt[:, 3 * KT + k, 0:1])
            linear(S_WQ, Q_WQ, OUT_TILES, to(lambda t: q_tok[:, 1, bass.ds(t * CW, CW)], CW))
            dve.wait_ge(sem("spread_ready"), 16)
            for b in range(NB):
                link(dve.tensor_tensor(XN2[:, b, :], XN2[:, b, :], sc_row[:, :], ALU.mult))
                link(dve.tensor_tensor(XN2[:, b, :], XN2[:, b, :], sh_row[:, :], ALU.add))
                dve.sem_inc(sem("hf_ready"), 1)
            if until < 9:
                return

            def top16(values, keep, pos):
                for r in range(2):
                    w = slice(8 * r, 8 * r + 8)
                    for v, k in zip(values, keep):
                        link.mark(dve.max(k[:, w], v))
                    link.sync()
                    for v, k, p in zip(values, keep, pos):
                        link.mark(dve.max_index(p[:, w], k[:, w], v))
                        if r == 0:
                            link.mark(dve.match_replace(v, k[:, w], v, LOWEST))
                    link.sync()

            def choose(b):
                dve.wait_ge(sem("key_s_ready"), 8)
                top16([key_s[:, b, hp, :] for hp in range(2 * PH)], [top_v[:, hp, :] for hp in range(2 * PH)],
                      [top_i[:, hp, :] for hp in range(2 * PH)])
                link.mark(dve.tensor_copy(top_f[:, :, :], top_i[:, :, :]))
                both = top_v[:, :, :].rearrange("p (h s) k -> p h s k", s=2)
                full = [P, PH, TOPK, TOPK]
                link(dve.tensor_tensor(cand[:, :, :, :], both[:, :, 0, :].unsqueeze(3).to_broadcast(full),
                                       both[:, :, 1, :].unsqueeze(2).to_broadcast(full), ALU.add))
                top16([cand[:, h, :, :].rearrange("p a b -> p (a b)") for h in range(PH)], [best_v[:, h, :] for h in range(PH)],
                      [best_i[:, h, :] for h in range(PH)])
                ranks = best_i[:, :, :].rearrange("p h k -> p (h k)")
                of = top_f[:, :, :].rearrange("p (h s) k -> p h s k", s=2)
                hots = hot[:, :, :, :].rearrange("p h j k -> p (h j) k")
                o = COL["iota"][0]
                for s in range(2):
                    op, by = (ALU.logical_shift_right, 4) if s == 0 else (ALU.bitwise_and, TOPK - 1)
                    link(dve.tensor_scalar(pick_i[:, :], ranks, by, None, op))
                    link(dve.tensor_copy(pick_f[:, :], pick_i[:, :]))
                    link(dve.tensor_tensor(hots, cols[:, o:o + TOPK].unsqueeze(1).to_broadcast([P, SLOTS, TOPK]),
                                           pick_f[:, :].unsqueeze(2).to_broadcast([P, SLOTS, TOPK]), ALU.is_equal))
                    link(dve.tensor_tensor(hot[:, :, :, :], hot[:, :, :, :], of[:, :, s, :].unsqueeze(2).to_broadcast(full),
                                           ALU.mult))
                    link(dve.tensor_reduce(exp_f[s][:, :], hots, AX.X, ALU.add))
                link(dve.scalar_tensor_tensor(pick_f[:, :], exp_f[0][:, :], float(NKEY), exp_f[1][:, :], ALU.mult, ALU.add))
                dve.tensor_copy(idx[:, b, :], pick_f[:, :]).then_inc(sem("idx_ready"), 1)
                w = gate_w[:, b, :].rearrange("p (h k) -> p h k", k=TOPK)
                dve.tensor_tensor(w, best_v[:, :, :], best_v[:, :, 0:1].to_broadcast([P, PH, TOPK]), ALU.subtract).then_inc(
                    sem("best_ready"), 1)
                dve.wait_ge(sem("soft_exp"), b + 1)
                link(dve.tensor_reduce(soft[:, :], w, AX.X, ALU.add))
                link(dve.reciprocal(soft[:, :], soft[:, :]))
                link(dve.tensor_tensor(w, w, soft[:, :].unsqueeze(2).to_broadcast([P, PH, TOPK]), ALU.mult))

            def landed(g0, s, i):
                dve.wait_ge(sem(f"row_landed{s % GATH}"), lin(16 * ((g0 + s) // GATH + 1), i, 16 * GSTEP // GATH))

            dve.sem_inc(sem("row_used"), GATH)
            for b in range(NB):
                choose(b)
            for b in range(NB):
                g0 = b * SLOTS
                with dve.Fori(0, SLOTS // GSTEP) as i:
                    for s in range(GSTEP):
                        landed(g0, s, i)
                        r = rows_g[:, s % GATH, :]
                        dve.tensor_tensor_reduce(r, r, XN2[:, b, :], 1.0, 0.0, ALU.mult, ALU.add,
                                                 step_dots[:, s:s + 1]).then_inc(sem("row_used"), 1)
                    dve.wait_ge(sem("row_used"), lin(GATH + g0 + GSTEP, i, GSTEP))
                    dve.tensor_copy(dots[:, b, bass.ds(i * GSTEP, GSTEP)], step_dots[:, :]).then_inc(sem("dots_kept"), 1)
                    dve.wait_ge(sem("dots_kept"), lin(b * SLOTS // GSTEP + 1, i, 1))
            dve.wait_ge(sem("dots_kept"), NB * SLOTS // GSTEP)
            dve.sem_inc(sem("dots_done"), 1)
            dve.wait_ge(sem("dots_gelu"), 1)
            link(dve.tensor_tensor(gate_w[:, :, :], gate_w[:, :, :], dots[:, :, :], ALU.mult))
            for b in range(NB):
                g0 = (NB + b) * SLOTS
                link(dve.memset(v_sum[:, :, :], 0.0))
                with dve.Fori(0, SLOTS // GSTEP) as i:
                    for s in range(GSTEP):
                        landed(g0, s, i)
                        dve.wait_ge(sem("row_used"), lin(GATH + g0 + s - 1, i, GSTEP))
                        v = v_sum[:, s % 2, :]
                        dve.scalar_tensor_tensor(v, rows_g[:, s % GATH, :], gate_w[:, b, bass.ds(lin(s, i, GSTEP), 1)], v,
                                                 ALU.mult, ALU.add).then_inc(sem("row_used"), 1)
                dve.wait_ge(sem("row_used"), GATH + g0 + SLOTS)
                v = v_sum[:, 0, :]
                link(dve.tensor_tensor(v, v, v_sum[:, 1, :], ALU.add))
                link(dve.tensor_tensor(v, v, gb2[:, :], ALU.mult))
                x = X[:, b, :]
                link(dve.tensor_tensor(x, x, v, ALU.add))
                link(dve.tensor_tensor_reduce(v_sum[:, 1, :], x, x, 1.0, 0.0, ALU.mult, ALU.add, ss[:, b:b + 1]))
                dve.tensor_scalar(ms[:, b:b + 1], ss[:, b:b + 1], 1.0 / D, EPS, ALU.mult, ALU.add).then_inc(sem("fin_ms"), 1)
                dve.wait_ge(sem("fin_root"), b + 1)
                link(dve.reciprocal(rinv[:, b:b + 1], rms[:, b:b + 1]))
                dve.wait_ge(sem("nfin_landed"), 16)
                dve.scalar_tensor_tensor(x, x, rinv[:, b:b + 1], nfin[:, :], ALU.mult, ALU.mult).then_inc(
                    sem("out_ready"), 1)


def tables():
    f = np.float32
    pos, half = np.arange(T, dtype=f), P // 2
    freq = (f(10000.0) ** (-np.arange(0, P, 2, dtype=f) / f(P))).astype(f)
    ang = pos[:, None] * freq[None, :]
    rope = np.stack([np.cos(ang), np.sin(ang)], 1).astype(f).reshape(NB, P, 2, half).transpose(1, 0, 2, 3)
    lg = np.log1p(-np.exp2(-5.0 - np.arange(HEADS, dtype=np.float64)))
    k = np.arange(P)
    diff = k[None, :] - k[:, None]
    decay = np.where(diff[:, None, :] >= 0, np.exp(lg[None, :, None] * np.maximum(diff, 0)[:, None, :]), 0.0) * P ** -0.5
    xi = np.exp(lg[None, :] * (k[:, None] + 1))
    zeta = np.exp(lg[None, :] * (P - 1 - k[:, None])) * P ** -0.5
    rows = T // GRID_W
    pool = np.zeros((P, len(PW), NB, T))
    for g, w in enumerate(PW):
        def box(n):
            i = np.arange(n)
            lo, hi = np.clip(i - w // 2, 0, n), np.clip(i - w // 2 + w, 0, n)
            return ((i[None, :] >= lo[:, None]) & (i[None, :] < hi[:, None])).astype(np.float64)
        m = np.kron(box(rows), box(GRID_W))
        m = m / m.sum(1, keepdims=True) - np.eye(T)
        pool[:, g] = m.T.reshape(NB, P, T).transpose(1, 0, 2)
    mask = np.stack([np.where(diff >= 0, 0.0, -1e30), np.where(diff <= 0, 0.0, -1e30)], 1)
    sel = np.zeros((P, 2))
    sel[[0, 2], 0] = sel[[1, 3], 1] = 1.0
    out = {"rope": rope, "decay": decay, "pool_t": pool, "mask": mask, "ident": np.eye(P), "xi": xi, "zeta": zeta, "sel": sel,
           "iota": np.tile(np.arange(TOPK), (P, 1))}
    return {n: np.ascontiguousarray(v, dtype=f) for n, v in out.items()}


def chunks(w, rows_first=False):
    k, n = w.shape
    c = w.reshape(k // (CK * P), CK, P, n // CW, CW)
    c = c.transpose(0, 3, 2, 1, 4) if rows_first else c.transpose(3, 0, 2, 1, 4)
    return c.reshape(c.shape[0], c.shape[1], P, CK * CW)


def layout(v):
    t = tables()
    one = {n: np.asarray(x) for n, x in v.items()}
    first = {n: x[0] for n, x in one.items() if n not in ("x", "final_norm_w", "c_ctx_2", "ctx_2", "c_2", "norm_final_2")}
    stream = np.empty((NCH, P, CK * CW), np.float32)

    def put(at, c):
        c = c.reshape(-1, P, CK * CW)
        stream[at:at + len(c)] = c

    w2 = first["w_in_2"]
    put(S_IN, chunks(first["w_in"]))
    put(S_OUT, chunks(first["w_out"]))
    gate, up, down = chunks(first["w_ffn_gate"]), chunks(first["w_ffn_up"]), chunks(first["w_ffn_down"], True)
    ada = chunks(first["ada_w_2"])
    at = S_FFN
    for i in range(FT + 1):
        rest = {"g": list(gate[i]), "u": list(up[i])} if i < FT else {}
        rest["a"] = list(ada[ADA_STEP * i:ADA_STEP * (i + 1)].reshape(-1, P, CK * CW))
        rest["d"] = list(down[i - 1]) if i else []
        for kind in FF_FIRST if i == 0 else FF_STEP if i < FT else FF_LAST:
            stream[at] = rest[kind].pop(0)
            at += 1
    put(S_CTX, chunks(w2[:, O_K:O_G]))
    put(S_IN2, chunks(w2[:, :O_G]))
    put(S_OUT2, chunks(first["w_out_2"]))
    put(S_WQ, chunks(first["peer_wq_2"]))

    def down_cols(x):
        return np.ascontiguousarray(x.reshape(-1, P).T)

    parts = {"ln1": down_cols(first["ln1_w"]), "ln2": down_cols(first["ln2_w"]), "ba": down_cols(first["gate_a_b"]),
             "bx": down_cols(first["gate_x_b"]), "conv": down_cols(first["conv_w"]), "convb": down_cols(first["conv_b"]),
             "lam": down_cols(first["lru_lambda"]), "gnw": down_cols(first["ret_gn_w"]), "nmix": down_cols(first["norm_mix_2"]),
             "nffn": down_cols(first["norm_ffn_2"]), "ada_b": down_cols(first["ada_b_2"]),
             "qkconv": down_cols(first["qk_conv_2"]), "mlnorm": down_cols(first["mlstm_norm_2"]),
             "pscale": down_cols(first["pool_scale_2"]), "c": down_cols(one["c_2"]), "cctx": down_cols(one["c_ctx_2"]),
             "sgub": down_cols(first["sgu_b_2"]), "xi": t["xi"], "zeta": t["zeta"], "sel": t["sel"], "iota": t["iota"]}
    cols = np.zeros((P, NCOL), np.float32)
    for name, x in parts.items():
        o, w = COL[name]
        cols[:, o:o + w] = x
    o, w = COL["bgate"]
    cols[0:MH, o:o + w] = first["b_gate_2"].reshape(4, MH).T

    def c(x):
        return np.ascontiguousarray(x)

    return {
        "x": one["x"], "ctx": one["ctx_2"], "wstream": stream, "cols": cols, "ident": t["ident"],
        "wa": c(first["gate_a_w"].transpose(1, 0, 2)), "wx": c(first["gate_x_w"].transpose(1, 0, 2)),
        "decay": t["decay"], "rope": t["rope"], "pool_t": t["pool_t"], "mask": t["mask"],
        "sgu_w": c(first["sgu_w_2"].transpose(2, 0, 1)), "pool_w": c(first["pool_w_2"].transpose(1, 0, 2)),
        "keys": c(first["peer_keys_2"].transpose(2, 0, 1)),
        "wg": c(w2[:, O_G:].reshape(KT, P, NG).transpose(1, 0, 2)),
        "fnw": one["final_norm_w"], "nfin": one["norm_final_2"], "sgu_n": first["sgu_norm_2"],
        "u_tab": first["peer_u_2"], "v_tab": first["peer_v_2"],
    }


def kernel(**inputs):
    import concourse.bacc as bacc
    from concourse.bass_utils import run_bass_kernel_spmd

    nc = bacc.Bacc("TRN2", target_bir_lowering=False, num_devices=1)
    arrays = {f"in_{n}_dram": np.ascontiguousarray(x) for n, x in layout(inputs).items()}
    args = {n[3:-5]: nc.dram_tensor(n, x.shape, mybir.dt.from_np(x.dtype), kind="ExternalInput").ap()
            for n, x in arrays.items()}
    out = nc.dram_tensor("out_dram", (1, T, D), F32, kind="ExternalOutput").ap()
    build(nc, args, out)
    return run_bass_kernel_spmd(nc, [arrays], core_ids=[0]).results[0]["out_dram"]
```

```python
from contextlib import ExitStack

import numpy as np
import concourse.bass as bass
from concourse import mybir

ALU = mybir.AluOpType
ACT = mybir.ActivationFunctionType
AX = mybir.AxisListType
F32 = mybir.dt.float32
F32R = mybir.dt.float32r
U32 = mybir.dt.uint32
I32 = mybir.dt.int32

P = 128
NB = 2
T = NB * P
D = 2048
KT = D // P
EPS = 1e-6
CW = 512
CK = 4
CPT = KT // CK
SLOTS_W = 4
LEAD = 2

D_LRU = 1024
LB = D_LRU // P
CONV_W = 4
LRU_C = 8.0
HEADS = 8
W_IN_TILES = 6144 // CW
W_IN_HEAD = 2
D_FF = 5632
FT = D_FF // CW
C_Q, C_V, C_G = 2048, 4096, 5120

D_SGU = 512
SH = 4
PW = (2, 4, 8, 16)
GRID_W = 64
MH = 4
MD = 256
MKT = MD // P
D_ML = MH * MD
MB = D_ML // P
O_U, O_V, O_P, O_Q, O_O, O_K, O_VM, O_G = 0, 512, 1024, 1536, 2560, 3584, 4608, 5632
W2_TILES = O_G // CW
W2_ORDER = (0, 1, 2, 3, 4, 7, 8, 9, 10, 5, 6)
W2_HEAD = 3
CTX_TILES = 2 * D_ML // CW
NG = 16
VA = MD + 1
NKEY = 128
PH = 8
TOPK = 16
SLOTS = PH * TOPK
GATH = 8
GSTEP = 2 * GATH
LOWEST = -3.0e38
ADA_TILES = 6 * D // CW
ADA_STEP = 2
OUT_TILES = D // CW
FF_FIRST = "gggg" + "uauauaua" + "aaaa"
FF_STEP = "gggg" + "uauauaua" + "dadadaad"
FF_LAST = "aad" * 4

S_IN = 0
S_OUT = S_IN + W_IN_TILES * CPT
S_FFN = S_OUT + OUT_TILES * CPT
S_STEP = S_FFN + len(FF_FIRST)
S_LAST = S_STEP + (FT - 1) * len(FF_STEP)
S_CTX = S_LAST + len(FF_LAST)
S_IN2 = S_CTX + CTX_TILES * CPT
S_OUT2 = S_IN2 + W2_TILES * CPT
S_WQ = S_OUT2 + OUT_TILES * CPT
NCH = S_WQ + OUT_TILES * CPT

Q_IN = 0
Q_OUT = Q_IN + W_IN_TILES
Q_FFN = Q_OUT + OUT_TILES
Q_CTX = Q_FFN + 2 * FT
Q_IN2 = Q_CTX + CTX_TILES
Q_OUT2 = Q_IN2 + W2_TILES
Q_WQ = Q_OUT2 + OUT_TILES

COL, NCOL = {}, 0
for _name, _w in (("ln1", KT), ("ln2", KT), ("ba", LB), ("bx", LB), ("conv", CONV_W * LB), ("convb", LB), ("lam", LB),
                  ("gnw", HEADS), ("nmix", KT), ("nffn", KT), ("ada_b", 6 * KT), ("qkconv", 3 * 2 * MB), ("mlnorm", MB),
                  ("pscale", len(PW)), ("c", KT), ("cctx", KT), ("sgub", SH), ("bgate", 4), ("xi", HEADS),
                  ("zeta", HEADS), ("sel", 2), ("iota", TOPK)):
    COL[_name] = (NCOL, _w)
    NCOL += _w

C1 = {"wa": 0, "wx": 1024, "decay": 2048, "rope": 3072, "_": 3584}
C2 = {"pool": 0, "sguw": 2048, "poolw": 2560, "keys": 3072, "mask": 3328, "_": 3584}


def pause(slots):
    for _ in range(slots):
        yield


def lin(const, i=None, step=0):
    return const if i is None else i * step + const


def build(nc, a, out, until=99):
    with ExitStack() as ctx:
        sems = {}

        def sem(name):
            if name not in sems:
                sems[name] = ctx.enter_context(nc.semaphore(name))
            return sems[name]

        class Chain:

            def __init__(self, eng, name):
                self.eng, self.sem, self.n = eng, sem(name), 0

            def mark(self, ins):
                self.n += 1
                ins.then_inc(self.sem, 1)

            def sync(self):
                self.eng.wait_ge(self.sem, self.n)

            def __call__(self, ins):
                self.mark(ins)
                self.sync()

        region, words = {}, 0
        for name, n in (("ident", P), ("cols", 512), ("modt", 12 * KT), ("small", 512), ("X", NB * D), ("UH", KT * T),
                        ("UL", KT * T), ("RAW", SLOTS_W * D), ("WH", SLOTS_W * D), ("P", 12288),
                        ("TMP", 6176), ("C", 3584), ("MISC", 1120)):
            region[name] = words
            words += n
        arena = ctx.enter_context(nc.sbuf_tensor("arena", [P, words], F32))
        arena_at = nc.lookup_mloc(arena).addr

        def view(name, where, off, shape, dt=F32):
            return nc.alloc_sbuf_tensor_at(name, [P] + shape, dt, offset=arena_at + 4 * (region[where] + off))

        ident = view("ident", "ident", 0, [P])
        cols = view("cols", "cols", 0, [512])
        modt = view("modt", "modt", 0, [6 * KT, 2])
        X = view("X", "X", 0, [NB, D])
        UH = view("UH", "UH", 0, [KT, T], F32R)
        UL = view("UL", "UL", 0, [KT, T], F32R)
        raw = view("raw", "RAW", 0, [SLOTS_W, CK * CW])
        WH = view("WH", "WH", 0, [SLOTS_W, CK * CW], F32R)
        WL = view("WL", "RAW", 0, [SLOTS_W, CK * CW], F32R)
        bank = [ctx.enter_context(nc.psum_tensor(f"bank{i}", [P, CW], F32)) for i in range(8)]
        ACC = [bank[0:2], bank[2:4]]
        DB = bank[4:8]
        ALLB = DB + bank[0:4]

        small_at = [0]

        def tiny(name, shape, dt=F32):
            n = int(np.prod(shape))
            v = view(name, "small", small_at[0], shape, dt)
            small_at[0] += -(-n // 8) * 8
            assert small_at[0] <= 512
            return v

        def col(name, j=0, n=1, rows=P):
            o, w = COL[name]
            assert j + n <= w
            return cols[0:rows, o + j:o + j + n]

        ss = tiny("ss", [NB])
        ms = tiny("ms", [NB])
        rms = tiny("rms", [NB])
        rinv = tiny("rinv", [NB])
        sc_mix = tiny("sc_mix", [2, KT])
        sc_ffn = tiny("sc_ffn", [KT])
        csil = tiny("csil", [KT, 2])
        lam_t = [tiny(f"lam_t{i}", [LB]) for i in range(5)]
        p_col = tiny("p_col", [LB])
        n_col = tiny("n_col", [LB])
        gn = [tiny(f"gn{i}", [NB * HEADS]) for i in range(3)]

        raw_landed = [sem(f"raw_landed{s}") for s in range(SLOTS_W)]
        hi_ready, lo_ready, split_used = sem("hi_ready"), sem("lo_ready"), sem("split_used")
        acc_free_act, acc_free_dve = sem("acc_free_act"), sem("acc_free_dve")

        Pin = view("Pin", "P", 0, [NB, 6144])
        XN = view("XN", "TMP", 0, [NB, D])
        mod_tmp = view("mod_tmp", "MISC", 0, [2, T])
        wa = view("wa", "C", C1["wa"], [LB, P])
        wx = view("wx", "C", C1["wx"], [LB, P])
        decay = view("decay", "C", C1["decay"], [HEADS, P])
        rope = view("rope", "C", C1["rope"], [NB, 2, P // 2])
        lru_x = view("lru_x", "TMP", 0, [LB, T + CONV_W - 1])
        lru_b = view("lru_b", "TMP", 0, [LB, T])
        lru_u = view("lru_u", "TMP", LB * (T + CONV_W - 1), [LB, T])
        lru_g = view("lru_g", "TMP", LB * (2 * T + CONV_W - 1), [LB, T])
        rt = [view(f"rt{i}", "TMP", 1024 * i, [KT, P // 2]) for i in range(4)]
        ret_s = view("ret_s", "TMP", 0, [HEADS, NB, P])
        ret_kz = view("ret_kz", "TMP", 2048, [HEADS, P])
        ret_r = view("ret_r", "TMP", 3072, [HEADS, P])
        ret_o = view("ret_o", "TMP", 4096, [NB, HEADS, P])
        ret_sq = view("ret_sq", "TMP", 0, [NB, HEADS, P])
        FH = view("FH", "P", 0, [CK, T], F32R)
        FL = view("FL", "P", 1024, [CK, T], F32R)
        ff_g = view("ff_g", "P", 2048, [NB, CW])
        ff = view("ff", "P", 3072, [NB, CW])
        fnw = view("fnw", "P", 4096, [D])
        cond = view("cond", "P", 8192, [KT, P], F32R)
        ada_rows = view("ada_rows", "P", 10240, [ADA_STEP, CW])

        def half(j):
            return lambda b: Pin[:, b // 4, 1024 * j + (b % 4) * T:1024 * j + (b % 4 + 1) * T]

        def wide(j):
            return Pin[:, :, 1024 * j:1024 * (j + 1)]

        pool_t = view("pool_t", "C", C2["pool"], [len(PW), NB, T])
        sgu_w = view("sgu_w", "C", C2["sguw"], [SH, P])
        pool_w = view("pool_w", "C", C2["poolw"], [len(PW), P])
        keys = view("keys", "C", C2["keys"], [2, NKEY])
        mask = view("mask", "C", C2["mask"], [2, P])
        wg = view("wg", "MISC", 776, [KT, NG])
        wg_h = [view("wg_h0", "P", 10768, [KT, NG], F32R), view("wg_h1", "TMP", 5136, [KT, NG], F32R)]
        wg_l = [view("wg_l0", "P", 10768 + KT * NG, [KT, NG], F32R), view("wg_l1", "TMP", 5136 + KT * NG, [KT, NG], F32R)]
        g_row = [view("g_row0", "P", 10768 + 2 * KT * NG, [T]), view("g_row1", "TMP", 5136 + 2 * KT * NG, [T])]
        ctx_x = view("ctx_x", "P", 0, [NB, D])
        ctx_n = view("ctx_n", "P", D * NB, [NB, D])
        kv = view("kv", "P", 0, [NB, 2 * D_ML])
        c_pad = view("c_pad", "P", 4096, [MB, T + 2])
        c_k = view("c_k", "P", 6160, [MB, T])
        c_ktok = view("c_ktok", "P", 8208, [NB, D_ML])
        c_v1 = view("c_v1", "P", 4096, [NB, MH, VA])
        c_rows = [view(f"c_rows{i}", "TMP", 4112 + 512 * i, [2, T]) for i in range(4)] + [view("c_rows4", "P", 10256, [2, T])]
        st = view("st", "TMP", 0, [2, MH, MKT, VA])
        P2 = view("P2", "P", 0, [NB, O_G])
        XN2 = view("XN2", "P", 0, [NB, D])
        l_pad = view("l_pad", "TMP", 4112, [MB, T + 2])
        l_v1 = view("l_v1", "TMP", 4112, [NB, MH, VA])
        pool_d = view("pool_d", "TMP", 4112, [len(PW), T])
        sc_t = view("sc_t", "P", NB * O_G, [MH, NB, P])
        pool_y = view("pool_y", "C", C2["pool"], [len(PW), T])
        sgu_t = view("sgu_t", "C", C2["pool"] + len(PW) * T, [D_SGU // P, T])
        sgu_n = view("sgu_n", "P", NB * O_G, [D_SGU])
        sgu_sq = view("sgu_sq", "P", NB * O_G + D_SGU, [D_SGU])
        ml_t = view("ml_t", "MISC", 0, [2, VA])
        vw = view("vw", "MISC", 0, [2, VA])
        wb = view("wb", "MISC", 520, [2, P])
        gb1 = view("gb1", "TMP", 0, [D])
        gb2 = view("gb2", "TMP", D, [D])
        g_tmp = view("g_tmp", "MISC", 0, [NB, CW])
        sc_row = view("sc_row", "P", 4096, [D])
        sh_row = view("sh_row", "P", 6144, [D])
        q_tok = view("q_tok", "P", 8192, [NB, D])
        q_t = view("q_t", "P", 4096, [2 * PH, T])
        key_s = view("key_s", "P", 8192, [NB, 2 * PH, NKEY])
        cand = view("cand", "TMP", 0, [PH, TOPK, TOPK])
        hot = view("hot", "TMP", 4096, [PH, TOPK, TOPK])
        top_v = view("top_v", "MISC", 0, [2 * PH, TOPK])
        top_i = view("top_i", "MISC", 256, [2 * PH, TOPK], U32)
        top_f = view("top_f", "MISC", 512, [2 * PH, TOPK])
        best_v = view("best_v", "MISC", 768, [PH, TOPK])
        best_i = view("best_i", "MISC", 896, [PH, TOPK], U32)
        pick_i = view("pick_i", "P", 4096, [SLOTS], U32)
        pick_f = view("pick_f", "P", 4096 + SLOTS, [SLOTS])
        exp_f = [view(f"exp_f{i}", "P", 4096 + SLOTS * (2 + i), [SLOTS]) for i in range(2)]
        soft = view("soft", "P", 4096 + SLOTS * 4, [PH])
        idx = view("idx", "P", 4096 + SLOTS * 5, [NB, SLOTS], U32)
        gate_w = view("gate_w", "P", 4096 + SLOTS * 7, [NB, SLOTS])
        dots = view("dots", "P", 4096 + SLOTS * 9, [NB, SLOTS])
        step_dots = view("step_dots", "P", 4096 + SLOTS * 11, [GSTEP])
        step_idx = view("step_idx", "P", 4096 + SLOTS * 12, [2, GATH], U32)
        v_sum = view("v_sum", "P", 8192, [2, D])
        nfin = view("nfin", "TMP", 0, [D])
        rows_g = view("rows_g", "RAW", 0, [GATH, D])
        m_st = tiny("m_st", [2, 2 * NB + 1])
        n_ml = tiny("n_ml", [2, NB])
        dcy = tiny("dcy", [2, NB])
        co = tiny("co", [5, 2, NB, MH])
        den = tiny("den", [2])
        l_ms = [tiny(f"l_ms{i}", [NB * MH]) for i in range(3)]

        def lat_half(o):
            return lambda b: P2[:, b // 4, o + (b % 4) * T:o + (b % 4 + 1) * T]

        l_rows = [P2[0:MH, 0, 512 * i:512 * (i + 1)].rearrange("p (d t) -> p d t", d=2) for i in range(3)] + \
                 [P2[0:MH, 1, 512 * i:512 * (i + 1)].rearrange("p (d t) -> p d t", d=2) for i in range(3)]

        class Stream:

            def __init__(self, s):
                self.s, self.lat = s, s == 1
                v = (c_pad, c_k, c_ktok, c_v1)
                if not self.lat:
                    self.pad, self.v1 = c_pad, c_v1
                    self.kT = lambda b: c_k[:, b, :]
                    self.k_raw = lambda n, b: kv[:, n, b * P:(b + 1) * P]
                    self.k_tok = lambda n, o, w: c_ktok[:, n, o:o + w]
                    self.v = lambda n: kv[:, n, D_ML:2 * D_ML]
                    r = [x[0:MH, :, :] for x in c_rows]
                    self.A, self.lf, self.b, self.M, self.wk = r
                else:
                    self.pad, self.v1 = l_pad, l_v1
                    self.kT = lat_half(O_K)
                    self.k_raw = lambda n, b: P2[:, n, O_K + b * P:O_K + (b + 1) * P]
                    self.k_tok = lambda n, o, w: P2[:, n, O_VM + o:O_VM + o + w]
                    self.v = lambda n: P2[:, n, O_VM:O_VM + D_ML]
                    self.A, self.lf, self.b, self.M, self.wk, self.ex = l_rows
                self.steps = [(step, d, step if d == 0 else NB - 1 - step) for step in range(NB) for d in range(2)]

        streams = [Stream(0), Stream(1)]

        def span(n):
            return slice(n * P, (n + 1) * P)

        def scan_ap(x, d, n):
            r = x[:, d, n * P:(n + 1) * P]
            return r if d == 0 else r[:, ::-1]

        def last_of(x, d, n):
            t = (n + 1) * P - 1 if d == 0 else n * P
            return x[:, d, t:t + 1]

        def hdim(x):
            return x[:, :].unsqueeze(2)

        block = ctx.enter_context(nc.Block())

        @block.sync
        def _(sp):
            sp.dma_start(cols[:, 0:NCOL], a["cols"]).then_inc(sem("cols_landed"), 16)
            sp.dma_start(ident[:, :], a["ident"]).then_inc(sem("ident_landed"), 16)

            def load_chunk(c, s):
                sp.dma_start(raw[:, s, :], a["wstream"][c]).then_inc(raw_landed[s], 16)

            for s in range(SLOTS_W):
                load_chunk(s, s)
            loads = [S_OUT, S_OUT, S_FFN, S_CTX, S_IN2, S_IN2, S_OUT2, S_OUT2, NCH, NCH]
            with sp.Fori(1, min(loads[min(until, 9)] + SLOTS_W, NCH) // SLOTS_W) as i:
                for s in range(SLOTS_W):
                    sp.wait_ge(split_used, lin(s + 1 - SLOTS_W, i, SLOTS_W))
                    load_chunk(lin(s, i, SLOTS_W), s)

            if until < 9:
                for s in range(SLOTS_W):
                    sp.wait_ge(raw_landed[s], 16 * (min(loads[until] + SLOTS_W, NCH) // SLOTS_W))
                sp.wait_ge(sem("cols_landed"), 16)
                return
            sp.wait_ge(sem("out_ready"), NB)
            sp.dma_start(out.rearrange("o (b p) d -> p (o b) d", p=P), X[:, :, :]).then_inc(sem("out_stored"), 16)
            sp.wait_ge(sem("out_stored"), 16)

        @block.gpsimd
        def _(pool):
            pool.dma_start(X[:, :, :], a["x"].rearrange("o (b p) d -> p (o b) d", p=P)).then_inc(sem("x_landed"), 16)
            pool.dma_start(wa[:, :, :], a["wa"]).then_inc(sem("gates_landed"), 16)
            pool.dma_start(wx[:, :, :], a["wx"]).then_inc(sem("gates_landed"), 16)
            pool.dma_start(decay[:, :, :], a["decay"]).then_inc(sem("decay_landed"), 16)
            pool.dma_start(rope[:, :, :, :], a["rope"]).then_inc(sem("rope_landed"), 16)
            if until < 3:
                return
            pool.wait_ge(sem("y1_ready"), 2 * LB)
            for dst, name in ((pool_t, "pool_t"), (sgu_w, "sgu_w"), (pool_w, "pool_w"), (keys, "keys"), (mask, "mask"),
                              (wg, "wg")):
                pool.dma_start(dst[tuple(slice(None) for _ in dst.shape)], a[name]).then_inc(sem("tables_landed"), 16)
            pool.dma_start(fnw[:, :], a["fnw"].partition_broadcast(P)).then_inc(sem("fnw_landed"), 16)
            if until < 4:
                return
            pool.wait_ge(sem("x2_ready"), 1)
            pool.dma_start(ctx_x[:, :, :], a["ctx"].rearrange("o (b p) d -> p (o b) d", p=P)).then_inc(
                sem("ctx_landed"), 16)
            if until < 6:
                return
            pool.wait_ge(sem("ctx_done"), 1)
            pool.dma_start(sgu_n[:, :], a["sgu_n"].partition_broadcast(P)).then_inc(sem("sgu_n_landed"), 16)
            if until < 9:
                return
            for table, g0, b in (("u_tab", 0, 0), ("u_tab", SLOTS, 1), ("v_tab", 2 * SLOTS, 0), ("v_tab", 3 * SLOTS, 1)):
                if g0 < 2 * SLOTS:
                    pool.wait_ge(sem("idx_ready"), b + 1)
                with pool.Fori(0, SLOTS // GSTEP) as i:
                    for s in range(GSTEP):
                        if s % GATH == 0:
                            pool.tensor_copy(step_idx[:, s // GATH, :], idx[:, b, bass.ds(lin(s, i, GSTEP), GATH)]).then_inc(
                                sem("step_idx_ready"), 1)
                            pool.wait_ge(sem("step_idx_ready"), lin(g0 // GATH + s // GATH + 1, i, GSTEP // GATH))
                        pool.wait_ge(sem("row_used"), lin(g0 + s + 1, i, GSTEP))
                        pool.sem_inc(sem("gathers"), 1)
                        pool.indirect_dma_start(
                            out=rows_g[:, s % GATH, :], out_offset=None, in_=a[table],
                            in_offset=bass.IndirectOffsetOnAxis(ap=step_idx[:, s // GATH, s % GATH:s % GATH + 1], axis=0),
                        ).then_inc(sem(f"row_landed{s % GATH}"), 16)

        @block.tensor
        def _(pe):
            def products(n, banks, k0, nk, i, per, ah, al, blocks=NB, first=True, last=True):
                pe.wait_ge(lo_ready, lin(n + 1, i, per))
                wh, wl = WH[:, n % SLOTS_W, :], WL[:, n % SLOTS_W, :]
                for k in range(nk):
                    w = slice(k * CW, (k + 1) * CW)
                    for b in range(blocks):
                        t = slice(b * P, (b + 1) * P)
                        o = banks[b][:, :]
                        pe.matmul(o, ah[:, k0 + k, t], wh[:, w], start=first and k == 0, stop=False)
                        mm = pe.matmul(o, ah[:, k0 + k, t], wl[:, w], start=False,
                                       stop=al is None and last and k == nk - 1)
                        if al is not None:
                            mm = pe.matmul(o, al[:, k0 + k, t], wh[:, w], start=False, stop=last and k == nk - 1)
                mm.then_inc(split_used, 1)

            def tile(n, q, par, i=None, per=0, qper=0, work=iter(())):
                pe.wait_ge(acc_free_act, lin(q + 1, i, qper))
                pe.wait_ge(acc_free_dve, lin(q + 1, i, qper))
                for m in range(CPT):
                    products(n + m, ACC[par], m * CK, CK, i, per, UH, UL, first=m == 0, last=m == CPT - 1)
                    next(work, None)

            def linear_among(n0, q0, t0, tiles, work):
                for t in range(t0, tiles):
                    tile(n0 + CPT * t, q0 + t, (q0 + t) % 2, work=work)
                for _ in work:
                    pass

            def linear(n0, q0, tiles):
                with pe.Fori(0, tiles // 2) as i:
                    for par in range(2):
                        tile(n0 + CPT * par, q0 + par, (q0 + par) % 2, i, 2 * CPT, 2)
                if tiles % 2:
                    tile(n0 + CPT * (tiles - 1), q0 + tiles - 1, (q0 + tiles - 1) % 2)

            def turn(src, banks, name, wait=None, per_bank=4):
                for j, bk in enumerate(banks):
                    if wait:
                        wait(j)
                    for m in range(per_bank):
                        mm = pe.transpose(bk[:, m * P:(m + 1) * P], src(j, m), ident[:, :])
                    mm.then_inc(sem(name), 1)

            def norm_turned(rows, call, xn):
                pe.wait_ge(sem("xn_ready"), NB * (rows + 1))
                turn(lambda j, m: xn[:, m % 2, (2 * j + m // 2) * P:(2 * j + m // 2 + 1) * P], ALLB, "xn_turned")

            def u_ready(call):
                pe.wait_ge(sem("u_ready"), KT * (call + 1))

            pe.wait_ge(sem("ident_landed"), 16)
            norm_turned(0, 0, XN)
            u_ready(0)
            linear(S_IN, Q_IN, W_IN_HEAD)

            def lru():
                pe.wait_ge(acc_free_act, Q_IN + W_IN_HEAD + 2)
                pe.wait_ge(acc_free_dve, Q_IN + W_IN_HEAD + 2)
                turn(lambda j, m: Pin[:, m % 2, (2 * j + m // 2) * P:(2 * j + m // 2 + 1) * P], DB, "lru_x_turned")
                yield from pause(9)
                pe.wait_ge(acc_free_act, Q_IN + 4 + 2)
                pe.wait_ge(acc_free_dve, Q_IN + 4 + 2)
                pe.wait_ge(sem("lru_x_ready"), 4)
                turn(lambda j, m: Pin[:, m % 2, 1024 + (2 * j + m // 2) * P:1024 + (2 * j + m // 2 + 1) * P], DB,
                     "lru_g_turned")
                yield from pause(4)
                pe.wait_ge(sem("gates_landed"), 32)
                pe.wait_ge(sem("lru_u_ready"), 1)
                pe.wait_ge(sem("lru_g_ready"), 4)
                for w in (wa, wx):
                    for b in range(LB):
                        mm = pe.matmul(DB[b // 2][:, (b % 2) * T:(b % 2 + 1) * T], w[:, b, :], lru_u[:, b, :], start=True,
                                       stop=True)
                        mm.then_inc(sem("lru_gate_ps"), 1)
                    if w is wa:
                        yield from pause(5)
                        pe.wait_ge(sem("lru_gates_ready"), LB)

            linear_among(S_IN, Q_IN, W_IN_HEAD, W_IN_TILES, lru())
            if until < 2:
                return

            pe.wait_ge(acc_free_act, Q_OUT + 2)
            pe.wait_ge(acc_free_dve, Q_OUT + 2)
            pe.wait_ge(sem("lru_gates_ready"), 2 * LB)
            pe.wait_ge(sem("rope_ready"), NB)
            for t0, banks in ((C_Q, DB), (C_Q + 1024, bank[0:4])):
                turn(lambda j, m: Pin[:, m % 2, t0 + (2 * j + m // 2) * P:t0 + (2 * j + m // 2 + 1) * P], banks,
                     "qk_turned")
            pe.wait_ge(sem("qk_ready"), 8)
            qT, kT = half(0), half(1)
            for h in range(HEADS):
                for n in range(NB):
                    t = slice(n * P, (n + 1) * P)
                    mm = pe.matmul(DB[h // 2][:, ((h % 2) * 2 + n) * P:((h % 2) * 2 + n + 1) * P], kT(h)[:, t], qT(h)[:, t],
                                   start=True, stop=True)
                if h % 2:
                    mm.then_inc(sem("ret_scores"), 1)
            for h in range(HEADS):
                pe.wait_ge(sem("ret_s_ready"), h // 2 + 1)
                for n in range(NB):
                    mm = pe.matmul(bank[2 * n + h // 4][:, (h % 4) * P:(h % 4 + 1) * P], ret_s[:, h, n, :],
                                   Pin[:, n, C_V + h * P:C_V + (h + 1) * P], start=True, stop=True)
            mm.then_inc(sem("ret_inner"), 1)
            pe.wait_ge(sem("ret_kz_ready"), 1)
            for h in range(HEADS):
                mm = pe.matmul(DB[h // 4][:, (h % 4) * P:(h % 4 + 1) * P], ret_kz[:, h, :],
                               Pin[:, 0, C_V + h * P:C_V + (h + 1) * P], start=True, stop=True)
            mm.then_inc(sem("ret_kv"), 1)
            pe.wait_ge(sem("ret_r_ready"), 2)
            for h in range(HEADS):
                mm = pe.matmul(DB[2 + h // 4][:, (h % 4) * P:(h % 4 + 1) * P], qT(h)[:, P:T], ret_r[:, h, :],
                               start=True, stop=True)
            mm.then_inc(sem("ret_cross"), 1)
            pe.wait_ge(sem("ret_o_ready"), 1)
            turn(lambda j, m: ret_o[:, m % 2, 2 * j + m // 2, :], bank[0:4], "ret_turned")
            pe.wait_ge(sem("y1_ready"), 2 * LB)
            linear(S_OUT, Q_OUT, OUT_TILES)
            if until < 3:
                return

            norm_turned(1, 1, XN)
            u_ready(1)

            def step(kinds, n, i=None, tile=0, down=0):
                m = dict.fromkeys(kinds, 0)
                for p, kind in enumerate(kinds):
                    at, k = n + p, m[kind]
                    m[kind] += 1
                    if k == 0 and kind in "gu":
                        q = Q_FFN + 2 * tile + "gu".index(kind)
                        pe.wait_ge(acc_free_act, lin(q + 1, i, 2))
                        pe.wait_ge(acc_free_dve, lin(q + 1, i, 2))
                    if kind == "g":
                        if k == 0 and tile:
                            pe.wait_ge(sem("mod_ready"), lin(ADA_STEP * tile, i, ADA_STEP))
                        products(at, ACC[0], k * CK, CK, i, len(FF_STEP), UH, UL, first=k == 0, last=k == CPT - 1)
                    elif kind == "u":
                        if k == 0 and tile:
                            pe.wait_ge(sem("ffT_ready"), lin(CK * tile, i, CK))
                        products(at, ACC[1], k * CK, CK, i, len(FF_STEP), UH, UL, first=k == 0, last=k == CPT - 1)
                    elif kind == "a":
                        if k == 0:
                            pe.wait_ge(acc_free_act, lin(Q_FFN + 4 + 2 * min(tile, FT - 1), i, 2))
                            if tile == FT:
                                pe.wait_ge(sem("mod_ready"), ADA_STEP * FT)
                        r = k % CPT
                        products(at, [ACC[0][k // CPT]], r * CK, CK, i, len(FF_STEP), cond, None, blocks=1, first=r == 0,
                                 last=r == CPT - 1)
                    else:
                        if k == 0:
                            pe.wait_ge(sem("ffT_ready"), lin(CK * (down + 1), i, CK))
                        pe.wait_ge(sem("down_added"), lin(2 + OUT_TILES * down + k - 1, i, OUT_TILES))
                        products(at, DB[2 * (k % 2):2 * (k % 2) + 2], 0, CK, i, len(FF_STEP), FH, FL)

            def turn_ff(i=None, nth=0):
                pe.wait_ge(sem("ff_ready"), lin(nth + 1, i, 1))
                for j in range(2):
                    for m in range(4):
                        k = 2 * j + m // 2
                        mm = pe.transpose(bank[2 + j][:, m * P:(m + 1) * P], ff[:, m % 2, k * P:(k + 1) * P], ident[:, :])
                mm.then_inc(sem("ff_turned"), 1)

            def ada_turned(i=None, nth=0):
                for t in range(ADA_STEP):
                    pe.wait_ge(sem("ada_rows_ready"), lin(ADA_STEP * nth + t + 1, i, ADA_STEP))
                    for j in range(CW // P):
                        mm = pe.matmul(ACC[0][t][:, 2 * j:2 * j + 2], ada_rows[0:4, t, j * P:(j + 1) * P],
                                       col("sel", 0, 2, rows=4), start=True, stop=True)
                    mm.then_inc(sem("ada_cols"), 1)

            pe.wait_ge(sem("cond_ready"), 1)
            step(FF_FIRST, S_FFN)
            turn_ff()
            ada_turned()
            with pe.Fori(0, FT - 1) as i:
                step(FF_STEP, S_STEP, i, tile=1)
                ada_turned(i, 1)
                turn_ff(i, 1)
            step(FF_LAST, S_LAST, tile=FT, down=FT - 1)
            ada_turned(nth=FT)
            if until < 4:
                return

            def gates(s):
                pe.wait_ge(sem("wg_ready"), s + 1)
                for k in range(KT):
                    for j, (part, w) in enumerate(((UH, wg_h), (UH, wg_l), (UL, wg_h))):
                        mm = pe.matmul(DB[2][0:NG, 0:T], w[s][:, k, :], part[:, k, :], start=j == 0 and k == 0,
                                       stop=j == 2 and k == KT - 1)
                mm.then_inc(sem("gate_ps"), 1)

            def gate_rows(s):
                pe.wait_ge(sem("g_row_ready"), s + 1)
                for typ in range(2):
                    for d in range(2):
                        g0 = (2 * d + typ) * MH
                        mm = pe.matmul(DB[2 + typ][0:MH, d * T:(d + 1) * T], ident[0:NG, g0:g0 + MH], g_row[s][0:NG, :],
                                       start=True, stop=True)
                mm.then_inc(sem("gate_rows_ps"), 1)

            def keys_turned(S, banks):
                turn(lambda j, m: S.k_raw(m % 2, 2 * j + m // 2), banks, "k_turned")

            def keys_back(S, banks):
                pe.wait_ge(sem("k_silu"), S.s + 1)
                for j in range(4):
                    for m in range(4):
                        mm = pe.transpose(banks[j][:, m * P:(m + 1) * P], S.kT(4 * (j % 2) + m)[:, span(j // 2)], ident[:, :])
                    mm.then_inc(sem("k_back"), 1)

            def columns(S):
                pe.wait_ge(sem("rows_ready"), S.s + 1)
                kinds = [S.A, S.wk, S.lf, S.ex] if S.lat else [None, S.wk]
                for kind, row in enumerate(kinds):
                    for d in range(2):
                        for n in range(NB):
                            o = ((kind * 2 + d) * NB + n) * MH
                            if row is not None:
                                pe.matmul(DB[2][:, o:o + MH], row[:, d, span(n)], ident[0:MH, 0:MH], start=True, stop=True)
                for d in range(2):
                    for n in range(NB):
                        o = ((4 * 2 + d) * NB + n) * MH
                        mm = pe.matmul(DB[2][:, o:o + MH], dcy[0:MH, d, n:n + 1].to_broadcast([MH, P]), ident[0:MH, 0:MH],
                                       start=True, stop=True)
                mm.then_inc(sem("cols_ps"), 1)

            upd = [0]

            def update(S, n):
                for h in range(MH):
                    pe.wait_ge(sem("vw_ready"), upd[0] * MH + h + 1)
                    for kt in range(MKT):
                        mm = pe.matmul(ALLB[2 * h + kt][:, 0:VA], S.k_tok(n, h * MD + kt * P, P), vw[:, h % 2, :], start=True,
                                       stop=True)
                    mm.then_inc(sem("state_ps"), 1)
                upd[0] += 1
                pe.wait_ge(sem("state_ready"), upd[0])

            pe.wait_ge(sem("down_added"), 2 + FT * OUT_TILES)
            norm_turned(3, 2, ctx_n)
            u_ready(2)
            linear(S_CTX, Q_CTX, CTX_TILES)
            if until < 5:
                return
            gates(0)
            gate_rows(0)
            pe.wait_ge(acc_free_act, Q_IN2 + 2)
            pe.wait_ge(acc_free_dve, Q_IN2 + 2)
            keys_turned(streams[0], bank[0:4])
            keys_back(streams[0], bank[0:4])
            columns(streams[0])
            pe.wait_ge(sem("k_tok_ready"), 4)
            pe.wait_ge(sem("co_ready"), 1)
            for step, d, n in streams[0].steps:
                update(streams[0], n)
            if until < 6:
                return

            norm_turned(4, 3, XN2)
            u_ready(3)
            linear(S_IN2, Q_IN2, W2_HEAD)
            L = streams[1]

            def rows_kept(tiles):
                pe.wait_ge(acc_free_act, Q_IN2 + tiles + 2)
                pe.wait_ge(acc_free_dve, Q_IN2 + tiles + 2)

            def mixers():
                gates(1)
                yield
                rows_kept(W2_HEAD)
                for g in range(len(PW)):
                    for b in range(NB):
                        mm = pe.matmul(DB[g // 2][:, (g % 2) * T:(g % 2 + 1) * T], P2[:, b, O_P + g * P:O_P + (g + 1) * P],
                                       pool_t[:, g, b, :], start=b == 0, stop=b == NB - 1)
                    mm.then_inc(sem("pool_ps"), 1)
                yield from pause(2)
                pe.wait_ge(sem("g_row_ready"), 2)
                for g in range(len(PW)):
                    pe.wait_ge(sem("pool_d_ready"), g + 1)
                    mm = pe.matmul(DB[2 + g // 2][:, (g % 2) * T:(g % 2 + 1) * T], pool_w[:, g, :], pool_d[:, g, :],
                                   start=True, stop=True)
                    mm.then_inc(sem("pool_y_ps"), 1)
                yield
                pe.wait_ge(sem("sgu_v_ready"), 1)
                for n in range(NB):
                    for h in range(SH):
                        mm = pe.matmul(DB[n][:, h * P:(h + 1) * P], sgu_w[:, h, :], P2[:, n, O_V + h * P:O_V + (h + 1) * P],
                                       start=True, stop=True)
                mm.then_inc(sem("sgu_ps"), 1)
                yield from pause(3)
                pe.wait_ge(sem("sgu_y_ready"), 1)
                turn(lambda j, m: P2[:, m % 2, O_U + (2 * j + m // 2) * P:O_U + (2 * j + m // 2 + 1) * P], DB[0:2],
                     "sgu_turned")
                yield
                pe.wait_ge(sem("pool_y_kept"), len(PW))
                gate_rows(1)
                yield from pause(2)
                rows_kept(5)
                pe.wait_ge(sem("sgu_t_kept"), 4)
                pe.wait_ge(sem("gate_rows_kept"), 2)
                turn(lambda j, m: P2[:, m % 2, O_Q + (2 * j + m // 2) * P:O_Q + (2 * j + m // 2 + 1) * P], DB, "q_turned")
                yield from pause(7)
                rows_kept(7)
                pe.wait_ge(sem("q_pad_ready"), 4)
                keys_turned(L, DB)
                yield from pause(9)
                keys_back(L, DB)
                yield from pause(2)
                pe.wait_ge(sem("q_silu"), 1)
                pe.wait_ge(sem("k_tok_ready"), 8)
                for h in range(MH):
                    for n in range(NB):
                        for kt in range(MKT):
                            mm = pe.matmul(DB[h // 2][:, ((h % 2) * NB + n) * P:((h % 2) * NB + n + 1) * P],
                                           L.kT(MKT * h + kt)[:, span(n)], lat_half(O_Q)(MKT * h + kt)[:, span(n)],
                                           start=kt == 0, stop=kt == MKT - 1)
                mm.then_inc(sem("ml_scores"), 1)
                yield
                columns(L)

            linear_among(S_IN2, Q_IN2, W2_HEAD, W2_TILES, mixers())
            rows_kept(W2_TILES)
            pe.wait_ge(sem("co_ready"), 2)
            pe.wait_ge(sem("sc_t_ready"), 1)
            x = 0
            for step, d, n in L.steps:
                def weights(h):
                    pe.matmul(DB[h % 2][:, 0:P], ident[0:MH, h:h + 1].to_broadcast([MH, P]), L.b[:, d, span(n)], start=True,
                              stop=False)
                    pe.matmul(DB[h % 2][:, 0:P], ident[:, :], mask[:, d, :], start=False, stop=True).then_inc(
                        sem("arg_ps"), 1)
                weights(0)
                for h in range(MH):
                    if h + 1 < MH:
                        if h >= 1:
                            pe.wait_ge(sem("w_exp"), x + h)
                        weights(h + 1)
                    if x + h >= 2:
                        pe.wait_ge(sem("h_ready"), x + h - 1)
                    for kt in range(MKT):
                        pe.matmul(ACC[h % 2][1][:, 0:VA], lat_half(O_Q)(MKT * h + kt)[:, span(n)], st[:, d, h, kt, :],
                                  start=kt == 0, stop=kt == MKT - 1)
                    pe.wait_ge(sem("w_ready"), x + h + 1)
                    pe.matmul(ACC[h % 2][0][:, 0:VA], wb[:, h % 2, :], L.v1[:, n, h, :], start=True, stop=True).then_inc(
                        sem("num_ps"), 1)
                x += MH
                pe.wait_ge(sem("w_exp"), x)
                if step == 0:
                    pe.wait_ge(sem("h_ready"), x)
                    update(L, n)
            pe.wait_ge(sem("ml_y_ready"), 1)
            turn(lambda j, m: P2[:, m % 2, O_K + (2 * j + m // 2) * P:O_K + (2 * j + m // 2 + 1) * P], DB, "ml_turned")
            if until < 8:
                return
            def spread(column):
                for j in range(4):
                    for m in range(4):
                        mm = pe.matmul(DB[j][:, m * P:(m + 1) * P], column(4 * j + m).to_broadcast([P, P]), ident[:, :],
                                       start=True, stop=True)
                    mm.then_inc(sem("spread_ps"), 1)

            pe.wait_ge(sem("y2_ready"), KT)
            spread(lambda k: modt[:, 2 * KT + k, 0:1])
            pe.wait_ge(sem("spread_ready"), 4)
            spread(lambda k: modt[:, 5 * KT + k, 0:1])
            linear(S_OUT2, Q_OUT2, OUT_TILES)

            pe.wait_ge(sem("spread_ready"), 8)
            norm_turned(5, 4, XN2)
            u_ready(4)
            spread(lambda k: sc_ffn[:, k:k + 1])
            pe.wait_ge(sem("spread_ready"), 12)
            spread(lambda k: modt[:, 3 * KT + k, 0:1])
            linear(S_WQ, Q_WQ, OUT_TILES)
            pe.wait_ge(sem("spread_ready"), 16)
            pe.wait_ge(acc_free_act, Q_WQ + OUT_TILES + 2)
            pe.wait_ge(acc_free_dve, Q_WQ + OUT_TILES + 2)
            pe.wait_ge(sem("hf_ready"), NB)
            turn(lambda j, m: q_tok[:, m % 2, (2 * j + m // 2) * P:(2 * j + m // 2 + 1) * P], ALLB, "pq_turned")
            pe.wait_ge(sem("q_t_ready"), 8)
            for b in range(NB):
                for hp in range(2 * PH):
                    mm = pe.matmul(ALLB[4 * b + hp // 4][:, (hp % 4) * NKEY:(hp % 4 + 1) * NKEY], q_t[:, hp, span(b)],
                                   keys[:, hp % 2, :], start=True, stop=True)
                    if hp % 4 == 3:
                        mm.then_inc(sem("key_ps"), 1)

        @block.scalar
        def _(act):
            chain = Chain(act, "act_chain")

            def hi(n, i=None, per=0):
                if i is None and n >= NCH:
                    return
                act.wait_ge(raw_landed[n % SLOTS_W], lin(16 * (n // SLOTS_W + 1), i, 16 * per // SLOTS_W))
                act.activation(WH[:, n % SLOTS_W, :], raw[:, n % SLOTS_W, :], ACT.Copy).then_inc(hi_ready, 1)

            def tile(n, evacuate, i=None, per=0, work=iter(())):
                for m in range(CPT):
                    hi(n + LEAD + m, i, per)
                    next(work, None)
                act.wait_ge(split_used, lin(n + CPT, i, per))
                evacuate()

            def linear(n0, q0, tiles, evacuate):
                pairs = tiles // 2
                last = n0 + tiles * CPT == NCH
                with act.Fori(0, pairs - last) as i:
                    for par in range(2):
                        tile(n0 + CPT * par, lambda: evacuate((q0 + par) % 2, lin(par, i, 2)), i, 2 * CPT)
                for t in range(2 * (pairs - last), tiles):
                    tile(n0 + CPT * t, lambda: evacuate((q0 + t) % 2, t))

            def linear_among(n0, q0, t0, tiles, evacuate, work):
                for t in range(t0, tiles):
                    tile(n0 + CPT * t, lambda: evacuate((q0 + t) % 2, t), work=work)
                for _ in work:
                    pass

            def to(dst, width):
                def evacuate(par, t):
                    act.activation(dst(t), ACC[par][0][:, 0:width], ACT.Copy).then_inc(acc_free_act, 1)
                return evacuate

            def nothing(par, t):
                act.sem_inc(acc_free_act, 1)

            def root(call):
                act.wait_ge(sem("ms_ready"), call + 1)
                act.activation(rms[:, :], ms[:, :], ACT.Sqrt).then_inc(sem("rms_ready"), 1)

            def norm_turned(rows, call, scale, bias=None):
                root(rows)
                for j in range(8):
                    act.wait_ge(sem("xn_turned"), 8 * call + j + 1)
                    for m in range(2):
                        k = 2 * j + m
                        src = ALLB[j][:, m * T:(m + 1) * T]
                        if bias is None:
                            ins = act.activation(UH[:, k, :], src, ACT.Copy, scale=scale(k))
                        else:
                            ins = act.activation(UH[:, k, :], src, ACT.Identity, scale=scale(k), bias=bias(k))
                        ins.then_inc(sem("uh_ready"), 1)

            act.wait_ge(sem("cols_landed"), 16)
            for r, name in enumerate(("c", "cctx")):
                chain.mark(act.activation(csil[:, :, r], col(name, 0, KT), ACT.Silu))
            chain.sync()
            act.wait_ge(sem("lam_abs"), 1)
            act.activation(lam_t[1][:, :], lam_t[0][:, :], ACT.Exp, scale=-1.0).then_inc(sem("lam_exp"), 1)
            for m in range(LEAD):
                hi(m)
            act.sem_inc(acc_free_act, 2)

            norm_turned(0, 0, lambda k: col("ln1", k))
            to_pin = to(lambda t: Pin[:, 0, bass.ds(t * CW, CW)], CW)
            linear(S_IN, Q_IN, W_IN_HEAD, to_pin)

            def lru():
                yield
                for j in range(4):
                    act.wait_ge(sem("lru_x_turned"), j + 1)
                    act.activation(lru_x[:, 2 * j:2 * j + 2, CONV_W - 1:],
                                   DB[j][:, :].rearrange("p (b t) -> p b t", t=T), ACT.Copy).then_inc(sem("lru_x_ready"), 1)
                yield from pause(9)
                for j in range(4):
                    act.wait_ge(sem("lru_g_turned"), j + 1)
                    act.activation(lru_g[:, 2 * j:2 * j + 2, :], DB[j][:, :].rearrange("p (b t) -> p b t", t=T),
                                   ACT.Gelu_apprx_tanh).then_inc(sem("lru_g_ready"), 1)
                yield from pause(4)
                rg, ig = half(0), half(1)
                for name, dst, w in (("ba", rg, 0), ("bx", ig, LB)):
                    for b in range(LB):
                        act.wait_ge(sem("lru_gate_ps"), w + b // 2 * 2 + 2)
                        act.activation(dst(b), DB[b // 2][:, (b % 2) * T:(b % 2 + 1) * T], ACT.Sigmoid,
                                       bias=col(name, b)).then_inc(sem("lru_gates_ready"), 1)
                        if b == LB // 2 - 1:
                            yield
                    yield from pause(4 if name == "ba" else 1)
                act.wait_ge(sem("lru_gates_ready"), 2 * LB)
                act.wait_ge(sem("lam_ready"), 1)
                for b in range(LB):
                    act.activation(lru_b[:, b, :], rg(b), ACT.Tanh, scale=p_col[:, b:b + 1]).then_inc(sem("lru_tanh"), 1)
                    if b == LB // 2 - 1:
                        yield
                yield
                for b in range(LB):
                    act.activation(rg(b), rg(b), ACT.Exp, scale=n_col[:, b:b + 1]).then_inc(sem("lru_a_ready"), 1)
                    if b == LB // 2 - 1:
                        yield
                yield from pause(3)
                act.wait_ge(sem("lru_sq_ready"), 1)
                act.activation(lru_b[:, :, :], lru_b[:, :, :], ACT.Sqrt).then_inc(sem("lru_root"), 1)

            linear_among(S_IN, Q_IN, W_IN_HEAD, W_IN_TILES, to_pin, lru())
            if until < 2:
                return
            act.wait_ge(sem("lru_y_ready"), 1)
            act.activation(UH[:, 0:LB, :], lru_g[:, :, :], ACT.Copy).then_inc(sem("lru_yh_ready"), 1)

            for j in range(8):
                act.wait_ge(sem("qk_turned"), j + 1)
                qk = half(j // 4)
                for m in range(2):
                    ins = act.activation(qk(2 * (j % 4) + m), (DB if j < 4 else bank[0:4])[j % 4][:, m * T:(m + 1) * T],
                                         ACT.Copy)
                ins.then_inc(sem("qk_ready"), 1)
            act.wait_ge(sem("ret_kv"), 1)
            for j in range(2):
                act.activation(ret_r[:, 4 * j:4 * j + 4, :], DB[j][:, :].rearrange("p (h e) -> p h e", e=P),
                               ACT.Copy).then_inc(sem("ret_r_ready"), 1)
            act.activation(Pin[:, :, C_G:C_G + 1024], Pin[:, :, C_G:C_G + 1024], ACT.Silu).then_inc(sem("ret_gate"), 1)
            act.wait_ge(sem("gn_var"), 1)
            act.activation(gn[1][:, :], gn[0][:, :], ACT.Sqrt).then_inc(sem("gn_root"), 1)
            for j in range(4):
                act.wait_ge(sem("ret_turned"), j + 1)
                for m in range(2):
                    h = 2 * j + m
                    act.activation(UH[:, LB + h, :], bank[j][:, m * T:(m + 1) * T], ACT.Copy,
                                   scale=col("gnw", h)).then_inc(sem("ret_yh_ready"), 1)
            linear(S_OUT, Q_OUT, OUT_TILES, nothing)
            if until < 3:
                return

            act.activation(cond[:, :, 0:2], csil[:, :, :], ACT.Copy).then_inc(sem("cond_hi"), 1)
            norm_turned(1, 1, lambda k: col("ln2", k))

            def step(kinds, n, i=None, tile=0):
                m = dict.fromkeys(kinds, 0)
                for p, kind in enumerate(kinds):
                    hi(n + LEAD + p, i, len(FF_STEP))
                    m[kind] += 1
                    if kind == "g" and m[kind] == CPT:
                        act.wait_ge(split_used, lin(n + p + 1, i, len(FF_STEP)))
                        if tile:
                            act.wait_ge(sem("ff_ready"), lin(tile, i, 1))
                        for b in range(NB):
                            ins = act.activation(ff_g[:, b, :], ACC[0][b][:, :], ACT.Silu)
                        ins.then_inc(acc_free_act, 2)
                    if kind == "a" and m[kind] % CPT == 0:
                        t = m[kind] // CPT - 1
                        act.wait_ge(split_used, lin(n + p + 1, i, len(FF_STEP)))
                        if tile:
                            act.wait_ge(sem("ada_cols"), lin(ADA_STEP * (tile - 1) + t + 1, i, ADA_STEP))
                        act.activation(ada_rows[0:4, t, :], ACC[0][t][0:4, :], ACT.Copy).then_inc(sem("ada_rows_ready"), 1)

            def turned(i=None, nth=0):
                act.wait_ge(sem("ff_turned"), lin(nth + 1, i, 1))
                for k in range(CK):
                    act.activation(FH[:, k, :], bank[2 + k // 2][:, (k % 2) * T:(k % 2 + 1) * T], ACT.Copy).then_inc(
                        sem("ffh_ready"), 1)

            step(FF_FIRST, S_FFN)
            turned()
            with act.Fori(0, FT - 1) as i:
                step(FF_STEP, S_STEP, i, tile=1)
                turned(i, 1)
            step(FF_LAST, S_LAST, tile=FT)
            if until < 4:
                return

            root(2)

            def pads(name, base, banks, pad, done):
                for j in range(4):
                    act.wait_ge(sem(name), base + j + 1)
                    act.activation(pad[:, 2 * j:2 * j + 2, 1:T + 1], banks[j][:, :].rearrange("p (b t) -> p b t", t=T),
                                   ACT.Copy).then_inc(sem(done), 1)

            def keys_turned(S, banks):
                pads("k_turned", 4 * S.s, banks, S.pad, "k_pad_ready")

            def keys_silu(S):
                act.wait_ge(sem("k_conv"), S.s + 1)
                for half_of in range(2):
                    for b in range(4 * half_of, 4 * half_of + 4):
                        chain.mark(act.activation(S.kT(b), S.kT(b), ACT.Silu))
                    yield
                chain.sync()
                for half_of in range(2):
                    for b in range(4 * half_of, 4 * half_of + 4):
                        ins = act.activation(S.kT(b), S.kT(b), ACT.Copy, scale=float(MD) ** -0.5)
                    if half_of == 0:
                        yield
                ins.then_inc(sem("k_silu"), 1)

            def keys_back(S, banks):
                if S.lat:
                    act.wait_ge(sem("v1_ready"), 1)
                for j in range(4):
                    act.wait_ge(sem("k_back"), 4 * S.s + j + 1)
                    act.activation(S.k_tok(j // 2, (j % 2) * CW, CW), banks[j][:, :], ACT.Copy).then_inc(sem("k_tok_ready"), 1)

            def gate_weights(s):
                act.wait_ge(sem("tables_landed"), 16 * 6)
                act.activation(wg_h[s][:, :, :], wg[:, :, :], ACT.Copy).then_inc(sem("wg_hi"), 1)

            def gate_log(S):
                act.wait_ge(sem("fg_abs"), S.s + 1)
                chain(act.activation(S.b, S.b, ACT.Exp, scale=-1.0))
                act.activation(S.b, S.b, ACT.Ln, bias=1.0).then_inc(sem("fg_log"), 1)

            def gate_rows(S):
                act.wait_ge(sem("row_max"), S.s + 1)
                for d in range(2):
                    for n in range(NB):
                        chain.mark(act.activation(S.wk[:, d, span(n)], S.A[:, d, span(n)], ACT.Exp,
                                                  bias=n_ml[0:MH, d, n:n + 1]))
                chain.mark(act.activation(dcy[0:MH, :, :], dcy[0:MH, :, :], ACT.Exp))
                if S.lat:
                    for step, d, n in S.steps:
                        chain.mark(act.activation(S.lf[:, d, span(n)], S.M[:, d, span(n)], ACT.Exp, scale=-1.0,
                                                  bias=m_st[0:MH, d, NB + step:NB + step + 1]))
                    chain.mark(act.activation(S.ex, S.ex, ACT.Exp, scale=-1.0))
                chain.sync()
                act.sem_inc(sem("rows_exp"), 1)

            norm_turned(3, 2, lambda k: sc_mix[:, 1, k:k + 1], lambda k: modt[:, k, 1:2])
            gate_weights(0)
            linear(S_CTX, Q_CTX, CTX_TILES, to(lambda t: kv[:, 0, bass.ds(t * CW, CW)], CW))
            if until < 5:
                return
            keys_turned(streams[0], bank[0:4])
            for _ in keys_silu(streams[0]):
                pass
            keys_back(streams[0], bank[0:4])
            gate_log(streams[0])
            gate_rows(streams[0])
            if until < 6:
                return

            norm_turned(4, 3, lambda k: sc_mix[:, 0, k:k + 1], lambda k: modt[:, k, 0:1])
            gate_weights(1)
            def to_p2(par, t):
                act.activation(P2[:, 0, W2_ORDER[t] * CW:(W2_ORDER[t] + 1) * CW], ACC[par][0][:, :], ACT.Copy).then_inc(
                    acc_free_act, 1)

            linear(S_IN2, Q_IN2, W2_HEAD, to(lambda t: P2[:, 0, bass.ds(t * CW, CW)], CW))
            L = streams[1]

            def mixers():
                act.wait_ge(acc_free_dve, Q_IN2 + W2_HEAD + 2)
                act.activation(P2[:, :, O_U:O_P], P2[:, :, O_U:O_P], ACT.Gelu_apprx_tanh).then_inc(sem("sgu_gelu"), 1)
                yield from pause(2)
                for g in range(len(PW)):
                    act.wait_ge(sem("pool_ps"), g // 2 * 2 + 2)
                    act.activation(pool_d[:, g, :], DB[g // 2][:, (g % 2) * T:(g % 2 + 1) * T], ACT.Copy).then_inc(
                        sem("pool_d_ready"), 1)
                act.wait_ge(sem("sgu_ms"), 1)
                act.activation(rms[:, :], ms[:, :], ACT.Sqrt).then_inc(sem("sgu_root"), 1)
                yield from pause(2)
                for g in range(len(PW)):
                    act.wait_ge(sem("pool_y_ps"), g // 2 * 2 + 2)
                    act.activation(pool_y[:, g, :], DB[2 + g // 2][:, (g % 2) * T:(g % 2 + 1) * T], ACT.Copy,
                                   scale=col("pscale", g)).then_inc(sem("pool_y_kept"), 1)
                yield from pause(4)
                for k in range(4):
                    act.wait_ge(sem("sgu_turned"), k // 2 + 1)
                    act.activation(sgu_t[:, k, :], DB[k // 2][:, (k % 2) * T:(k % 2 + 1) * T], ACT.Copy).then_inc(
                        sem("sgu_t_kept"), 1)
                yield from pause(2)
                gate_log(L)
                yield
                pads("q_turned", 0, DB, L.pad, "q_pad_ready")
                yield from pause(3)
                gate_rows(L)
                yield from pause(4)
                act.wait_ge(sem("q_conv"), 1)
                keys_turned(L, DB)
                yield
                qT = lat_half(O_Q)
                for b in range(MB):
                    ins = act.activation(qT(b), qT(b), ACT.Silu)
                    if b == 3:
                        yield
                ins.then_inc(sem("q_silu"), 1)
                yield from pause(3)
                yield from keys_silu(L)
                yield
                keys_back(L, DB)

            linear_among(S_IN2, Q_IN2, W2_HEAD, W2_TILES, to_p2, mixers())
            if until < 6:
                return
            act.wait_ge(sem("co_ready"), 2)
            x = 0
            for step, d, n in L.steps:
                def weights(h):
                    act.wait_ge(sem("arg_ps"), x + h + 1)
                    if x + h >= 2:
                        act.wait_ge(sem("num_ps"), x + h - 1)
                    act.activation(wb[:, h % 2, :], DB[h % 2][:, 0:P], ACT.Exp, bias=co[:, 0, d, n, h:h + 1]).then_inc(
                        sem("w_exp"), 1)
                weights(0)
                for h in range(MH):
                    if h + 1 < MH:
                        weights(h + 1)
                    act.wait_ge(sem("num_ps"), x + h + 1)
                    if x + h >= 2:
                        act.wait_ge(sem("h_ready"), x + h - 1)
                    act.activation(ml_t[:, h % 2, :], ACC[h % 2][1][:, 0:VA], ACT.Copy,
                                   scale=co[:, 2, d, n, h:h + 1]).then_inc(sem("inter_ready"), 1)
                x += MH
            act.activation(P2[:, :, O_O:O_O + D_ML], P2[:, :, O_O:O_O + D_ML], ACT.Sigmoid).then_inc(sem("ml_gate"), 1)
            for g in range(len(PW)):
                act.activation(UH[:, 12 + g, :], pool_y[:, g, :], ACT.Copy).then_inc(sem("yh2_ready"), 1)
            for k in range(4):
                act.activation(UH[:, k, :], sgu_t[:, k, :], ACT.Copy).then_inc(sem("yh2_ready"), 1)
            act.wait_ge(sem("ml_ms"), 1)
            act.activation(l_ms[1][:, :], l_ms[0][:, :], ACT.Sqrt).then_inc(sem("ml_root"), 1)
            for j in range(4):
                act.wait_ge(sem("ml_turned"), j + 1)
                for m in range(2):
                    b = 2 * j + m
                    act.activation(UH[:, 4 + b, :], DB[j][:, m * T:(m + 1) * T], ACT.Copy, scale=col("mlnorm", b)).then_inc(
                        sem("yh2_ready"), 1)
            if until < 8:
                return

            def spread(q, dst):
                for j in range(4):
                    act.wait_ge(sem("spread_ps"), 4 * q + j + 1)
                    act.activation(dst[:, j * CW:(j + 1) * CW], DB[j][:, :], ACT.Copy).then_inc(sem("spread_ready"), 1)

            spread(0, gb1)
            spread(1, gb2)
            linear(S_OUT2, Q_OUT2, OUT_TILES, nothing)
            norm_turned(5, 4, lambda k: sc_ffn[:, k:k + 1], lambda k: modt[:, 3 * KT + k, 0:1])
            act.wait_ge(sem("u_ready"), KT * 5)
            spread(2, sc_row)
            spread(3, sh_row)
            linear(S_WQ, Q_WQ, OUT_TILES, to(lambda t: q_tok[:, 0, bass.ds(t * CW, CW)], CW))
            act.wait_ge(sem("hf_ready"), NB)
            for j in range(8):
                act.wait_ge(sem("pq_turned"), j + 1)
                act.activation(q_t[:, 2 * j:2 * j + 2, :], ALLB[j][:, :].rearrange("p (b t) -> p b t", t=T),
                               ACT.Copy).then_inc(sem("q_t_ready"), 1)
            for j in range(8):
                act.wait_ge(sem("key_ps"), j + 1)
                act.activation(key_s[:, j // 4, 4 * (j % 4):4 * (j % 4) + 4, :],
                               ALLB[j][:, :].rearrange("p (b t) -> p b t", t=NKEY), ACT.Copy).then_inc(sem("key_s_ready"), 1)
            if until < 9:
                return
            for b in range(NB):
                act.wait_ge(sem("best_ready"), b + 1)
                act.activation(gate_w[:, b, :], gate_w[:, b, :], ACT.Exp).then_inc(sem("soft_exp"), 1)
            act.wait_ge(sem("dots_done"), 1)
            act.activation(dots[:, :, :], dots[:, :, :], ACT.Gelu_apprx_tanh).then_inc(sem("dots_gelu"), 1)
            act.dma_start(nfin[:, :], a["nfin"].partition_broadcast(P)).then_inc(sem("nfin_landed"), 16)
            for b in range(NB):
                act.wait_ge(sem("fin_ms"), b + 1)
                act.activation(rms[:, b:b + 1], ms[:, b:b + 1], ACT.Sqrt).then_inc(sem("fin_root"), 1)

        @block.vector
        def _(dve):
            link = Chain(dve, "dve_chain")

            def lo(n, i=None, per=0):
                if i is None and n >= NCH:
                    return
                dve.wait_ge(hi_ready, lin(n + 1, i, per))
                dve.tensor_tensor(WL[:, n % SLOTS_W, :], raw[:, n % SLOTS_W, :], WH[:, n % SLOTS_W, :].bitcast(F32),
                                  ALU.subtract).then_inc(lo_ready, 1)

            def tile(n, evacuate, i=None, per=0, work=iter(())):
                for m in range(CPT):
                    lo(n + LEAD + m, i, per)
                    next(work, None)
                dve.wait_ge(split_used, lin(n + CPT, i, per))
                evacuate()

            def linear(n0, q0, tiles, evacuate):
                pairs = tiles // 2
                last = n0 + tiles * CPT == NCH
                with dve.Fori(0, pairs - last) as i:
                    for par in range(2):
                        tile(n0 + CPT * par, lambda: evacuate((q0 + par) % 2, lin(par, i, 2)), i, 2 * CPT)
                for t in range(2 * (pairs - last), tiles):
                    tile(n0 + CPT * t, lambda: evacuate((q0 + t) % 2, t))

            def linear_among(n0, q0, t0, tiles, evacuate, work):
                for t in range(t0, tiles):
                    tile(n0 + CPT * t, lambda: evacuate((q0 + t) % 2, t), work=work)
                for _ in work:
                    pass

            def to(dst, width):
                def evacuate(par, t):
                    dve.tensor_copy(dst(t), ACC[par][1][:, 0:width]).then_inc(acc_free_dve, 1)
                return evacuate

            def add_to_x(par, t):
                for b in range(NB):
                    x = X[:, b, bass.ds(t * CW, CW)]
                    ins = dve.tensor_tensor(x, ACC[par][b][:, :], x, ALU.add)
                ins.then_inc(acc_free_dve, 1)

            def norm_rows(call, x, xn):
                for b in range(NB):
                    link(dve.tensor_tensor_reduce(xn[:, b, :], x[:, b, :], x[:, b, :], 1.0, 0.0, ALU.mult, ALU.add,
                                                  ss[:, b:b + 1]))
                dve.tensor_scalar(ms[:, :], ss[:, :], 1.0 / D, EPS, ALU.mult, ALU.add).then_inc(sem("ms_ready"), 1)
                dve.wait_ge(sem("rms_ready"), call + 1)
                link(dve.reciprocal(rinv[:, :], rms[:, :]))
                for b in range(NB):
                    dve.tensor_scalar(xn[:, b, :], x[:, b, :], rinv[:, b:b + 1], None, ALU.mult).then_inc(
                        sem("xn_ready"), 1)

            def norm_turned(rows, call, x, xn, scale, bias=None):
                norm_rows(rows, x, xn)
                for k in range(KT):
                    src = ALLB[k // 2][:, (k % 2) * T:(k % 2 + 1) * T]
                    dve.wait_ge(sem("uh_ready"), KT * call + k // 2 * 2 + 2)
                    if bias is None:
                        ins = dve.scalar_tensor_tensor(UL[:, k, :], src, scale(k), UH[:, k, :].bitcast(F32), ALU.mult,
                                                       ALU.subtract)
                    else:
                        link(dve.tensor_scalar(mod_tmp[:, k % 2, :], src, scale(k), bias(k), ALU.mult, ALU.add))
                        ins = dve.tensor_tensor(UL[:, k, :], mod_tmp[:, k % 2, :], UH[:, k, :].bitcast(F32), ALU.subtract)
                    ins.then_inc(sem("u_ready"), 1)

            dve.wait_ge(sem("cols_landed"), 16)
            o = COL["ada_b"][0]
            link(dve.tensor_copy(modt[:, :, :], cols[:, o:o + 6 * KT].unsqueeze(2).to_broadcast([P, 6 * KT, 2])))
            z, s, s2, acc, e = lam_t[1], lam_t[2], lam_t[3], lam_t[4], lam_t[0]
            dve.scalar_tensor_tensor(lam_t[0][:, :], col("lam", 0, LB), -1.0, col("lam", 0, LB), ALU.mult, ALU.max).then_inc(sem("lam_abs"), 1)
            dve.wait_ge(sem("lam_exp"), 1)
            link(dve.tensor_scalar(s[:, :], z[:, :], 2.0, None, ALU.add))
            link(dve.reciprocal(s[:, :], s[:, :]))
            link(dve.tensor_tensor(s[:, :], s[:, :], z[:, :], ALU.mult))
            link(dve.tensor_tensor(s2[:, :], s[:, :], s[:, :], ALU.mult))
            link(dve.memset(acc[:, :], 1.0 / 19))
            for n in range(17, 0, -2):
                link(dve.tensor_tensor(acc[:, :], acc[:, :], s2[:, :], ALU.mult))
                link(dve.tensor_scalar(acc[:, :], acc[:, :], 1.0 / n, None, ALU.add))
            link(dve.tensor_tensor(acc[:, :], acc[:, :], s[:, :], ALU.mult))
            link(dve.tensor_scalar(e[:, :], col("lam", 0, LB), -1.0, 0.0, ALU.mult, ALU.max))
            link(dve.scalar_tensor_tensor(acc[:, :], acc[:, :], 2.0, e[:, :], ALU.mult, ALU.add))
            link.mark(dve.tensor_scalar(p_col[:, :], acc[:, :], LRU_C, None, ALU.mult))
            dve.tensor_scalar(n_col[:, :], acc[:, :], -LRU_C, None, ALU.mult).then_inc(sem("lam_ready"), 1)
            for m in range(LEAD):
                lo(m)
            dve.sem_inc(acc_free_dve, 2)
            dve.wait_ge(sem("x_landed"), 16)
            norm_turned(0, 0, X, XN, lambda k: col("ln1", k))
            to_pin = to(lambda t: Pin[:, 1, bass.ds(t * CW, CW)], CW)
            linear(S_IN, Q_IN, W_IN_HEAD, to_pin)

            def lru():
                link(dve.memset(lru_x[:, :, 0:CONV_W - 1], 0.0))
                yield from pause(2)
                for j in range(4):
                    dve.wait_ge(sem("lru_x_ready"), j + 1)
                    for tap in range(CONV_W):
                        for b in (2 * j, 2 * j + 1):
                            w, x = col("conv", tap * LB + b), lru_x[:, b, tap:tap + T]
                            if tap == 0:
                                link.mark(dve.tensor_scalar(lru_u[:, b, :], x, w, col("convb", b), ALU.mult, ALU.add))
                            else:
                                link.mark(dve.scalar_tensor_tensor(lru_u[:, b, :], x, w, lru_u[:, b, :], ALU.mult, ALU.add))
                        link.sync()
                        if tap % 2:
                            yield
                dve.sem_inc(sem("lru_u_ready"), 1)
                yield from pause(12)
                dve.wait_ge(sem("lru_gates_ready"), 2 * LB)
                link(dve.tensor_tensor(wide(1), wide(1), lru_u[:, :, :].rearrange("p (n b) t -> p n (b t)", n=NB), ALU.mult))
                yield from pause(2)
                dve.wait_ge(sem("lru_tanh"), LB)
                link(dve.tensor_scalar(lru_u[:, :, :], lru_b[:, :, :], 1.0, None, ALU.add))
                yield
                link(dve.reciprocal(lru_u[:, :, :], lru_u[:, :, :]))
                yield
                dve.scalar_tensor_tensor(lru_b[:, :, :], lru_b[:, :, :], 2.0, lru_u[:, :, :], ALU.mult, ALU.mult).then_inc(
                    sem("lru_sq_ready"), 1)
                yield from pause(2)
                dve.wait_ge(sem("lru_root"), 1)
                link(dve.tensor_tensor(lru_b[:, :, :].rearrange("p (n b) t -> p n (b t)", n=NB),
                                       lru_b[:, :, :].rearrange("p (n b) t -> p n (b t)", n=NB), wide(1), ALU.mult))
                yield
                dve.wait_ge(sem("lru_a_ready"), LB)
                for b in range(LB):
                    link.mark(dve.tensor_tensor_scan(lru_u[:, b, :], half(0)(b), lru_b[:, b, :], 0.0, ALU.mult, ALU.add))
                    if b % 2:
                        yield
                link.sync()
                dve.tensor_tensor(lru_g[:, :, :], lru_g[:, :, :], lru_u[:, :, :], ALU.mult).then_inc(sem("lru_y_ready"), 1)
                yield
                dve.wait_ge(sem("rope_landed"), 16)
                dve.wait_ge(acc_free_act, Q_IN + 8 + 2)
                dve.wait_ge(acc_free_dve, Q_IN + 8 + 2)
                dve.wait_ge(sem("lru_y_ready"), 1)
                for b in range(NB):
                    qk = Pin[:, b, C_Q:C_V].rearrange("p (h u e) -> p h u e", u=2, e=P // 2)
                    t1, t2 = qk[:, :, 0, :], qk[:, :, 1, :]
                    c, s = (rope[:, b, j:j + 1, :].to_broadcast([P, KT, P // 2]) for j in range(2))
                    for k, (dst, t, w) in enumerate(((rt[0], t1, c), (rt[1], t2, s), (rt[2], t1, s), (rt[3], t2, c))):
                        link.mark(dve.tensor_tensor(dst[:, :, :], t, w, ALU.mult))
                        if k == 1:
                            yield
                    link.sync()
                    yield
                    link.mark(dve.tensor_tensor(t1, rt[0][:, :, :], rt[1][:, :, :], ALU.subtract))
                    link(dve.tensor_tensor(t2, rt[2][:, :, :], rt[3][:, :, :], ALU.add))
                    dve.sem_inc(sem("rope_ready"), 1)
                    yield

            linear_among(S_IN, Q_IN, W_IN_HEAD, W_IN_TILES, to_pin, lru())
            if until < 2:
                return
            dve.wait_ge(sem("lru_yh_ready"), 1)
            dve.tensor_tensor(UL[:, 0:LB, :], lru_g[:, :, :], UH[:, 0:LB, :].bitcast(F32), ALU.subtract).then_inc(
                sem("y1_ready"), LB)
            dve.wait_ge(sem("y1_ready"), LB)

            o = COL["zeta"][0]
            dve.tensor_tensor(ret_kz[:, :, :], Pin[:, 0, C_Q + 1024:C_V].rearrange("p (h e) -> p h e", e=P),
                              cols[:, o:o + HEADS].unsqueeze(2).to_broadcast([P, HEADS, P]), ALU.mult).then_inc(
                sem("ret_kz_ready"), 1)
            dve.wait_ge(sem("decay_landed"), 16)
            for j in range(4):
                dve.wait_ge(sem("ret_scores"), j + 1)
                for m in range(2):
                    h = 2 * j + m
                    ins = dve.tensor_tensor(ret_s[:, h, :, :], DB[j][:, m * T:(m + 1) * T].rearrange("p (n q) -> p n q", q=P),
                                            decay[:, h:h + 1, :].to_broadcast([P, NB, P]), ALU.mult)
                ins.then_inc(sem("ret_s_ready"), 1)
            dve.wait_ge(sem("ret_inner"), 1)
            for j in range(2):
                link.mark(dve.tensor_copy(ret_o[:, 0, 4 * j:4 * j + 4, :], bank[j][:, :].rearrange("p (h e) -> p h e", e=P)))
            dve.wait_ge(sem("ret_cross"), 1)
            o = COL["xi"][0]
            for j in range(2):
                link(dve.tensor_tensor(ret_o[:, 1, 4 * j:4 * j + 4, :], DB[2 + j][:, :].rearrange("p (h e) -> p h e", e=P),
                                       cols[:, o + 4 * j:o + 4 * j + 4].unsqueeze(2).to_broadcast([P, 4, P]), ALU.mult))
                link(dve.tensor_tensor(ret_o[:, 1, 4 * j:4 * j + 4, :], ret_o[:, 1, 4 * j:4 * j + 4, :],
                                       bank[2 + j][:, :].rearrange("p (h e) -> p h e", e=P), ALU.add))
            heads = ret_o[:, :, :, :].rearrange("p n h e -> p (n h) e")
            sq = ret_sq[:, :, :, :].rearrange("p n h e -> p (n h) e")
            nh = [P, NB * HEADS, P]
            link(dve.tensor_reduce(gn[0][:, :], heads, AX.X, ALU.add))
            link(dve.tensor_scalar(gn[0][:, :], gn[0][:, :], 1.0 / P, None, ALU.mult))
            link(dve.tensor_tensor(heads, heads, gn[0][:, :].unsqueeze(2).to_broadcast(nh), ALU.subtract))
            link(dve.tensor_tensor(sq, heads, heads, ALU.mult))
            link(dve.tensor_reduce(gn[0][:, :], sq, AX.X, ALU.add))
            dve.tensor_scalar(gn[0][:, :], gn[0][:, :], 1.0 / P, EPS, ALU.mult, ALU.add).then_inc(sem("gn_var"), 1)
            dve.wait_ge(sem("gn_root"), 1)
            link(dve.reciprocal(gn[2][:, :], gn[1][:, :]))
            link(dve.tensor_tensor(heads, heads, gn[2][:, :].unsqueeze(2).to_broadcast(nh), ALU.mult))
            dve.wait_ge(sem("ret_gate"), 1)
            dve.tensor_tensor(ret_o[:, :, :, :].rearrange("p n h e -> p n (h e)"),
                              ret_o[:, :, :, :].rearrange("p n h e -> p n (h e)"), Pin[:, :, C_G:C_G + 1024],
                              ALU.mult).then_inc(sem("ret_o_ready"), 1)
            for h in range(HEADS):
                dve.wait_ge(sem("ret_yh_ready"), h // 2 * 2 + 2)
                dve.scalar_tensor_tensor(UL[:, LB + h, :], bank[h // 2][:, (h % 2) * T:(h % 2 + 1) * T], col("gnw", h),
                                         UH[:, LB + h, :].bitcast(F32), ALU.mult, ALU.subtract).then_inc(
                    sem("y1_ready"), 1)
            linear(S_OUT, Q_OUT, OUT_TILES, add_to_x)
            dve.wait_ge(acc_free_dve, Q_FFN + 2)
            if until < 3:
                return

            link.mark(dve.memset(cond[:, :, 4:P].bitcast(F32), 0.0))
            dve.wait_ge(sem("cond_hi"), 1)
            link.mark(dve.tensor_tensor(cond[:, :, 2:4], csil[:, :, :], cond[:, :, 0:2].bitcast(F32), ALU.subtract))
            link.sync()
            dve.sem_inc(sem("cond_ready"), 1)
            norm_turned(1, 1, X, XN, lambda k: col("ln2", k))
            dve.sem_inc(sem("down_added"), 2)

            def up(i=None, nth=0):
                dve.wait_ge(acc_free_act, lin(Q_FFN + 2 + 2 * (nth + 1), i, 2))
                if i is not None:
                    dve.wait_ge(sem("ff_turned"), lin(nth, i, 1))
                for b in range(NB):
                    ins = dve.tensor_tensor(ff[:, b, :], ACC[1][b][:, :], ff_g[:, b, :], ALU.mult)
                ins.then_inc(sem("ff_ready"), 1)
                dve.sem_inc(acc_free_dve, 2)

            def turned(i=None, nth=0):
                for k in range(CK):
                    dve.wait_ge(sem("ffh_ready"), lin(CK * nth + k // 2 * 2 + 2, i, CK))
                    dve.tensor_tensor(FL[:, k, :], bank[2 + k // 2][:, (k % 2) * T:(k % 2 + 1) * T],
                                      FH[:, k, :].bitcast(F32), ALU.subtract).then_inc(sem("ffT_ready"), 1)

            def add_down(n, j, i=None, per=0):
                dve.wait_ge(split_used, lin(n + 1, i, per))
                for b in range(NB):
                    x = X[:, b, j * CW:(j + 1) * CW]
                    ins = dve.tensor_tensor(x, DB[2 * (j % 2) + b][:, :], x, ALU.add)
                ins.then_inc(sem("down_added"), 1)

            def step(kinds, n, i=None, tile=0):
                m = dict.fromkeys(kinds, 0)
                for p, kind in enumerate(kinds):
                    lo(n + LEAD + p, i, len(FF_STEP))
                    m[kind] += 1
                    if kind == "u" and m[kind] == CPT:
                        dve.wait_ge(split_used, lin(n + p + 1, i, len(FF_STEP)))
                        up(i, tile)
                    if kind == "d":
                        add_down(n + p, m[kind] - 1, i, len(FF_STEP))

            def modulation(i=None, nth=0):
                for t in range(ADA_STEP):
                    dve.wait_ge(sem("ada_cols"), lin(ADA_STEP * nth + t + 1, i, ADA_STEP))
                    w = CW // P
                    m = modt[:, bass.ds(lin(w * (ADA_STEP * nth + t), i, w * ADA_STEP), w), :]
                    dve.tensor_tensor(m, ACC[0][t][:, 0:2 * w].rearrange("p (j r) -> p j r", r=2), m, ALU.add).then_inc(
                        sem("mod_ready"), 1)

            step(FF_FIRST, S_FFN)
            turned()
            modulation()
            with dve.Fori(0, FT - 1) as i:
                step(FF_STEP, S_STEP, i, tile=1)
                modulation(i, 1)
                turned(i, 1)
            step(FF_LAST, S_LAST)
            modulation(nth=FT)
            dve.wait_ge(sem("down_added"), 2 + FT * OUT_TILES)
            if until < 4:
                return

            dve.wait_ge(sem("mod_ready"), ADA_TILES)
            for r in range(2):
                link(dve.scalar_tensor_tensor(sc_mix[:, r, :], modt[:, KT:2 * KT, r], 1.0, col("nmix", 0, KT), ALU.add,
                                              ALU.mult))
            link(dve.scalar_tensor_tensor(sc_ffn[:, :], modt[:, 4 * KT:5 * KT, 0], 1.0, col("nffn", 0, KT), ALU.add,
                                          ALU.mult))

            norm_rows(2, X, XN)
            dve.wait_ge(sem("xn_ready"), 2 * 3)
            dve.wait_ge(sem("fnw_landed"), 16)
            for b in range(NB):
                link.mark(dve.tensor_tensor(X[:, b, :], XN[:, b, :], fnw[:, :], ALU.mult))
            link.sync()
            dve.sem_inc(sem("x2_ready"), 1)

            def conv(S, dst, taps, padded, base):
                for j in range(4):
                    dve.wait_ge(sem(padded), base + (4 if S.lat else j + 1))
                    for tap in range(3):
                        for b in (2 * j, 2 * j + 1):
                            w, x = col("qkconv", tap * 2 * MB + taps + b), S.pad[:, b, tap:tap + T]
                            if tap == 0:
                                link.mark(dve.tensor_scalar(dst(b), x, w, None, ALU.mult))
                            else:
                                link.mark(dve.scalar_tensor_tensor(dst(b), x, w, dst(b), ALU.mult, ALU.add))
                        link.sync()
                    yield

            def edges(S):
                for t in (0, T + 1):
                    link.mark(dve.memset(S.pad[:, :, t:t + 1], 0.0))
                link.sync()

            def gates(s):
                dve.wait_ge(sem("gate_ps"), s + 1)
                dve.tensor_copy(g_row[s][0:NG, :], DB[2][0:NG, 0:T]).then_inc(sem("g_row_ready"), 1)

            def gate_rows(S):
                dve.wait_ge(sem("gate_rows_ps"), S.s + 1)
                for typ, dst in ((0, S.A), (1, S.lf)):
                    for d in range(2):
                        link.mark(dve.tensor_scalar(dst[:, d, :], DB[2 + typ][0:MH, d * T:(d + 1) * T],
                                                    col("bgate", 2 * d + typ, rows=MH), None, ALU.add))
                link.sync()
                dve.sem_inc(sem("gate_rows_kept"), 1)
                dve.scalar_tensor_tensor(S.b, S.lf, -1.0, S.lf, ALU.mult, ALU.max).then_inc(sem("fg_abs"), 1)
                link(dve.memset(S.M, 0.0))
                yield
                dve.wait_ge(sem("fg_log"), S.s + 1)
                link(dve.scalar_tensor_tensor(S.lf, S.lf, 0.0, S.b, ALU.min, ALU.subtract))
                for d in range(2):
                    for n in range(NB):
                        link.mark(dve.tensor_tensor_scan(scan_ap(S.b, d, n), scan_ap(S.lf, d, n), scan_ap(S.M, d, n), 0.0,
                                                         ALU.add, ALU.add))
                link.sync()
                link(dve.tensor_tensor(S.A, S.A, S.b, ALU.subtract))
                yield
                for step, d, n in S.steps:
                    m0 = NB * S.s + step
                    link(dve.tensor_tensor_scan(scan_ap(S.M, d, n), scan_ap(S.A, d, n), scan_ap(S.A, d, n),
                                                m_st[0:MH, d, m0:m0 + 1], ALU.max, ALU.max))
                    last = last_of(S.M, d, n)
                    link.mark(dve.tensor_tensor(m_st[0:MH, d, m0 + 1:m0 + 2], last_of(S.b, d, n), last, ALU.add))
                    link.mark(dve.tensor_scalar(n_ml[0:MH, d, n:n + 1], last, -1.0, None, ALU.mult))
                    link(dve.tensor_tensor(dcy[0:MH, d, n:n + 1], m_st[0:MH, d, m0:m0 + 1], last, ALU.subtract))
                    if d == 1:
                        yield
                if S.lat:
                    link(dve.tensor_tensor(S.ex, S.b, S.M, ALU.add))
                dve.sem_inc(sem("row_max"), 1)
                if S.lat:
                    link(dve.tensor_scalar(S.b, S.M, -1.0, None, ALU.mult))

            def rows_done(S):
                dve.wait_ge(sem("rows_exp"), S.s + 1)
                dve.sem_inc(sem("rows_ready"), 1)

            def columns(S):
                dve.wait_ge(sem("cols_ps"), S.s + 1)
                for k in range(5) if S.lat else (1, 4):
                    w = 2 * NB * MH
                    link.mark(dve.tensor_copy(co[:, k, :, :, :].rearrange("p d n h -> p (d n h)"), DB[2][:, k * w:(k + 1) * w]))
                link.sync()
                dve.sem_inc(sem("co_ready"), 1)

            def ones(S):
                link.mark(dve.memset(S.v1[:, :, :, MD:VA], 1.0))
                for n in range(NB):
                    link.mark(dve.tensor_copy(S.v1[:, n, :, 0:MD], S.v(n).rearrange("p (h e) -> p h e", e=MD)))
                link.sync()

            upd = [0]

            def update(S, d, n):
                u = upd[0]
                for h in range(MH):
                    if u * MH + h >= 2:
                        dve.wait_ge(sem("state_ps"), u * MH + h - 1)
                    dve.tensor_scalar(vw[:, h % 2, :], S.v1[:, n, h, :], co[:, 1, d, n, h:h + 1], None, ALU.mult).then_inc(
                        sem("vw_ready"), 1)
                for h in range(MH):
                    dve.wait_ge(sem("state_ps"), u * MH + h + 1)
                    for kt in range(MKT):
                        s = st[:, d, h, kt, :]
                        link.mark(dve.scalar_tensor_tensor(s, s, co[:, 4, d, n, h:h + 1], ALLB[2 * h + kt][:, 0:VA], ALU.mult,
                                                           ALU.add))
                link.sync()
                dve.sem_inc(sem("state_ready"), 1)
                upd[0] += 1

            def gate_weights(s):
                dve.wait_ge(sem("wg_hi"), s + 1)
                dve.tensor_tensor(wg_l[s][:, :, :], wg[:, :, :], wg_h[s][:, :, :].bitcast(F32), ALU.subtract).then_inc(
                    sem("wg_ready"), 1)

            dve.wait_ge(sem("ctx_landed"), 16)
            norm_turned(3, 2, ctx_x, ctx_n, lambda k: sc_mix[:, 1, k:k + 1], lambda k: modt[:, k, 1:2])
            gate_weights(0)
            linear(S_CTX, Q_CTX, CTX_TILES, to(lambda t: kv[:, 1, bass.ds(t * CW, CW)], CW))
            if until < 5:
                return
            C = streams[0]
            gates(0)
            edges(C)
            link.mark(dve.memset(m_st[0:MH, :, :], 0.0))
            link.mark(dve.memset(st[:, :, :, :, :], 0.0))
            for _ in conv(C, C.kT, MB, "k_pad_ready", 0):
                pass
            dve.sem_inc(sem("k_conv"), 1)
            for _ in gate_rows(C):
                pass
            rows_done(C)
            dve.wait_ge(sem("k_silu"), 1)
            dve.wait_ge(acc_free_act, Q_IN2 + 2)
            dve.wait_ge(acc_free_dve, Q_IN2 + 2)
            ones(C)
            columns(C)
            for step, d, n in C.steps:
                update(C, d, n)
            dve.sem_inc(sem("ctx_done"), 1)
            if until < 6:
                return

            norm_turned(4, 3, X, XN2, lambda k: sc_mix[:, 0, k:k + 1], lambda k: modt[:, k, 0:1])
            gate_weights(1)
            def to_p2(par, t):
                dve.tensor_copy(P2[:, 1, W2_ORDER[t] * CW:(W2_ORDER[t] + 1) * CW], ACC[par][1][:, :]).then_inc(acc_free_dve, 1)

            linear(S_IN2, Q_IN2, W2_HEAD, to(lambda t: P2[:, 1, bass.ds(t * CW, CW)], CW))
            L = streams[1]

            def mixers():
                yield
                gates(1)
                dve.wait_ge(sem("sgu_gelu"), 1)
                dve.wait_ge(sem("sgu_n_landed"), 16)
                for b in range(NB):
                    v = P2[:, b, O_V:O_P]
                    link(dve.tensor_tensor_reduce(sgu_sq[:, :], v, v, 1.0, 0.0, ALU.mult, ALU.add, ss[:, b:b + 1]))
                dve.tensor_scalar(ms[:, :], ss[:, :], 1.0 / D_SGU, EPS, ALU.mult, ALU.add).then_inc(sem("sgu_ms"), 1)
                yield from pause(2)
                dve.wait_ge(sem("sgu_root"), 1)
                link(dve.reciprocal(rinv[:, :], rms[:, :]))
                for b in range(NB):
                    v = P2[:, b, O_V:O_P]
                    ins = dve.scalar_tensor_tensor(v, v, rinv[:, b:b + 1], sgu_n[:, :], ALU.mult, ALU.mult)
                ins.then_inc(sem("sgu_v_ready"), 1)
                yield from pause(2)
                dve.wait_ge(sem("sgu_ps"), 1)
                for n in range(NB):
                    for h in range(SH):
                        u = P2[:, n, O_U + h * P:O_U + (h + 1) * P]
                        ins = dve.scalar_tensor_tensor(u, DB[n][:, h * P:(h + 1) * P], col("sgub", h), u, ALU.add, ALU.mult)
                ins.then_inc(sem("sgu_y_ready"), 1)
                yield from pause(4)
                dve.wait_ge(sem("sgu_turned"), 2)
                dve.wait_ge(sem("pool_ps"), len(PW))
                yield from gate_rows(L)
                yield
                dve.wait_ge(sem("pool_y_ps"), len(PW))
                edges(L)
                qT = lat_half(O_Q)
                yield from conv(L, qT, 0, "q_pad_ready", 0)
                dve.sem_inc(sem("q_conv"), 1)
                yield
                yield from conv(L, L.kT, MB, "k_pad_ready", 4)
                dve.sem_inc(sem("k_conv"), 1)
                yield from pause(3)
                dve.wait_ge(acc_free_act, Q_IN2 + 9 + 2)
                dve.wait_ge(acc_free_dve, Q_IN2 + 9 + 2)
                ones(L)
                dve.sem_inc(sem("v1_ready"), 1)
                rows_done(L)
                yield from pause(2)
                dve.wait_ge(sem("ml_scores"), 1)
                for j in range(2):
                    link.mark(dve.tensor_copy(sc_t[:, 2 * j:2 * j + 2, :, :].rearrange("p h n t -> p (h n t)"), DB[j][:, :]))
                link.sync()
                dve.sem_inc(sem("sc_t_ready"), 1)
                yield
                columns(L)

            linear_among(S_IN2, Q_IN2, W2_HEAD, W2_TILES, to_p2, mixers())
            x = 0
            for step, d, n in L.steps:
                def weights(h):
                    dve.wait_ge(sem("w_exp"), x + h + 1)
                    dve.tensor_tensor(wb[:, h % 2, :], wb[:, h % 2, :], sc_t[:, h, n, :], ALU.mult).then_inc(sem("w_ready"), 1)
                weights(0)
                for h in range(MH):
                    if h + 1 < MH:
                        weights(h + 1)
                    dve.wait_ge(sem("inter_ready"), x + h + 1)
                    t = ml_t[:, h % 2, :]
                    link(dve.tensor_tensor(t, t, ACC[h % 2][0][:, 0:VA], ALU.add))
                    link(dve.scalar_tensor_tensor(den[:, 0:1], t[:, MD:VA], -1.0, t[:, MD:VA], ALU.mult, ALU.max))
                    link(dve.tensor_scalar(den[:, 0:1], den[:, 0:1], co[:, 3, d, n, h:h + 1], None, ALU.max))
                    link(dve.reciprocal(den[:, 1:2], den[:, 0:1]))
                    y = P2[:, n, O_K + h * MD:O_K + (h + 1) * MD]
                    if step == 0:
                        ins = dve.tensor_scalar(y, t[:, 0:MD], den[:, 1:2], None, ALU.mult)
                    else:
                        ins = dve.scalar_tensor_tensor(y, t[:, 0:MD], den[:, 1:2], y, ALU.mult, ALU.add)
                    ins.then_inc(sem("h_ready"), 1)
                x += MH
                dve.wait_ge(sem("h_ready"), x)
                if step == 0:
                    update(L, d, n)
            nh = [P, MH, MD]
            for n in range(NB):
                y = P2[:, n, O_K:O_K + D_ML]
                sq = P2[:, n, O_Q:O_Q + D_ML]
                link(dve.tensor_tensor(sq, y, y, ALU.mult))
                link(dve.tensor_reduce(l_ms[2][:, n * MH:(n + 1) * MH], sq.rearrange("p (h e) -> p h e", e=MD), AX.X, ALU.add))
            dve.tensor_scalar(l_ms[0][:, :], l_ms[2][:, :], 1.0 / MD, EPS, ALU.mult, ALU.add).then_inc(sem("ml_ms"), 1)
            dve.wait_ge(sem("ml_root"), 1)
            link(dve.reciprocal(l_ms[2][:, :], l_ms[1][:, :]))
            dve.wait_ge(sem("ml_gate"), 1)
            for n in range(NB):
                y = P2[:, n, O_K:O_K + D_ML]
                yh = y.rearrange("p (h e) -> p h e", e=MD)
                link(dve.tensor_tensor(yh, yh, l_ms[2][:, n * MH:(n + 1) * MH].unsqueeze(2).to_broadcast(nh), ALU.mult))
                link(dve.tensor_tensor(y, y, P2[:, n, O_O:O_O + D_ML], ALU.mult))
            dve.sem_inc(sem("ml_y_ready"), 1)
            for g in range(len(PW)):
                dve.wait_ge(sem("yh2_ready"), g + 1)
                dve.tensor_tensor(UL[:, 12 + g, :], pool_y[:, g, :], UH[:, 12 + g, :].bitcast(F32), ALU.subtract).then_inc(
                    sem("y2_ready"), 1)
            for k in range(4):
                dve.wait_ge(sem("yh2_ready"), 4 + k + 1)
                dve.tensor_tensor(UL[:, k, :], sgu_t[:, k, :], UH[:, k, :].bitcast(F32), ALU.subtract).then_inc(
                    sem("y2_ready"), 1)
            for b in range(MB):
                dve.wait_ge(sem("yh2_ready"), 8 + b // 2 * 2 + 2)
                dve.scalar_tensor_tensor(UL[:, 4 + b, :], DB[b // 2][:, (b % 2) * T:(b % 2 + 1) * T], col("mlnorm", b),
                                         UH[:, 4 + b, :].bitcast(F32), ALU.mult, ALU.subtract).then_inc(sem("y2_ready"), 1)
            if until < 8:
                return

            def add_gated(par, t):
                for b in range(NB):
                    ins = dve.tensor_tensor(g_tmp[:, b, :], ACC[par][b][:, :], gb1[:, bass.ds(t * CW, CW)], ALU.mult)
                ins.then_inc(sem("gated"), 1)
                dve.wait_ge(sem("gated"), t + 1)
                for b in range(NB):
                    x = X[:, b, bass.ds(t * CW, CW)]
                    ins = dve.tensor_tensor(x, g_tmp[:, b, :], x, ALU.add)
                ins.then_inc(acc_free_dve, 1)

            dve.wait_ge(sem("spread_ready"), 8)
            linear(S_OUT2, Q_OUT2, OUT_TILES, add_gated)
            dve.wait_ge(acc_free_dve, Q_WQ + 2)
            norm_turned(5, 4, X, XN2, lambda k: sc_ffn[:, k:k + 1], lambda k: modt[:, 3 * KT + k, 0:1])
            linear(S_WQ, Q_WQ, OUT_TILES, to(lambda t: q_tok[:, 1, bass.ds(t * CW, CW)], CW))
            dve.wait_ge(sem("spread_ready"), 16)
            for b in range(NB):
                link(dve.tensor_tensor(XN2[:, b, :], XN2[:, b, :], sc_row[:, :], ALU.mult))
                link(dve.tensor_tensor(XN2[:, b, :], XN2[:, b, :], sh_row[:, :], ALU.add))
                dve.sem_inc(sem("hf_ready"), 1)
            if until < 9:
                return

            def top16(values, keep, pos):
                for r in range(2):
                    w = slice(8 * r, 8 * r + 8)
                    for v, k in zip(values, keep):
                        link.mark(dve.max(k[:, w], v))
                    link.sync()
                    yield
                    for v, k, p in zip(values, keep, pos):
                        link.mark(dve.max_index(p[:, w], k[:, w], v))
                    if r == 0:
                        yield
                        for v, k in zip(values, keep):
                            link.mark(dve.match_replace(v, k[:, w], v, LOWEST))
                    link.sync()
                    yield

            def choose(b):
                dve.wait_ge(sem("key_s_ready"), 4 * (b + 1))
                yield from top16([key_s[:, b, hp, :] for hp in range(2 * PH)], [top_v[:, hp, :] for hp in range(2 * PH)],
                      [top_i[:, hp, :] for hp in range(2 * PH)])
                link.mark(dve.tensor_copy(top_f[:, :, :], top_i[:, :, :]))
                both = top_v[:, :, :].rearrange("p (h s) k -> p h s k", s=2)
                full = [P, PH, TOPK, TOPK]
                link(dve.tensor_tensor(cand[:, :, :, :], both[:, :, 0, :].unsqueeze(3).to_broadcast(full),
                                       both[:, :, 1, :].unsqueeze(2).to_broadcast(full), ALU.add))
                yield from top16([cand[:, h, :, :].rearrange("p a b -> p (a b)") for h in range(PH)], [best_v[:, h, :] for h in range(PH)],
                      [best_i[:, h, :] for h in range(PH)])
                dve.wait_ge(sem("key_s_ready"), 8)
                ranks = best_i[:, :, :].rearrange("p h k -> p (h k)")
                of = top_f[:, :, :].rearrange("p (h s) k -> p h s k", s=2)
                hots = hot[:, :, :, :].rearrange("p h j k -> p (h j) k")
                o = COL["iota"][0]
                for s in range(2):
                    op, by = (ALU.logical_shift_right, 4) if s == 0 else (ALU.bitwise_and, TOPK - 1)
                    link(dve.tensor_scalar(pick_i[:, :], ranks, by, None, op))
                    link(dve.tensor_copy(pick_f[:, :], pick_i[:, :]))
                    link(dve.tensor_tensor(hots, cols[:, o:o + TOPK].unsqueeze(1).to_broadcast([P, SLOTS, TOPK]),
                                           pick_f[:, :].unsqueeze(2).to_broadcast([P, SLOTS, TOPK]), ALU.is_equal))
                    link(dve.tensor_tensor(hot[:, :, :, :], hot[:, :, :, :], of[:, :, s, :].unsqueeze(2).to_broadcast(full),
                                           ALU.mult))
                    link(dve.tensor_reduce(exp_f[s][:, :], hots, AX.X, ALU.add))
                    yield
                link(dve.scalar_tensor_tensor(pick_f[:, :], exp_f[0][:, :], float(NKEY), exp_f[1][:, :], ALU.mult, ALU.add))
                dve.tensor_copy(idx[:, b, :], pick_f[:, :]).then_inc(sem("idx_ready"), 1)
                w = gate_w[:, b, :].rearrange("p (h k) -> p h k", k=TOPK)
                dve.tensor_tensor(w, best_v[:, :, :], best_v[:, :, 0:1].to_broadcast([P, PH, TOPK]), ALU.subtract).then_inc(
                    sem("best_ready"), 1)
                dve.wait_ge(sem("soft_exp"), b + 1)
                link(dve.tensor_reduce(soft[:, :], w, AX.X, ALU.add))
                link(dve.reciprocal(soft[:, :], soft[:, :]))
                link(dve.tensor_tensor(w, w, soft[:, :].unsqueeze(2).to_broadcast([P, PH, TOPK]), ALU.mult))

            def landed(g0, s, i=None):
                dve.wait_ge(sem(f"row_landed{s % GATH}"), lin(16 * ((g0 + s) // GATH + 1), i, 16 * GSTEP // GATH))

            dve.sem_inc(sem("row_used"), GATH)
            for _ in choose(0):
                pass
            pieces = choose(1)
            for s in range(SLOTS):
                landed(0, s)
                r = rows_g[:, s % GATH, :]
                dve.tensor_tensor_reduce(r, r, XN2[:, 0, :], 1.0, 0.0, ALU.mult, ALU.add, dots[:, 0, s:s + 1]).then_inc(
                    sem("row_used"), 1)
                if s % GATH == GATH - 1:
                    next(pieces, None)
            for _ in pieces:
                pass
            with dve.Fori(0, SLOTS // GSTEP) as i:
                for s in range(GSTEP):
                    landed(SLOTS, s, i)
                    r = rows_g[:, s % GATH, :]
                    dve.tensor_tensor_reduce(r, r, XN2[:, 1, :], 1.0, 0.0, ALU.mult, ALU.add,
                                             step_dots[:, s:s + 1]).then_inc(sem("row_used"), 1)
                dve.wait_ge(sem("row_used"), lin(GATH + SLOTS + GSTEP, i, GSTEP))
                dve.tensor_copy(dots[:, 1, bass.ds(i * GSTEP, GSTEP)], step_dots[:, :]).then_inc(sem("dots_kept"), 1)
                dve.wait_ge(sem("dots_kept"), lin(1, i, 1))
            dve.wait_ge(sem("dots_kept"), SLOTS // GSTEP)
            dve.sem_inc(sem("dots_done"), 1)
            dve.wait_ge(sem("dots_gelu"), 1)
            link(dve.tensor_tensor(gate_w[:, :, :], gate_w[:, :, :], dots[:, :, :], ALU.mult))
            for b in range(NB):
                g0 = (NB + b) * SLOTS
                link(dve.memset(v_sum[:, :, :], 0.0))
                with dve.Fori(0, SLOTS // GSTEP) as i:
                    for s in range(GSTEP):
                        landed(g0, s, i)
                        dve.wait_ge(sem("row_used"), lin(GATH + g0 + s - 1, i, GSTEP))
                        v = v_sum[:, s % 2, :]
                        dve.scalar_tensor_tensor(v, rows_g[:, s % GATH, :], gate_w[:, b, bass.ds(lin(s, i, GSTEP), 1)], v,
                                                 ALU.mult, ALU.add).then_inc(sem("row_used"), 1)
                dve.wait_ge(sem("row_used"), GATH + g0 + SLOTS)
                v = v_sum[:, 0, :]
                link(dve.tensor_tensor(v, v, v_sum[:, 1, :], ALU.add))
                link(dve.tensor_tensor(v, v, gb2[:, :], ALU.mult))
                x = X[:, b, :]
                link(dve.tensor_tensor(x, x, v, ALU.add))
                link(dve.tensor_tensor_reduce(v_sum[:, 1, :], x, x, 1.0, 0.0, ALU.mult, ALU.add, ss[:, b:b + 1]))
                dve.tensor_scalar(ms[:, b:b + 1], ss[:, b:b + 1], 1.0 / D, EPS, ALU.mult, ALU.add).then_inc(sem("fin_ms"), 1)
                dve.wait_ge(sem("fin_root"), b + 1)
                link(dve.reciprocal(rinv[:, b:b + 1], rms[:, b:b + 1]))
                dve.wait_ge(sem("nfin_landed"), 16)
                dve.scalar_tensor_tensor(x, x, rinv[:, b:b + 1], nfin[:, :], ALU.mult, ALU.mult).then_inc(
                    sem("out_ready"), 1)


def tables():
    f = np.float32
    pos, half = np.arange(T, dtype=f), P // 2
    freq = (f(10000.0) ** (-np.arange(0, P, 2, dtype=f) / f(P))).astype(f)
    ang = pos[:, None] * freq[None, :]
    rope = np.stack([np.cos(ang), np.sin(ang)], 1).astype(f).reshape(NB, P, 2, half).transpose(1, 0, 2, 3)
    lg = np.log1p(-np.exp2(-5.0 - np.arange(HEADS, dtype=np.float64)))
    k = np.arange(P)
    diff = k[None, :] - k[:, None]
    decay = np.where(diff[:, None, :] >= 0, np.exp(lg[None, :, None] * np.maximum(diff, 0)[:, None, :]), 0.0) * P ** -0.5
    xi = np.exp(lg[None, :] * (k[:, None] + 1))
    zeta = np.exp(lg[None, :] * (P - 1 - k[:, None])) * P ** -0.5
    rows = T // GRID_W
    pool = np.zeros((P, len(PW), NB, T))
    for g, w in enumerate(PW):
        def box(n):
            i = np.arange(n)
            lo, hi = np.clip(i - w // 2, 0, n), np.clip(i - w // 2 + w, 0, n)
            return ((i[None, :] >= lo[:, None]) & (i[None, :] < hi[:, None])).astype(np.float64)
        m = np.kron(box(rows), box(GRID_W))
        m = m / m.sum(1, keepdims=True) - np.eye(T)
        pool[:, g] = m.T.reshape(NB, P, T).transpose(1, 0, 2)
    mask = np.stack([np.where(diff >= 0, 0.0, -1e30), np.where(diff <= 0, 0.0, -1e30)], 1)
    sel = np.zeros((P, 2))
    sel[[0, 2], 0] = sel[[1, 3], 1] = 1.0
    out = {"rope": rope, "decay": decay, "pool_t": pool, "mask": mask, "ident": np.eye(P), "xi": xi, "zeta": zeta, "sel": sel,
           "iota": np.tile(np.arange(TOPK), (P, 1))}
    return {n: np.ascontiguousarray(v, dtype=f) for n, v in out.items()}


def chunks(w, rows_first=False):
    k, n = w.shape
    c = w.reshape(k // (CK * P), CK, P, n // CW, CW)
    c = c.transpose(0, 3, 2, 1, 4) if rows_first else c.transpose(3, 0, 2, 1, 4)
    return c.reshape(c.shape[0], c.shape[1], P, CK * CW)


def layout(v):
    t = tables()
    one = {n: np.asarray(x) for n, x in v.items()}
    first = {n: x[0] for n, x in one.items() if n not in ("x", "final_norm_w", "c_ctx_2", "ctx_2", "c_2", "norm_final_2")}
    stream = np.empty((NCH, P, CK * CW), np.float32)

    def put(at, c):
        c = c.reshape(-1, P, CK * CW)
        stream[at:at + len(c)] = c

    w2 = first["w_in_2"]
    put(S_IN, chunks(first["w_in"]))
    put(S_OUT, chunks(first["w_out"]))
    gate, up, down = chunks(first["w_ffn_gate"]), chunks(first["w_ffn_up"]), chunks(first["w_ffn_down"], True)
    ada = chunks(first["ada_w_2"])
    at = S_FFN
    for i in range(FT + 1):
        rest = {"g": list(gate[i]), "u": list(up[i])} if i < FT else {}
        rest["a"] = list(ada[ADA_STEP * i:ADA_STEP * (i + 1)].reshape(-1, P, CK * CW))
        rest["d"] = list(down[i - 1]) if i else []
        for kind in FF_FIRST if i == 0 else FF_STEP if i < FT else FF_LAST:
            stream[at] = rest[kind].pop(0)
            at += 1
    put(S_CTX, chunks(w2[:, O_K:O_G]))
    put(S_IN2, chunks(w2[:, :O_G])[list(W2_ORDER)])
    put(S_OUT2, chunks(first["w_out_2"]))
    put(S_WQ, chunks(first["peer_wq_2"]))

    def down_cols(x):
        return np.ascontiguousarray(x.reshape(-1, P).T)

    parts = {"ln1": down_cols(first["ln1_w"]), "ln2": down_cols(first["ln2_w"]), "ba": down_cols(first["gate_a_b"]),
             "bx": down_cols(first["gate_x_b"]), "conv": down_cols(first["conv_w"]), "convb": down_cols(first["conv_b"]),
             "lam": down_cols(first["lru_lambda"]), "gnw": down_cols(first["ret_gn_w"]), "nmix": down_cols(first["norm_mix_2"]),
             "nffn": down_cols(first["norm_ffn_2"]), "ada_b": down_cols(first["ada_b_2"]),
             "qkconv": down_cols(first["qk_conv_2"]), "mlnorm": down_cols(first["mlstm_norm_2"]),
             "pscale": down_cols(first["pool_scale_2"]), "c": down_cols(one["c_2"]), "cctx": down_cols(one["c_ctx_2"]),
             "sgub": down_cols(first["sgu_b_2"]), "xi": t["xi"], "zeta": t["zeta"], "sel": t["sel"], "iota": t["iota"]}
    cols = np.zeros((P, NCOL), np.float32)
    for name, x in parts.items():
        o, w = COL[name]
        cols[:, o:o + w] = x
    o, w = COL["bgate"]
    cols[0:MH, o:o + w] = first["b_gate_2"].reshape(4, MH).T

    def c(x):
        return np.ascontiguousarray(x)

    return {
        "x": one["x"], "ctx": one["ctx_2"], "wstream": stream, "cols": cols, "ident": t["ident"],
        "wa": c(first["gate_a_w"].transpose(1, 0, 2)), "wx": c(first["gate_x_w"].transpose(1, 0, 2)),
        "decay": t["decay"], "rope": t["rope"], "pool_t": t["pool_t"], "mask": t["mask"],
        "sgu_w": c(first["sgu_w_2"].transpose(2, 0, 1)), "pool_w": c(first["pool_w_2"].transpose(1, 0, 2)),
        "keys": c(first["peer_keys_2"].transpose(2, 0, 1)),
        "wg": c(w2[:, O_G:].reshape(KT, P, NG).transpose(1, 0, 2)),
        "fnw": one["final_norm_w"], "nfin": one["norm_final_2"], "sgu_n": first["sgu_norm_2"],
        "u_tab": first["peer_u_2"], "v_tab": first["peer_v_2"],
    }


def kernel(**inputs):
    import concourse.bacc as bacc
    from concourse.bass_utils import run_bass_kernel_spmd

    nc = bacc.Bacc("TRN2", target_bir_lowering=False, num_devices=1)
    arrays = {f"in_{n}_dram": np.ascontiguousarray(x) for n, x in layout(inputs).items()}
    args = {n[3:-5]: nc.dram_tensor(n, x.shape, mybir.dt.from_np(x.dtype), kind="ExternalInput").ap()
            for n, x in arrays.items()}
    out = nc.dram_tensor("out_dram", (1, T, D), F32, kind="ExternalOutput").ap()
    build(nc, args, out)
    return run_bass_kernel_spmd(nc, [arrays], core_ids=[0]).results[0]["out_dram"]
```

```python
from contextlib import ExitStack

import numpy as np
import concourse.bass as bass
from concourse import mybir

ALU = mybir.AluOpType
ACT = mybir.ActivationFunctionType
AX = mybir.AxisListType
F32 = mybir.dt.float32
F32R = mybir.dt.float32r
U32 = mybir.dt.uint32
I32 = mybir.dt.int32

P = 128
NB = 2
T = NB * P
D = 2048
KT = D // P
EPS = 1e-6
CW = 512
CK = 4
CPT = KT // CK
SLOTS_W = 4
LEAD = 2

D_LRU = 1024
LB = D_LRU // P
CONV_W = 4
LRU_C = 8.0
HEADS = 8
W_IN_TILES = 6144 // CW
W_IN_HEAD = 2
D_FF = 5632
FT = D_FF // CW
C_Q, C_V, C_G = 2048, 4096, 5120

D_SGU = 512
SH = 4
PW = (2, 4, 8, 16)
GRID_W = 64
MH = 4
MD = 256
MKT = MD // P
D_ML = MH * MD
MB = D_ML // P
O_U, O_V, O_P, O_Q, O_O, O_K, O_VM, O_G = 0, 512, 1024, 1536, 2560, 3584, 4608, 5632
W2_TILES = O_G // CW
W2_ORDER = (0, 1, 2, 3, 4, 7, 8, 9, 10, 5, 6)
W2_HEAD = 3
CTX_TILES = 2 * D_ML // CW
NG = 16
VA = MD + 1
NKEY = 128
PH = 8
TOPK = 16
SLOTS = PH * TOPK
GATH = 8
GROUPS = 4
GH = PH // GROUPS
GSTEP = SLOTS // GROUPS
LOWEST = -3.0e38
ADA_TILES = 6 * D // CW
ADA_STEP = 2
OUT_TILES = D // CW
FF_FIRST = "gggg" + "uauauaua" + "aaaa"
FF_STEP = "gggg" + "uauauaua" + "dadadaad"
FF_LAST = "aad" * 4

S_IN = 0
S_OUT = S_IN + W_IN_TILES * CPT
S_FFN = S_OUT + OUT_TILES * CPT
S_STEP = S_FFN + len(FF_FIRST)
S_LAST = S_STEP + (FT - 1) * len(FF_STEP)
S_CTX = S_LAST + len(FF_LAST)
S_IN2 = S_CTX + CTX_TILES * CPT
S_OUT2 = S_IN2 + W2_TILES * CPT
S_WQ = S_OUT2 + OUT_TILES * CPT
NCH = S_WQ + OUT_TILES * CPT

Q_IN = 0
Q_OUT = Q_IN + W_IN_TILES
Q_FFN = Q_OUT + OUT_TILES
Q_CTX = Q_FFN + 2 * FT
Q_IN2 = Q_CTX + CTX_TILES
Q_OUT2 = Q_IN2 + W2_TILES
Q_WQ = Q_OUT2 + OUT_TILES

COL, NCOL = {}, 0
for _name, _w in (("ln1", KT), ("ln2", KT), ("ba", LB), ("bx", LB), ("conv", CONV_W * LB), ("convb", LB), ("lam", LB),
                  ("gnw", HEADS), ("nmix", KT), ("nffn", KT), ("ada_b", 6 * KT), ("qkconv", 3 * 2 * MB), ("mlnorm", MB),
                  ("pscale", len(PW)), ("c", KT), ("cctx", KT), ("sgub", SH), ("bgate", 4), ("xi", HEADS),
                  ("zeta", HEADS), ("sel", 2), ("iota", TOPK)):
    COL[_name] = (NCOL, _w)
    NCOL += _w

C1 = {"wa": 0, "wx": 1024, "decay": 2048, "rope": 3072, "_": 3584}
C2 = {"pool": 0, "sguw": 2048, "poolw": 2560, "keys": 3072, "mask": 3328, "_": 3584}


def pause(slots):
    for _ in range(slots):
        yield


def lin(const, i=None, step=0):
    return const if i is None else i * step + const


def build(nc, a, out):
    with ExitStack() as ctx:
        sems = {}

        def sem(name):
            if name not in sems:
                sems[name] = ctx.enter_context(nc.semaphore(name))
            return sems[name]

        class Chain:

            def __init__(self, eng, name):
                self.eng, self.sem, self.n = eng, sem(name), 0

            def mark(self, ins):
                self.n += 1
                ins.then_inc(self.sem, 1)

            def sync(self):
                self.eng.wait_ge(self.sem, self.n)

            def __call__(self, ins):
                self.mark(ins)
                self.sync()

        region, words = {}, 0
        for name, n in (("ident", P), ("cols", 512), ("modt", 12 * KT), ("small", 512), ("X", NB * D), ("UH", KT * T),
                        ("UL", KT * T), ("RAW", SLOTS_W * D), ("WH", SLOTS_W * D), ("P", 12288),
                        ("TMP", 6176), ("C", 3584), ("MISC", 1120)):
            region[name] = words
            words += n
        arena = ctx.enter_context(nc.sbuf_tensor("arena", [P, words], F32))
        arena_at = nc.lookup_mloc(arena).addr

        def view(name, where, off, shape, dt=F32):
            return nc.alloc_sbuf_tensor_at(name, [P] + shape, dt, offset=arena_at + 4 * (region[where] + off))

        ident = view("ident", "ident", 0, [P])
        cols = view("cols", "cols", 0, [512])
        modt = view("modt", "modt", 0, [6 * KT, 2])
        X = view("X", "X", 0, [NB, D])
        UH = view("UH", "UH", 0, [KT, T], F32R)
        UL = view("UL", "UL", 0, [KT, T], F32R)
        raw = view("raw", "RAW", 0, [SLOTS_W, CK * CW])
        WH = view("WH", "WH", 0, [SLOTS_W, CK * CW], F32R)
        WL = view("WL", "RAW", 0, [SLOTS_W, CK * CW], F32R)
        bank = [ctx.enter_context(nc.psum_tensor(f"bank{i}", [P, CW], F32)) for i in range(8)]
        ACC = [bank[0:2], bank[2:4]]
        DB = bank[4:8]
        ALLB = DB + bank[0:4]

        small_at = [0]

        def tiny(name, shape, dt=F32):
            n = int(np.prod(shape))
            v = view(name, "small", small_at[0], shape, dt)
            small_at[0] += -(-n // 8) * 8
            assert small_at[0] <= 512
            return v

        def col(name, j=0, n=1, rows=P):
            o, w = COL[name]
            assert j + n <= w
            return cols[0:rows, o + j:o + j + n]

        ss = tiny("ss", [NB])
        ms = tiny("ms", [NB])
        rms = tiny("rms", [NB])
        rinv = tiny("rinv", [NB])
        sc_mix = tiny("sc_mix", [2, KT])
        sc_ffn = tiny("sc_ffn", [KT])
        csil = tiny("csil", [KT, 2])
        lam_t = [tiny(f"lam_t{i}", [LB]) for i in range(5)]
        p_col = tiny("p_col", [LB])
        n_col = tiny("n_col", [LB])
        gn = [tiny(f"gn{i}", [NB * HEADS]) for i in range(3)]

        raw_landed = [sem(f"raw_landed{s}") for s in range(SLOTS_W)]
        hi_ready, lo_ready, split_used = sem("hi_ready"), sem("lo_ready"), sem("split_used")
        acc_free_act, acc_free_dve = sem("acc_free_act"), sem("acc_free_dve")

        Pin = view("Pin", "P", 0, [NB, 6144])
        XN = view("XN", "TMP", 0, [NB, D])
        mod_tmp = view("mod_tmp", "MISC", 0, [2, T])
        wa = view("wa", "C", C1["wa"], [LB, P])
        wx = view("wx", "C", C1["wx"], [LB, P])
        decay = view("decay", "C", C1["decay"], [HEADS, P])
        rope = view("rope", "C", C1["rope"], [NB, 2, P // 2])
        lru_x = view("lru_x", "TMP", 0, [LB, T + CONV_W - 1])
        lru_b = view("lru_b", "TMP", 0, [LB, T])
        lru_u = view("lru_u", "TMP", LB * (T + CONV_W - 1), [LB, T])
        lru_g = view("lru_g", "TMP", LB * (2 * T + CONV_W - 1), [LB, T])
        rt = [view(f"rt{i}", "TMP", 1024 * i, [KT, P // 2]) for i in range(4)]
        ret_s = view("ret_s", "TMP", 0, [HEADS, NB, P])
        ret_kz = view("ret_kz", "TMP", 2048, [HEADS, P])
        ret_r = view("ret_r", "TMP", 3072, [HEADS, P])
        ret_o = view("ret_o", "TMP", 4096, [NB, HEADS, P])
        ret_sq = view("ret_sq", "TMP", 0, [NB, HEADS, P])
        FH = view("FH", "P", 0, [CK, T], F32R)
        FL = view("FL", "P", 1024, [CK, T], F32R)
        ff_g = view("ff_g", "P", 2048, [NB, CW])
        ff = view("ff", "P", 3072, [NB, CW])
        fnw = view("fnw", "P", 4096, [D])
        cond = view("cond", "P", 8192, [KT, P], F32R)
        ada_rows = view("ada_rows", "P", 10240, [ADA_STEP, CW])

        def half(j):
            return lambda b: Pin[:, b // 4, 1024 * j + (b % 4) * T:1024 * j + (b % 4 + 1) * T]

        def wide(j):
            return Pin[:, :, 1024 * j:1024 * (j + 1)]

        pool_t = view("pool_t", "C", C2["pool"], [len(PW), NB, T])
        sgu_w = view("sgu_w", "C", C2["sguw"], [SH, P])
        pool_w = view("pool_w", "C", C2["poolw"], [len(PW), P])
        keys = view("keys", "C", C2["keys"], [2, NKEY])
        mask = view("mask", "C", C2["mask"], [2, P])
        wg = view("wg", "MISC", 776, [KT, NG])
        wg_h = [view("wg_h0", "P", 10768, [KT, NG], F32R), view("wg_h1", "TMP", 5136, [KT, NG], F32R)]
        wg_l = [view("wg_l0", "P", 10768 + KT * NG, [KT, NG], F32R), view("wg_l1", "TMP", 5136 + KT * NG, [KT, NG], F32R)]
        g_row = [view("g_row0", "P", 10768 + 2 * KT * NG, [T]), view("g_row1", "TMP", 5136 + 2 * KT * NG, [T])]
        ctx_x = view("ctx_x", "P", 0, [NB, D])
        ctx_n = view("ctx_n", "P", D * NB, [NB, D])
        kv = view("kv", "P", 0, [NB, 2 * D_ML])
        c_pad = view("c_pad", "P", 4096, [MB, T + 2])
        c_k = view("c_k", "P", 6160, [MB, T])
        c_ktok = view("c_ktok", "P", 8208, [NB, D_ML])
        c_v1 = view("c_v1", "P", 4096, [NB, MH, VA])
        c_rows = [view(f"c_rows{i}", "TMP", 4112 + 512 * i, [2, T]) for i in range(4)] + [view("c_rows4", "P", 10256, [2, T])]
        st = view("st", "TMP", 0, [2, MH, MKT, VA])
        P2 = view("P2", "P", 0, [NB, O_G])
        XN2 = view("XN2", "P", 0, [NB, D])
        l_pad = view("l_pad", "TMP", 4112, [MB, T + 2])
        l_v1 = view("l_v1", "TMP", 4112, [NB, MH, VA])
        pool_d = view("pool_d", "TMP", 4112, [len(PW), T])
        sc_t = view("sc_t", "P", NB * O_G, [MH, NB, P])
        pool_y = view("pool_y", "C", C2["pool"], [len(PW), T])
        sgu_t = view("sgu_t", "C", C2["pool"] + len(PW) * T, [D_SGU // P, T])
        sgu_n = view("sgu_n", "P", NB * O_G, [D_SGU])
        sgu_sq = view("sgu_sq", "P", NB * O_G + D_SGU, [D_SGU])
        ml_t = view("ml_t", "MISC", 0, [2, VA])
        vw = view("vw", "MISC", 0, [2, VA])
        wb = view("wb", "MISC", 520, [2, P])
        gb1 = view("gb1", "TMP", 0, [D])
        gb2 = view("gb2", "TMP", D, [D])
        g_tmp = view("g_tmp", "MISC", 0, [NB, CW])
        sc_row = view("sc_row", "P", 4096, [D])
        sh_row = view("sh_row", "P", 6144, [D])
        q_tok = view("q_tok", "P", 8192, [2, NB, CW])
        q_t = view("q_t", "P", 10240, [2, 2 * GH, T])
        key_s = [view("key_s0", "C", 0, [2 * PH, NKEY]), view("key_s1", "TMP", 0, [2 * PH, NKEY])]
        cand = view("cand", "C", 2048, [GH, TOPK, TOPK])
        hot = view("hot", "C", 2048 + GH * TOPK * TOPK, [GH, TOPK, TOPK])
        top_v = view("top_v", "MISC", 0, [2 * GH, TOPK])
        top_i = view("top_i", "MISC", 64, [2 * GH, TOPK], U32)
        top_f = view("top_f", "MISC", 128, [2 * GH, TOPK])
        best_v = view("best_v", "MISC", 192, [GH, TOPK])
        best_i = view("best_i", "MISC", 224, [GH, TOPK], U32)
        pick_i = view("pick_i", "MISC", 256, [GSTEP], U32)
        pick_f = view("pick_f", "MISC", 288, [GSTEP])
        exp_f = [view(f"exp_f{i}", "MISC", 320 + 32 * i, [GSTEP]) for i in range(2)]
        soft = view("soft", "TMP", 4096, [NB * PH])
        idx = view("idx", "TMP", 4096 + SLOTS, [NB, SLOTS], U32)
        gate_w = view("gate_w", "TMP", 4096 + SLOTS * 3, [NB, SLOTS])
        dots = view("dots", "TMP", 4096 + SLOTS * 5, [NB, SLOTS])
        step_dots = view("step_dots", "TMP", 4096 + SLOTS * 7, [GSTEP])
        step_idx = view("step_idx", "TMP", 4096 + SLOTS * 8, [GSTEP // GATH, GATH], U32)
        v_sum = view("v_sum", "P", 8192, [2, D])
        nfin = view("nfin", "TMP", 0, [D])
        rows_g = view("rows_g", "RAW", 0, [GATH, D])
        m_st = tiny("m_st", [2, 2 * NB + 1])
        n_ml = tiny("n_ml", [2, NB])
        dcy = tiny("dcy", [2, NB])
        co = tiny("co", [5, 2, NB, MH])
        den = tiny("den", [2])
        l_ms = [tiny(f"l_ms{i}", [NB * MH]) for i in range(3)]

        def lat_half(o):
            return lambda b: P2[:, b // 4, o + (b % 4) * T:o + (b % 4 + 1) * T]

        l_rows = [P2[0:MH, 0, 512 * i:512 * (i + 1)].rearrange("p (d t) -> p d t", d=2) for i in range(3)] + \
                 [P2[0:MH, 1, 512 * i:512 * (i + 1)].rearrange("p (d t) -> p d t", d=2) for i in range(3)]

        class Stream:

            def __init__(self, s):
                self.s, self.lat = s, s == 1
                v = (c_pad, c_k, c_ktok, c_v1)
                if not self.lat:
                    self.pad, self.v1 = c_pad, c_v1
                    self.kT = lambda b: c_k[:, b, :]
                    self.k_raw = lambda n, b: kv[:, n, b * P:(b + 1) * P]
                    self.k_tok = lambda n, o, w: c_ktok[:, n, o:o + w]
                    self.v = lambda n: kv[:, n, D_ML:2 * D_ML]
                    r = [x[0:MH, :, :] for x in c_rows]
                    self.A, self.lf, self.b, self.M, self.wk = r
                else:
                    self.pad, self.v1 = l_pad, l_v1
                    self.kT = lat_half(O_K)
                    self.k_raw = lambda n, b: P2[:, n, O_K + b * P:O_K + (b + 1) * P]
                    self.k_tok = lambda n, o, w: P2[:, n, O_VM + o:O_VM + o + w]
                    self.v = lambda n: P2[:, n, O_VM:O_VM + D_ML]
                    self.A, self.lf, self.b, self.M, self.wk, self.ex = l_rows
                self.steps = [(step, d, step if d == 0 else NB - 1 - step) for step in range(NB) for d in range(2)]

        streams = [Stream(0), Stream(1)]

        norm_of = ((X, XN), (X, XN), (X, XN), (ctx_x, ctx_n), (X, XN2), (X, XN2))

        def span(n):
            return slice(n * P, (n + 1) * P)

        def scan_ap(x, d, n):
            r = x[:, d, n * P:(n + 1) * P]
            return r if d == 0 else r[:, ::-1]

        def last_of(x, d, n):
            t = (n + 1) * P - 1 if d == 0 else n * P
            return x[:, d, t:t + 1]

        def hdim(x):
            return x[:, :].unsqueeze(2)

        block = ctx.enter_context(nc.Block())

        @block.sync
        def _(sp):
            sp.dma_start(X[:, :, :], a["x"].rearrange("o (b p) d -> p (o b) d", p=P)).then_inc(sem("x_landed"), 16)
            sp.dma_start(cols[:, 0:NCOL], a["cols"]).then_inc(sem("cols_landed"), 16)
            sp.dma_start(ident[:, :], a["ident"]).then_inc(sem("ident_landed"), 16)

            def load_chunk(c, s):
                sp.dma_start(raw[:, s, :], a["wstream"][c]).then_inc(raw_landed[s], 16)

            for s in range(SLOTS_W):
                load_chunk(s, s)
            with sp.Fori(1, NCH // SLOTS_W) as i:
                for s in range(SLOTS_W):
                    sp.wait_ge(split_used, lin(s + 1 - SLOTS_W, i, SLOTS_W))
                    load_chunk(lin(s, i, SLOTS_W), s)

            sp.wait_ge(sem("out_ready"), NB)
            sp.dma_start(out.rearrange("o (b p) d -> p (o b) d", p=P), X[:, :, :]).then_inc(sem("out_stored"), 16)
            sp.wait_ge(sem("out_stored"), 16)

        @block.gpsimd
        def _(pool):
            pool.wait_ge(sem("x_landed"), 16)
            pool.dma_start(wa[:, :, :], a["wa"]).then_inc(sem("gates_landed"), 16)
            pool.dma_start(wx[:, :, :], a["wx"]).then_inc(sem("gates_landed"), 16)
            pool.dma_start(decay[:, :, :], a["decay"]).then_inc(sem("decay_landed"), 16)
            pool.dma_start(rope[:, :, :, :], a["rope"]).then_inc(sem("rope_landed"), 16)
            pool.wait_ge(sem("y1_ready"), 2 * LB)
            for dst, name in ((pool_t, "pool_t"), (sgu_w, "sgu_w"), (pool_w, "pool_w"), (keys, "keys"), (mask, "mask"),
                              (wg, "wg")):
                pool.dma_start(dst[tuple(slice(None) for _ in dst.shape)], a[name]).then_inc(sem("tables_landed"), 16)
            pool.dma_start(fnw[:, :], a["fnw"].partition_broadcast(P)).then_inc(sem("fnw_landed"), 16)
            pool.wait_ge(sem("x2_ready"), 1)
            pool.dma_start(ctx_x[:, :, :], a["ctx"].rearrange("o (b p) d -> p (o b) d", p=P)).then_inc(
                sem("ctx_landed"), 16)
            pool.wait_ge(sem("ctx_done"), 1)
            pool.dma_start(sgu_n[:, :], a["sgu_n"].partition_broadcast(P)).then_inc(sem("sgu_n_landed"), 16)
            for table, g0, b in (("u_tab", 0, 0), ("u_tab", SLOTS, 1), ("v_tab", 2 * SLOTS, 0), ("v_tab", 3 * SLOTS, 1)):
                with pool.Fori(0, GROUPS) as i:
                    if g0 < 2 * SLOTS:
                        pool.wait_ge(sem("idx_ready"), lin(b * GROUPS + 1, i, 1))
                        pool.sem_inc(sem("gathers"), 1)
                    for s in range(GSTEP):
                        if s % GATH == 0:
                            pool.tensor_copy(step_idx[:, s // GATH, :], idx[:, b, bass.ds(lin(s, i, GSTEP), GATH)]).then_inc(
                                sem("step_idx_ready"), 1)
                            pool.wait_ge(sem("step_idx_ready"), lin(g0 // GATH + s // GATH + 1, i, GSTEP // GATH))
                        pool.wait_ge(sem("row_used"), lin(g0 + s + 1, i, GSTEP))
                        pool.sem_inc(sem("gathers"), 1)
                        pool.indirect_dma_start(
                            out=rows_g[:, s % GATH, :], out_offset=None, in_=a[table],
                            in_offset=bass.IndirectOffsetOnAxis(ap=step_idx[:, s // GATH, s % GATH:s % GATH + 1], axis=0),
                        ).then_inc(sem(f"row_landed{s % GATH}"), 16)

        @block.tensor
        def _(pe):
            def products(n, banks, k0, nk, i, per, ah, al, blocks=NB, first=True, last=True):
                pe.wait_ge(lo_ready, lin(n + 1, i, per))
                wh, wl = WH[:, n % SLOTS_W, :], WL[:, n % SLOTS_W, :]
                for k in range(nk):
                    w = slice(k * CW, (k + 1) * CW)
                    for b in range(blocks):
                        t = slice(b * P, (b + 1) * P)
                        o = banks[b][:, :]
                        pe.matmul(o, ah[:, k0 + k, t], wh[:, w], start=first and k == 0, stop=False)
                        mm = pe.matmul(o, ah[:, k0 + k, t], wl[:, w], start=False,
                                       stop=al is None and last and k == nk - 1)
                        if al is not None:
                            mm = pe.matmul(o, al[:, k0 + k, t], wh[:, w], start=False, stop=last and k == nk - 1)
                mm.then_inc(split_used, 1)

            def tile(n, q, par, i=None, per=0, qper=0, work=iter(())):
                pe.wait_ge(acc_free_act, lin(q + 1, i, qper))
                pe.wait_ge(acc_free_dve, lin(q + 1, i, qper))
                for m in range(CPT):
                    products(n + m, ACC[par], m * CK, CK, i, per, UH, UL, first=m == 0, last=m == CPT - 1)
                    next(work, None)

            def linear_among(n0, q0, t0, tiles, work):
                for t in range(t0, tiles):
                    tile(n0 + CPT * t, q0 + t, (q0 + t) % 2, work=work)
                for _ in work:
                    pass

            def linear(n0, q0, tiles):
                with pe.Fori(0, tiles // 2) as i:
                    for par in range(2):
                        tile(n0 + CPT * par, q0 + par, (q0 + par) % 2, i, 2 * CPT, 2)
                if tiles % 2:
                    tile(n0 + CPT * (tiles - 1), q0 + tiles - 1, (q0 + tiles - 1) % 2)

            def turn(src, banks, name, wait=None, per_bank=4):
                for j, bk in enumerate(banks):
                    if wait:
                        wait(j)
                    for m in range(per_bank):
                        mm = pe.transpose(bk[:, m * P:(m + 1) * P], src(j, m), ident[:, :])
                    mm.then_inc(sem(name), 1)

            def norm_turned(rows, call, xn):
                pe.wait_ge(sem("xn_ready"), NB * (rows + 1))
                turn(lambda j, m: xn[:, m % 2, (2 * j + m // 2) * P:(2 * j + m // 2 + 1) * P], ALLB, "xn_turned")

            def u_ready(call):
                pe.wait_ge(sem("u_ready"), KT * (call + 1))

            pe.wait_ge(sem("ident_landed"), 16)
            norm_turned(0, 0, XN)
            u_ready(0)
            linear(S_IN, Q_IN, W_IN_HEAD)

            def lru():
                pe.wait_ge(acc_free_act, Q_IN + W_IN_HEAD + 2)
                pe.wait_ge(acc_free_dve, Q_IN + W_IN_HEAD + 2)
                turn(lambda j, m: Pin[:, m % 2, (2 * j + m // 2) * P:(2 * j + m // 2 + 1) * P], DB, "lru_x_turned")
                yield from pause(9)
                pe.wait_ge(acc_free_act, Q_IN + 4 + 2)
                pe.wait_ge(acc_free_dve, Q_IN + 4 + 2)
                pe.wait_ge(sem("lru_x_ready"), 4)
                turn(lambda j, m: Pin[:, m % 2, 1024 + (2 * j + m // 2) * P:1024 + (2 * j + m // 2 + 1) * P], DB,
                     "lru_g_turned")
                yield from pause(4)
                pe.wait_ge(sem("gates_landed"), 32)
                pe.wait_ge(sem("lru_u_ready"), 1)
                pe.wait_ge(sem("lru_g_ready"), 4)
                for w in (wa, wx):
                    for b in range(LB):
                        mm = pe.matmul(DB[b // 2][:, (b % 2) * T:(b % 2 + 1) * T], w[:, b, :], lru_u[:, b, :], start=True,
                                       stop=True)
                        mm.then_inc(sem("lru_gate_ps"), 1)
                    if w is wa:
                        yield from pause(5)
                        pe.wait_ge(sem("lru_gates_ready"), LB)

            linear_among(S_IN, Q_IN, W_IN_HEAD, W_IN_TILES, lru())

            pe.wait_ge(acc_free_act, Q_OUT + 2)
            pe.wait_ge(acc_free_dve, Q_OUT + 2)
            pe.wait_ge(sem("lru_gates_ready"), 2 * LB)
            pe.wait_ge(sem("rope_ready"), NB)
            for t0, banks in ((C_Q, DB), (C_Q + 1024, bank[0:4])):
                turn(lambda j, m: Pin[:, m % 2, t0 + (2 * j + m // 2) * P:t0 + (2 * j + m // 2 + 1) * P], banks,
                     "qk_turned")
            pe.wait_ge(sem("qk_ready"), 8)
            qT, kT = half(0), half(1)
            for h in range(HEADS):
                for n in range(NB):
                    t = slice(n * P, (n + 1) * P)
                    mm = pe.matmul(DB[h // 2][:, ((h % 2) * 2 + n) * P:((h % 2) * 2 + n + 1) * P], kT(h)[:, t], qT(h)[:, t],
                                   start=True, stop=True)
                if h % 2:
                    mm.then_inc(sem("ret_scores"), 1)
            for h in range(HEADS):
                pe.wait_ge(sem("ret_s_ready"), h // 2 + 1)
                for n in range(NB):
                    mm = pe.matmul(bank[2 * n + h // 4][:, (h % 4) * P:(h % 4 + 1) * P], ret_s[:, h, n, :],
                                   Pin[:, n, C_V + h * P:C_V + (h + 1) * P], start=True, stop=True)
            mm.then_inc(sem("ret_inner"), 1)
            pe.wait_ge(sem("ret_kz_ready"), 1)
            for h in range(HEADS):
                mm = pe.matmul(DB[h // 4][:, (h % 4) * P:(h % 4 + 1) * P], ret_kz[:, h, :],
                               Pin[:, 0, C_V + h * P:C_V + (h + 1) * P], start=True, stop=True)
            mm.then_inc(sem("ret_kv"), 1)
            pe.wait_ge(sem("ret_r_ready"), 2)
            for h in range(HEADS):
                mm = pe.matmul(DB[2 + h // 4][:, (h % 4) * P:(h % 4 + 1) * P], qT(h)[:, P:T], ret_r[:, h, :],
                               start=True, stop=True)
            mm.then_inc(sem("ret_cross"), 1)
            pe.wait_ge(sem("ret_o_ready"), 1)
            turn(lambda j, m: ret_o[:, m % 2, 2 * j + m // 2, :], bank[0:4], "ret_turned")
            pe.wait_ge(sem("y1_ready"), 2 * LB)
            linear(S_OUT, Q_OUT, OUT_TILES)

            norm_turned(1, 1, XN)
            u_ready(1)

            def step(kinds, n, i=None, tile=0, down=0):
                m = dict.fromkeys(kinds, 0)
                for p, kind in enumerate(kinds):
                    at, k = n + p, m[kind]
                    m[kind] += 1
                    if k == 0 and kind in "gu":
                        q = Q_FFN + 2 * tile + "gu".index(kind)
                        pe.wait_ge(acc_free_act, lin(q + 1, i, 2))
                        pe.wait_ge(acc_free_dve, lin(q + 1, i, 2))
                    if kind == "g":
                        if k == 0 and tile:
                            pe.wait_ge(sem("mod_ready"), lin(ADA_STEP * tile, i, ADA_STEP))
                        products(at, ACC[0], k * CK, CK, i, len(FF_STEP), UH, UL, first=k == 0, last=k == CPT - 1)
                    elif kind == "u":
                        if k == 0 and tile:
                            pe.wait_ge(sem("ffT_ready"), lin(CK * tile, i, CK))
                        products(at, ACC[1], k * CK, CK, i, len(FF_STEP), UH, UL, first=k == 0, last=k == CPT - 1)
                    elif kind == "a":
                        if k == 0:
                            pe.wait_ge(acc_free_act, lin(Q_FFN + 4 + 2 * min(tile, FT - 1), i, 2))
                            if tile == FT:
                                pe.wait_ge(sem("mod_ready"), ADA_STEP * FT)
                        r = k % CPT
                        products(at, [ACC[0][k // CPT]], r * CK, CK, i, len(FF_STEP), cond, None, blocks=1, first=r == 0,
                                 last=r == CPT - 1)
                    else:
                        if k == 0:
                            pe.wait_ge(sem("ffT_ready"), lin(CK * (down + 1), i, CK))
                        pe.wait_ge(sem("down_added"), lin(2 + OUT_TILES * down + k - 1, i, OUT_TILES))
                        products(at, DB[2 * (k % 2):2 * (k % 2) + 2], 0, CK, i, len(FF_STEP), FH, FL)

            def turn_ff(i=None, nth=0):
                pe.wait_ge(sem("ff_ready"), lin(nth + 1, i, 1))
                for j in range(2):
                    for m in range(4):
                        k = 2 * j + m // 2
                        mm = pe.transpose(bank[2 + j][:, m * P:(m + 1) * P], ff[:, m % 2, k * P:(k + 1) * P], ident[:, :])
                mm.then_inc(sem("ff_turned"), 1)

            def ada_turned(i=None, nth=0):
                for t in range(ADA_STEP):
                    pe.wait_ge(sem("ada_rows_ready"), lin(ADA_STEP * nth + t + 1, i, ADA_STEP))
                    for j in range(CW // P):
                        mm = pe.matmul(ACC[0][t][:, 2 * j:2 * j + 2], ada_rows[0:4, t, j * P:(j + 1) * P],
                                       col("sel", 0, 2, rows=4), start=True, stop=True)
                    mm.then_inc(sem("ada_cols"), 1)

            pe.wait_ge(sem("cond_ready"), 1)
            step(FF_FIRST, S_FFN)
            turn_ff()
            ada_turned()
            with pe.Fori(0, FT - 1) as i:
                step(FF_STEP, S_STEP, i, tile=1)
                ada_turned(i, 1)
                turn_ff(i, 1)
            step(FF_LAST, S_LAST, tile=FT, down=FT - 1)
            ada_turned(nth=FT)

            def gates(s):
                pe.wait_ge(sem("wg_ready"), s + 1)
                for k in range(KT):
                    for j, (part, w) in enumerate(((UH, wg_h), (UH, wg_l), (UL, wg_h))):
                        mm = pe.matmul(DB[2][0:NG, 0:T], w[s][:, k, :], part[:, k, :], start=j == 0 and k == 0,
                                       stop=j == 2 and k == KT - 1)
                mm.then_inc(sem("gate_ps"), 1)

            def gate_rows(s):
                pe.wait_ge(sem("g_row_ready"), s + 1)
                for typ in range(2):
                    for d in range(2):
                        g0 = (2 * d + typ) * MH
                        mm = pe.matmul(DB[2 + typ][0:MH, d * T:(d + 1) * T], ident[0:NG, g0:g0 + MH], g_row[s][0:NG, :],
                                       start=True, stop=True)
                mm.then_inc(sem("gate_rows_ps"), 1)

            def keys_turned(S, banks):
                turn(lambda j, m: S.k_raw(m % 2, 2 * j + m // 2), banks, "k_turned")

            def keys_back(S, banks):
                pe.wait_ge(sem("k_silu"), S.s + 1)
                for j in range(4):
                    for m in range(4):
                        mm = pe.transpose(banks[j][:, m * P:(m + 1) * P], S.kT(4 * (j % 2) + m)[:, span(j // 2)], ident[:, :])
                    mm.then_inc(sem("k_back"), 1)

            def columns(S):
                pe.wait_ge(sem("rows_ready"), S.s + 1)
                kinds = [S.A, S.wk, S.lf, S.ex] if S.lat else [None, S.wk]
                for kind, row in enumerate(kinds):
                    for d in range(2):
                        for n in range(NB):
                            o = ((kind * 2 + d) * NB + n) * MH
                            if row is not None:
                                pe.matmul(DB[2][:, o:o + MH], row[:, d, span(n)], ident[0:MH, 0:MH], start=True, stop=True)
                for d in range(2):
                    for n in range(NB):
                        o = ((4 * 2 + d) * NB + n) * MH
                        mm = pe.matmul(DB[2][:, o:o + MH], dcy[0:MH, d, n:n + 1].to_broadcast([MH, P]), ident[0:MH, 0:MH],
                                       start=True, stop=True)
                mm.then_inc(sem("cols_ps"), 1)

            upd = [0]

            def update(S, n):
                for h in range(MH):
                    u = upd[0] * MH + h
                    pe.wait_ge(sem("vw_ready"), u + 1)
                    if u >= MH:
                        pe.wait_ge(sem("state_ready"), u + 1 - MH)
                    for kt in range(MKT):
                        mm = pe.matmul(ALLB[2 * h + kt][:, 0:VA], S.k_tok(n, h * MD + kt * P, P), vw[:, h % 2, :], start=True,
                                       stop=True)
                    mm.then_inc(sem("state_ps"), 1)
                upd[0] += 1

            def updated():
                pe.wait_ge(sem("state_ready"), upd[0] * MH)

            pe.wait_ge(sem("down_added"), 2 + FT * OUT_TILES)
            norm_turned(3, 2, ctx_n)
            u_ready(2)
            def context():
                gates(0)
                yield from pause(2)
                gate_rows(0)
                yield from pause(7)
                pe.wait_ge(acc_free_act, Q_CTX + CTX_TILES // 2 + 2)
                pe.wait_ge(acc_free_dve, Q_CTX + CTX_TILES // 2 + 2)
                pe.wait_ge(sem("gate_rows_kept"), 1)
                keys_turned(streams[0], DB)
                yield from pause(7)
                keys_back(streams[0], DB)

            linear_among(S_CTX, Q_CTX, 0, CTX_TILES, context())
            pe.wait_ge(acc_free_act, Q_IN2 + 2)
            pe.wait_ge(acc_free_dve, Q_IN2 + 2)
            pe.wait_ge(sem("k_tok_ready"), 4)
            columns(streams[0])
            pe.wait_ge(sem("co_ready"), 1)
            for step, d, n in streams[0].steps:
                update(streams[0], n)
            updated()

            norm_turned(4, 3, XN2)
            u_ready(3)
            linear(S_IN2, Q_IN2, W2_HEAD)
            L = streams[1]

            def rows_kept(tiles):
                pe.wait_ge(acc_free_act, Q_IN2 + tiles + 2)
                pe.wait_ge(acc_free_dve, Q_IN2 + tiles + 2)

            def mixers():
                gates(1)
                yield
                rows_kept(W2_HEAD)
                for g in range(len(PW)):
                    for b in range(NB):
                        mm = pe.matmul(DB[g // 2][:, (g % 2) * T:(g % 2 + 1) * T], P2[:, b, O_P + g * P:O_P + (g + 1) * P],
                                       pool_t[:, g, b, :], start=b == 0, stop=b == NB - 1)
                    mm.then_inc(sem("pool_ps"), 1)
                yield from pause(2)
                pe.wait_ge(sem("g_row_ready"), 2)
                for g in range(len(PW)):
                    pe.wait_ge(sem("pool_d_ready"), g + 1)
                    mm = pe.matmul(DB[2 + g // 2][:, (g % 2) * T:(g % 2 + 1) * T], pool_w[:, g, :], pool_d[:, g, :],
                                   start=True, stop=True)
                    mm.then_inc(sem("pool_y_ps"), 1)
                yield
                pe.wait_ge(sem("sgu_v_ready"), 1)
                for n in range(NB):
                    for h in range(SH):
                        mm = pe.matmul(DB[n][:, h * P:(h + 1) * P], sgu_w[:, h, :], P2[:, n, O_V + h * P:O_V + (h + 1) * P],
                                       start=True, stop=True)
                mm.then_inc(sem("sgu_ps"), 1)
                yield from pause(3)
                pe.wait_ge(sem("sgu_y_ready"), 1)
                turn(lambda j, m: P2[:, m % 2, O_U + (2 * j + m // 2) * P:O_U + (2 * j + m // 2 + 1) * P], DB[0:2],
                     "sgu_turned")
                yield
                pe.wait_ge(sem("pool_y_kept"), len(PW))
                gate_rows(1)
                yield from pause(2)
                rows_kept(5)
                pe.wait_ge(sem("sgu_t_kept"), 4)
                pe.wait_ge(sem("gate_rows_kept"), 2)
                turn(lambda j, m: P2[:, m % 2, O_Q + (2 * j + m // 2) * P:O_Q + (2 * j + m // 2 + 1) * P], DB, "q_turned")
                yield from pause(7)
                rows_kept(7)
                pe.wait_ge(sem("q_pad_ready"), 4)
                keys_turned(L, DB)
                yield from pause(9)
                keys_back(L, DB)
                yield from pause(2)
                pe.wait_ge(sem("q_silu"), 1)
                pe.wait_ge(sem("k_tok_ready"), 8)
                for h in range(MH):
                    for n in range(NB):
                        for kt in range(MKT):
                            mm = pe.matmul(DB[h // 2][:, ((h % 2) * NB + n) * P:((h % 2) * NB + n + 1) * P],
                                           L.kT(MKT * h + kt)[:, span(n)], lat_half(O_Q)(MKT * h + kt)[:, span(n)],
                                           start=kt == 0, stop=kt == MKT - 1)
                mm.then_inc(sem("ml_scores"), 1)
                yield
                columns(L)

            linear_among(S_IN2, Q_IN2, W2_HEAD, W2_TILES, mixers())
            rows_kept(W2_TILES)
            pe.wait_ge(sem("co_ready"), 2)
            pe.wait_ge(sem("sc_t_ready"), 1)
            x = 0
            for step, d, n in L.steps:
                def weights(h):
                    pe.matmul(DB[h % 2][:, 0:P], ident[0:MH, h:h + 1].to_broadcast([MH, P]), L.b[:, d, span(n)], start=True,
                              stop=False)
                    pe.matmul(DB[h % 2][:, 0:P], ident[:, :], mask[:, d, :], start=False, stop=True).then_inc(
                        sem("arg_ps"), 1)
                weights(0)
                for h in range(MH):
                    if h + 1 < MH:
                        if h >= 1:
                            pe.wait_ge(sem("w_exp"), x + h)
                        weights(h + 1)
                    if x + h >= 2:
                        pe.wait_ge(sem("h_ready"), x + h - 1)
                    for kt in range(MKT):
                        pe.matmul(ACC[h % 2][1][:, 0:VA], lat_half(O_Q)(MKT * h + kt)[:, span(n)], st[:, d, h, kt, :],
                                  start=kt == 0, stop=kt == MKT - 1)
                    pe.wait_ge(sem("w_ready"), x + h + 1)
                    pe.matmul(ACC[h % 2][0][:, 0:VA], wb[:, h % 2, :], L.v1[:, n, h, :], start=True, stop=True).then_inc(
                        sem("num_ps"), 1)
                x += MH
                pe.wait_ge(sem("w_exp"), x)
                if step == 0:
                    pe.wait_ge(sem("h_ready"), x)
                    update(L, n)
                    updated()
            pe.wait_ge(sem("ml_y_ready"), 1)
            turn(lambda j, m: P2[:, m % 2, O_K + (2 * j + m // 2) * P:O_K + (2 * j + m // 2 + 1) * P], DB, "ml_turned")
            def spread(column):
                for j in range(4):
                    for m in range(4):
                        mm = pe.matmul(DB[j][:, m * P:(m + 1) * P], column(4 * j + m).to_broadcast([P, P]), ident[:, :],
                                       start=True, stop=True)
                    mm.then_inc(sem("spread_ps"), 1)

            pe.wait_ge(sem("y2_ready"), KT)
            spread(lambda k: modt[:, 2 * KT + k, 0:1])
            pe.wait_ge(sem("spread_ready"), 4)
            spread(lambda k: modt[:, 5 * KT + k, 0:1])
            linear(S_OUT2, Q_OUT2, OUT_TILES)

            pe.wait_ge(sem("spread_ready"), 8)
            norm_turned(5, 4, XN2)
            u_ready(4)
            spread(lambda k: sc_ffn[:, k:k + 1])
            pe.wait_ge(sem("spread_ready"), 12)
            spread(lambda k: modt[:, 3 * KT + k, 0:1])

            def queries():
                pe.wait_ge(sem("spread_ready"), 16)
                yield from pause(5)
                for t in range(OUT_TILES):
                    pe.wait_ge(acc_free_act, Q_WQ + t + 3)
                    pe.wait_ge(acc_free_dve, Q_WQ + t + 3)
                    turn(lambda j, m: q_tok[:, t % 2, m % 2, (2 * j + m // 2) * P:(2 * j + m // 2 + 1) * P], DB[0:2], "pq_turned")
                    yield from pause(2)
                    pe.wait_ge(sem("q_t_ready"), 2 * (t + 1))
                    if t:
                        pe.wait_ge(sem("key_s_ready"), 2 * t)
                    for b in range(NB):
                        for hp in range(2 * GH):
                            mm = pe.matmul(DB[2 + b][:, hp * NKEY:(hp + 1) * NKEY], q_t[:, t % 2, hp, span(b)],
                                           keys[:, hp % 2, :], start=True, stop=True)
                        mm.then_inc(sem("key_ps"), 1)
                    yield from pause(2)

            linear_among(S_WQ, Q_WQ, 0, OUT_TILES, queries())

        @block.scalar
        def _(act):
            chain = Chain(act, "act_chain")

            def hi(n, i=None, per=0):
                if i is None and n >= NCH:
                    return
                act.wait_ge(raw_landed[n % SLOTS_W], lin(16 * (n // SLOTS_W + 1), i, 16 * per // SLOTS_W))
                act.activation(WH[:, n % SLOTS_W, :], raw[:, n % SLOTS_W, :], ACT.Copy).then_inc(hi_ready, 1)

            def tile(n, evacuate, i=None, per=0, work=iter(())):
                for m in range(CPT):
                    hi(n + LEAD + m, i, per)
                    next(work, None)
                act.wait_ge(split_used, lin(n + CPT, i, per))
                evacuate()

            def linear(n0, q0, tiles, evacuate):
                pairs = tiles // 2
                last = n0 + tiles * CPT == NCH
                with act.Fori(0, pairs - last) as i:
                    for par in range(2):
                        tile(n0 + CPT * par, lambda: evacuate((q0 + par) % 2, lin(par, i, 2)), i, 2 * CPT)
                for t in range(2 * (pairs - last), tiles):
                    tile(n0 + CPT * t, lambda: evacuate((q0 + t) % 2, t))

            def linear_among(n0, q0, t0, tiles, evacuate, work):
                for t in range(t0, tiles):
                    tile(n0 + CPT * t, lambda: evacuate((q0 + t) % 2, t), work=work)
                for _ in work:
                    pass

            def to(dst, width):
                def evacuate(par, t):
                    act.activation(dst(t), ACC[par][0][:, 0:width], ACT.Copy).then_inc(acc_free_act, 1)
                return evacuate

            def nothing(par, t):
                act.sem_inc(acc_free_act, 1)

            def norm_rows(call):
                x, xn = norm_of[call]
                act.wait_ge(sem("norm_begins"), call + 1)
                act.activation(xn[:, 1, :], x[:, 1, :], ACT.Square, accum_out=ss[:, 1:2]).then_inc(sem("ss_ready"), 1)
                act.wait_ge(sem("ms_ready"), call + 1)
                act.activation(rms[:, :], ms[:, :], ACT.Sqrt).then_inc(sem("rms_ready"), 1)
                act.wait_ge(sem("rinv_ready"), call + 1)
                act.activation(xn[:, 1, :], x[:, 1, :], ACT.Copy, scale=rinv[:, 1:2]).then_inc(sem("xn_ready"), 1)

            def norm_turned(rows, call, scale, bias=None, normed=False):
                if not normed:
                    norm_rows(rows)
                for j in range(8):
                    act.wait_ge(sem("xn_turned"), 8 * call + j + 1)
                    for m in range(2):
                        k = 2 * j + m
                        src = ALLB[j][:, m * T:(m + 1) * T]
                        if bias is None:
                            ins = act.activation(UH[:, k, :], src, ACT.Copy, scale=scale(k))
                        else:
                            ins = act.activation(UH[:, k, :], src, ACT.Identity, scale=scale(k), bias=bias(k))
                        ins.then_inc(sem("uh_ready"), 1)

            act.wait_ge(sem("cols_landed"), 16)
            for r, name in enumerate(("c", "cctx")):
                chain.mark(act.activation(csil[:, :, r], col(name, 0, KT), ACT.Silu))
            chain.sync()
            act.wait_ge(sem("lam_abs"), 1)
            act.activation(lam_t[1][:, :], lam_t[0][:, :], ACT.Exp, scale=-1.0).then_inc(sem("lam_exp"), 1)
            for m in range(LEAD):
                hi(m)
            act.sem_inc(acc_free_act, 2)

            norm_turned(0, 0, lambda k: col("ln1", k))
            to_pin = to(lambda t: Pin[:, 0, bass.ds(t * CW, CW)], CW)
            linear(S_IN, Q_IN, W_IN_HEAD, to_pin)

            def lru():
                yield
                for j in range(4):
                    act.wait_ge(sem("lru_x_turned"), j + 1)
                    act.activation(lru_x[:, 2 * j:2 * j + 2, CONV_W - 1:],
                                   DB[j][:, :].rearrange("p (b t) -> p b t", t=T), ACT.Copy).then_inc(sem("lru_x_ready"), 1)
                yield from pause(9)
                for j in range(4):
                    act.wait_ge(sem("lru_g_turned"), j + 1)
                    act.activation(lru_g[:, 2 * j:2 * j + 2, :], DB[j][:, :].rearrange("p (b t) -> p b t", t=T),
                                   ACT.Gelu_apprx_tanh).then_inc(sem("lru_g_ready"), 1)
                yield from pause(4)
                rg, ig = half(0), half(1)
                for name, dst, w in (("ba", rg, 0), ("bx", ig, LB)):
                    for b in range(LB):
                        act.wait_ge(sem("lru_gate_ps"), w + b // 2 * 2 + 2)
                        act.activation(dst(b), DB[b // 2][:, (b % 2) * T:(b % 2 + 1) * T], ACT.Sigmoid,
                                       bias=col(name, b)).then_inc(sem("lru_gates_ready"), 1)
                        if b == LB // 2 - 1:
                            yield
                    yield from pause(4 if name == "ba" else 1)
                act.wait_ge(sem("lru_gates_ready"), 2 * LB)
                act.wait_ge(sem("lam_ready"), 1)
                for b in range(LB):
                    act.activation(lru_b[:, b, :], rg(b), ACT.Tanh, scale=p_col[:, b:b + 1]).then_inc(sem("lru_tanh"), 1)
                    if b == LB // 2 - 1:
                        yield
                yield
                for b in range(LB):
                    act.activation(rg(b), rg(b), ACT.Exp, scale=n_col[:, b:b + 1]).then_inc(sem("lru_a_ready"), 1)
                    if b == LB // 2 - 1:
                        yield
                yield from pause(3)
                act.wait_ge(sem("lru_sq_ready"), 1)
                act.activation(lru_b[:, :, :], lru_b[:, :, :], ACT.Sqrt).then_inc(sem("lru_root"), 1)

            linear_among(S_IN, Q_IN, W_IN_HEAD, W_IN_TILES, to_pin, lru())
            act.wait_ge(sem("lru_y_ready"), 1)
            act.activation(UH[:, 0:LB, :], lru_g[:, :, :], ACT.Copy).then_inc(sem("lru_yh_ready"), 1)

            for j in range(8):
                act.wait_ge(sem("qk_turned"), j + 1)
                qk = half(j // 4)
                for m in range(2):
                    ins = act.activation(qk(2 * (j % 4) + m), (DB if j < 4 else bank[0:4])[j % 4][:, m * T:(m + 1) * T],
                                         ACT.Copy)
                ins.then_inc(sem("qk_ready"), 1)
            act.wait_ge(sem("ret_kv"), 1)
            for j in range(2):
                act.activation(ret_r[:, 4 * j:4 * j + 4, :], DB[j][:, :].rearrange("p (h e) -> p h e", e=P),
                               ACT.Copy).then_inc(sem("ret_r_ready"), 1)
            act.activation(Pin[:, :, C_G:C_G + 1024], Pin[:, :, C_G:C_G + 1024], ACT.Silu).then_inc(sem("ret_gate"), 1)
            act.wait_ge(sem("gn_var"), 1)
            act.activation(gn[1][:, :], gn[0][:, :], ACT.Sqrt).then_inc(sem("gn_root"), 1)
            for j in range(4):
                act.wait_ge(sem("ret_turned"), j + 1)
                for m in range(2):
                    h = 2 * j + m
                    act.activation(UH[:, LB + h, :], bank[j][:, m * T:(m + 1) * T], ACT.Copy,
                                   scale=col("gnw", h)).then_inc(sem("ret_yh_ready"), 1)
            linear(S_OUT, Q_OUT, OUT_TILES, nothing)

            act.activation(cond[:, :, 0:2], csil[:, :, :], ACT.Copy).then_inc(sem("cond_hi"), 1)
            norm_turned(1, 1, lambda k: col("ln2", k))

            def step(kinds, n, i=None, tile=0):
                m = dict.fromkeys(kinds, 0)
                for p, kind in enumerate(kinds):
                    hi(n + LEAD + p, i, len(FF_STEP))
                    m[kind] += 1
                    if kind == "g" and m[kind] == CPT:
                        act.wait_ge(split_used, lin(n + p + 1, i, len(FF_STEP)))
                        if tile:
                            act.wait_ge(sem("ff_ready"), lin(tile, i, 1))
                        for b in range(NB):
                            ins = act.activation(ff_g[:, b, :], ACC[0][b][:, :], ACT.Silu)
                        ins.then_inc(acc_free_act, 2)
                    if kind == "a" and m[kind] % CPT == 0:
                        t = m[kind] // CPT - 1
                        act.wait_ge(split_used, lin(n + p + 1, i, len(FF_STEP)))
                        if tile:
                            act.wait_ge(sem("ada_cols"), lin(ADA_STEP * (tile - 1) + t + 1, i, ADA_STEP))
                        act.activation(ada_rows[0:4, t, :], ACC[0][t][0:4, :], ACT.Copy).then_inc(sem("ada_rows_ready"), 1)

            def turned(i=None, nth=0):
                act.wait_ge(sem("ff_turned"), lin(nth + 1, i, 1))
                for k in range(CK):
                    act.activation(FH[:, k, :], bank[2 + k // 2][:, (k % 2) * T:(k % 2 + 1) * T], ACT.Copy).then_inc(
                        sem("ffh_ready"), 1)

            step(FF_FIRST, S_FFN)
            turned()
            with act.Fori(0, FT - 1) as i:
                step(FF_STEP, S_STEP, i, tile=1)
                turned(i, 1)
            step(FF_LAST, S_LAST, tile=FT)

            norm_rows(2)

            def pads(name, base, banks, pad, done):
                for j in range(4):
                    act.wait_ge(sem(name), base + j + 1)
                    act.activation(pad[:, 2 * j:2 * j + 2, 1:T + 1], banks[j][:, :].rearrange("p (b t) -> p b t", t=T),
                                   ACT.Copy).then_inc(sem(done), 1)

            def keys_turned(S, banks):
                pads("k_turned", 4 * S.s, banks, S.pad, "k_pad_ready")

            def keys_silu(S):
                act.wait_ge(sem("k_conv"), S.s + 1)
                for b in range(MB):
                    ins = act.activation(S.kT(b), S.kT(b), ACT.Silu)
                    if b == MB // 2 - 1:
                        yield
                ins.then_inc(sem("k_silu"), 1)

            def keys_back(S, banks):
                if S.lat:
                    act.wait_ge(sem("v1_ready"), 1)
                for j in range(4):
                    act.wait_ge(sem("k_back"), 4 * S.s + j + 1)
                    act.activation(S.k_tok(j // 2, (j % 2) * CW, CW), banks[j][:, :], ACT.Copy,
                                   scale=float(MD) ** -0.5).then_inc(sem("k_tok_ready"), 1)

            def gate_weights(s):
                act.wait_ge(sem("tables_landed"), 16 * 6)
                act.activation(wg_h[s][:, :, :], wg[:, :, :], ACT.Copy).then_inc(sem("wg_hi"), 1)

            def gate_log(S):
                act.wait_ge(sem("fg_abs"), S.s + 1)
                chain(act.activation(S.b, S.b, ACT.Exp, scale=-1.0))
                act.activation(S.b, S.b, ACT.Ln, bias=1.0).then_inc(sem("fg_log"), 1)

            def gate_rows(S):
                act.wait_ge(sem("row_max"), S.s + 1)
                for d in range(2):
                    for n in range(NB):
                        chain.mark(act.activation(S.wk[:, d, span(n)], S.A[:, d, span(n)], ACT.Exp,
                                                  bias=n_ml[0:MH, d, n:n + 1]))
                chain.mark(act.activation(dcy[0:MH, :, :], dcy[0:MH, :, :], ACT.Exp))
                if S.lat:
                    for step, d, n in S.steps:
                        chain.mark(act.activation(S.lf[:, d, span(n)], S.M[:, d, span(n)], ACT.Exp, scale=-1.0,
                                                  bias=m_st[0:MH, d, NB + step:NB + step + 1]))
                    chain.mark(act.activation(S.ex, S.ex, ACT.Exp, scale=-1.0))
                chain.sync()
                act.sem_inc(sem("rows_exp"), 1)

            norm_turned(3, 2, lambda k: sc_mix[:, 1, k:k + 1], lambda k: modt[:, k, 1:2])
            gate_weights(0)
            to_kv = to(lambda t: kv[:, 0, bass.ds(t * CW, CW)], CW)

            def context():
                yield from pause(4)
                gate_log(streams[0])
                yield from pause(4)
                gate_rows(streams[0])
                yield from pause(2)
                keys_turned(streams[0], DB)
                yield from pause(4)
                yield from keys_silu(streams[0])
                keys_back(streams[0], DB)

            linear_among(S_CTX, Q_CTX, 0, CTX_TILES, to_kv, context())
            norm_rows(4)

            norm_turned(4, 3, lambda k: sc_mix[:, 0, k:k + 1], lambda k: modt[:, k, 0:1], normed=True)
            gate_weights(1)
            def to_p2(par, t):
                act.activation(P2[:, 0, W2_ORDER[t] * CW:(W2_ORDER[t] + 1) * CW], ACC[par][0][:, :], ACT.Copy).then_inc(
                    acc_free_act, 1)

            linear(S_IN2, Q_IN2, W2_HEAD, to(lambda t: P2[:, 0, bass.ds(t * CW, CW)], CW))
            L = streams[1]

            def mixers():
                act.wait_ge(acc_free_dve, Q_IN2 + W2_HEAD + 2)
                act.activation(P2[:, :, O_U:O_P], P2[:, :, O_U:O_P], ACT.Gelu_apprx_tanh).then_inc(sem("sgu_gelu"), 1)
                yield from pause(2)
                for g in range(len(PW)):
                    act.wait_ge(sem("pool_ps"), g // 2 * 2 + 2)
                    act.activation(pool_d[:, g, :], DB[g // 2][:, (g % 2) * T:(g % 2 + 1) * T], ACT.Copy).then_inc(
                        sem("pool_d_ready"), 1)
                act.wait_ge(sem("sgu_ms"), 1)
                act.activation(rms[:, :], ms[:, :], ACT.Sqrt).then_inc(sem("sgu_root"), 1)
                yield from pause(2)
                for g in range(len(PW)):
                    act.wait_ge(sem("pool_y_ps"), g // 2 * 2 + 2)
                    act.activation(pool_y[:, g, :], DB[2 + g // 2][:, (g % 2) * T:(g % 2 + 1) * T], ACT.Copy,
                                   scale=col("pscale", g)).then_inc(sem("pool_y_kept"), 1)
                yield from pause(4)
                for k in range(4):
                    act.wait_ge(sem("sgu_turned"), k // 2 + 1)
                    act.activation(sgu_t[:, k, :], DB[k // 2][:, (k % 2) * T:(k % 2 + 1) * T], ACT.Copy).then_inc(
                        sem("sgu_t_kept"), 1)
                yield from pause(2)
                gate_log(L)
                yield
                pads("q_turned", 0, DB, L.pad, "q_pad_ready")
                yield from pause(3)
                gate_rows(L)
                yield from pause(4)
                act.wait_ge(sem("q_conv"), 1)
                keys_turned(L, DB)
                yield
                qT = lat_half(O_Q)
                for b in range(MB):
                    ins = act.activation(qT(b), qT(b), ACT.Silu)
                    if b == 3:
                        yield
                ins.then_inc(sem("q_silu"), 1)
                yield from pause(3)
                yield from keys_silu(L)
                yield from pause(3)
                keys_back(L, DB)

            linear_among(S_IN2, Q_IN2, W2_HEAD, W2_TILES, to_p2, mixers())
            act.wait_ge(sem("co_ready"), 2)
            x = 0
            for step, d, n in L.steps:
                def weights(h):
                    act.wait_ge(sem("arg_ps"), x + h + 1)
                    if x + h >= 2:
                        act.wait_ge(sem("num_ps"), x + h - 1)
                    act.activation(wb[:, h % 2, :], DB[h % 2][:, 0:P], ACT.Exp, bias=co[:, 0, d, n, h:h + 1]).then_inc(
                        sem("w_exp"), 1)
                weights(0)
                for h in range(MH):
                    if h + 1 < MH:
                        weights(h + 1)
                    act.wait_ge(sem("num_ps"), x + h + 1)
                    if x + h >= 2:
                        act.wait_ge(sem("h_ready"), x + h - 1)
                    act.activation(ml_t[:, h % 2, :], ACC[h % 2][1][:, 0:VA], ACT.Copy,
                                   scale=co[:, 2, d, n, h:h + 1]).then_inc(sem("inter_ready"), 1)
                x += MH
            act.activation(P2[:, :, O_O:O_O + D_ML], P2[:, :, O_O:O_O + D_ML], ACT.Sigmoid).then_inc(sem("ml_gate"), 1)
            for g in range(len(PW)):
                act.activation(UH[:, 12 + g, :], pool_y[:, g, :], ACT.Copy).then_inc(sem("yh2_ready"), 1)
            for k in range(4):
                act.activation(UH[:, k, :], sgu_t[:, k, :], ACT.Copy).then_inc(sem("yh2_ready"), 1)
            act.wait_ge(sem("ml_ms"), 1)
            act.activation(l_ms[1][:, :], l_ms[0][:, :], ACT.Sqrt).then_inc(sem("ml_root"), 1)
            for j in range(4):
                act.wait_ge(sem("ml_turned"), j + 1)
                for m in range(2):
                    b = 2 * j + m
                    act.activation(UH[:, 4 + b, :], DB[j][:, m * T:(m + 1) * T], ACT.Copy, scale=col("mlnorm", b)).then_inc(
                        sem("yh2_ready"), 1)

            def spread(q, dst):
                for j in range(4):
                    act.wait_ge(sem("spread_ps"), 4 * q + j + 1)
                    act.activation(dst[:, j * CW:(j + 1) * CW], DB[j][:, :], ACT.Copy).then_inc(sem("spread_ready"), 1)

            spread(0, gb1)
            spread(1, gb2)
            linear(S_OUT2, Q_OUT2, OUT_TILES, nothing)
            norm_turned(5, 4, lambda k: sc_ffn[:, k:k + 1], lambda k: modt[:, 3 * KT + k, 0:1])
            act.wait_ge(sem("u_ready"), KT * 5)
            spread(2, sc_row)
            spread(3, sh_row)

            def to_q(par, t):
                if t >= 2:
                    act.wait_ge(sem("pq_turned"), 2 * (t - 1))
                act.activation(q_tok[:, t % 2, 0, :], ACC[par][0][:, :], ACT.Copy).then_inc(acc_free_act, 1)

            def queries():
                yield from pause(6)
                for t in range(OUT_TILES):
                    for j in range(2):
                        act.wait_ge(sem("pq_turned"), 2 * t + j + 1)
                        act.activation(q_t[:, t % 2, 2 * j:2 * j + 2, :], DB[j][:, :].rearrange("p (b t) -> p b t", t=T),
                                       ACT.Copy).then_inc(sem("q_t_ready"), 1)
                    yield from pause(2)
                    for b in range(NB):
                        act.wait_ge(sem("key_ps"), NB * t + b + 1)
                        act.activation(key_s[b][:, 2 * GH * t:2 * GH * (t + 1), :],
                                       DB[2 + b][:, :].rearrange("p (b t) -> p b t", t=NKEY), ACT.Copy).then_inc(
                            sem("key_s_ready"), 1)
                    yield from pause(2)

            linear_among(S_WQ, Q_WQ, 0, OUT_TILES, to_q, queries())
            act.wait_ge(sem("row_used"), GATH + SLOTS)
            act.wait_ge(sem("dots_kept"), SLOTS // GSTEP)
            act.activation(gate_w[:, :, :], gate_w[:, :, :], ACT.Exp).then_inc(sem("slots_ready"), 1)
            act.activation(dots[:, :, :], dots[:, :, :], ACT.Gelu_apprx_tanh).then_inc(sem("slots_ready"), 1)
            act.dma_start(nfin[:, :], a["nfin"].partition_broadcast(P)).then_inc(sem("nfin_landed"), 16)
            for b in range(NB):
                act.wait_ge(sem("fin_ms"), b + 1)
                act.activation(rms[:, b:b + 1], ms[:, b:b + 1], ACT.Sqrt).then_inc(sem("fin_root"), 1)

        @block.vector
        def _(dve):
            link = Chain(dve, "dve_chain")

            def lo(n, i=None, per=0):
                if i is None and n >= NCH:
                    return
                dve.wait_ge(hi_ready, lin(n + 1, i, per))
                dve.tensor_tensor(WL[:, n % SLOTS_W, :], raw[:, n % SLOTS_W, :], WH[:, n % SLOTS_W, :].bitcast(F32),
                                  ALU.subtract).then_inc(lo_ready, 1)

            def tile(n, evacuate, i=None, per=0, work=iter(())):
                for m in range(CPT):
                    lo(n + LEAD + m, i, per)
                    next(work, None)
                dve.wait_ge(split_used, lin(n + CPT, i, per))
                evacuate()

            def linear(n0, q0, tiles, evacuate):
                pairs = tiles // 2
                last = n0 + tiles * CPT == NCH
                with dve.Fori(0, pairs - last) as i:
                    for par in range(2):
                        tile(n0 + CPT * par, lambda: evacuate((q0 + par) % 2, lin(par, i, 2)), i, 2 * CPT)
                for t in range(2 * (pairs - last), tiles):
                    tile(n0 + CPT * t, lambda: evacuate((q0 + t) % 2, t))

            def linear_among(n0, q0, t0, tiles, evacuate, work):
                for t in range(t0, tiles):
                    tile(n0 + CPT * t, lambda: evacuate((q0 + t) % 2, t), work=work)
                for _ in work:
                    pass

            def to(dst, width):
                def evacuate(par, t):
                    dve.tensor_copy(dst(t), ACC[par][1][:, 0:width]).then_inc(acc_free_dve, 1)
                return evacuate

            def add_to_x(par, t):
                for b in range(NB):
                    x = X[:, b, bass.ds(t * CW, CW)]
                    ins = dve.tensor_tensor(x, ACC[par][b][:, :], x, ALU.add)
                ins.then_inc(acc_free_dve, 1)

            def norm_rows(call):
                x, xn = norm_of[call]
                dve.sem_inc(sem("norm_begins"), 1)
                link(dve.tensor_tensor_reduce(xn[:, 0, :], x[:, 0, :], x[:, 0, :], 1.0, 0.0, ALU.mult, ALU.add, ss[:, 0:1]))
                dve.wait_ge(sem("ss_ready"), call + 1)
                dve.tensor_scalar(ms[:, :], ss[:, :], 1.0 / D, EPS, ALU.mult, ALU.add).then_inc(sem("ms_ready"), 1)
                dve.wait_ge(sem("rms_ready"), call + 1)
                dve.reciprocal(rinv[:, :], rms[:, :]).then_inc(sem("rinv_ready"), 1)
                dve.wait_ge(sem("rinv_ready"), call + 1)
                dve.tensor_scalar(xn[:, 0, :], x[:, 0, :], rinv[:, 0:1], None, ALU.mult).then_inc(sem("xn_ready"), 1)

            def norm_turned(rows, call, scale, bias=None, normed=False):
                if not normed:
                    norm_rows(rows)
                for k in range(KT):
                    src = ALLB[k // 2][:, (k % 2) * T:(k % 2 + 1) * T]
                    dve.wait_ge(sem("uh_ready"), KT * call + k // 2 * 2 + 2)
                    if bias is None:
                        ins = dve.scalar_tensor_tensor(UL[:, k, :], src, scale(k), UH[:, k, :].bitcast(F32), ALU.mult,
                                                       ALU.subtract)
                    else:
                        link(dve.tensor_scalar(mod_tmp[:, k % 2, :], src, scale(k), bias(k), ALU.mult, ALU.add))
                        ins = dve.tensor_tensor(UL[:, k, :], mod_tmp[:, k % 2, :], UH[:, k, :].bitcast(F32), ALU.subtract)
                    ins.then_inc(sem("u_ready"), 1)

            dve.wait_ge(sem("cols_landed"), 16)
            o = COL["ada_b"][0]
            link(dve.tensor_copy(modt[:, :, :], cols[:, o:o + 6 * KT].unsqueeze(2).to_broadcast([P, 6 * KT, 2])))
            z, s, s2, acc, e = lam_t[1], lam_t[2], lam_t[3], lam_t[4], lam_t[0]
            dve.scalar_tensor_tensor(lam_t[0][:, :], col("lam", 0, LB), -1.0, col("lam", 0, LB), ALU.mult, ALU.max).then_inc(sem("lam_abs"), 1)
            dve.wait_ge(sem("lam_exp"), 1)
            link(dve.tensor_scalar(s[:, :], z[:, :], 2.0, None, ALU.add))
            link(dve.reciprocal(s[:, :], s[:, :]))
            link(dve.tensor_tensor(s[:, :], s[:, :], z[:, :], ALU.mult))
            link(dve.tensor_tensor(s2[:, :], s[:, :], s[:, :], ALU.mult))
            link(dve.memset(acc[:, :], 1.0 / 19))
            for n in range(17, 0, -2):
                link(dve.tensor_tensor(acc[:, :], acc[:, :], s2[:, :], ALU.mult))
                link(dve.tensor_scalar(acc[:, :], acc[:, :], 1.0 / n, None, ALU.add))
            link(dve.tensor_tensor(acc[:, :], acc[:, :], s[:, :], ALU.mult))
            link(dve.tensor_scalar(e[:, :], col("lam", 0, LB), -1.0, 0.0, ALU.mult, ALU.max))
            link(dve.scalar_tensor_tensor(acc[:, :], acc[:, :], 2.0, e[:, :], ALU.mult, ALU.add))
            link.mark(dve.tensor_scalar(p_col[:, :], acc[:, :], LRU_C, None, ALU.mult))
            dve.tensor_scalar(n_col[:, :], acc[:, :], -LRU_C, None, ALU.mult).then_inc(sem("lam_ready"), 1)
            for m in range(LEAD):
                lo(m)
            dve.sem_inc(acc_free_dve, 2)
            dve.wait_ge(sem("x_landed"), 16)
            norm_turned(0, 0, lambda k: col("ln1", k))
            to_pin = to(lambda t: Pin[:, 1, bass.ds(t * CW, CW)], CW)
            linear(S_IN, Q_IN, W_IN_HEAD, to_pin)

            def lru():
                link(dve.memset(lru_x[:, :, 0:CONV_W - 1], 0.0))
                yield from pause(2)
                for j in range(4):
                    dve.wait_ge(sem("lru_x_ready"), j + 1)
                    for tap in range(CONV_W):
                        for b in (2 * j, 2 * j + 1):
                            w, x = col("conv", tap * LB + b), lru_x[:, b, tap:tap + T]
                            if tap == 0:
                                link.mark(dve.tensor_scalar(lru_u[:, b, :], x, w, col("convb", b), ALU.mult, ALU.add))
                            else:
                                link.mark(dve.scalar_tensor_tensor(lru_u[:, b, :], x, w, lru_u[:, b, :], ALU.mult, ALU.add))
                        link.sync()
                        if tap % 2:
                            yield
                dve.sem_inc(sem("lru_u_ready"), 1)
                yield from pause(12)
                dve.wait_ge(sem("lru_gates_ready"), 2 * LB)
                link(dve.tensor_tensor(wide(1), wide(1), lru_u[:, :, :].rearrange("p (n b) t -> p n (b t)", n=NB), ALU.mult))
                yield from pause(2)
                dve.wait_ge(sem("lru_tanh"), LB)
                link(dve.tensor_scalar(lru_u[:, :, :], lru_b[:, :, :], 1.0, None, ALU.add))
                yield
                link(dve.reciprocal(lru_u[:, :, :], lru_u[:, :, :]))
                yield
                dve.scalar_tensor_tensor(lru_b[:, :, :], lru_b[:, :, :], 2.0, lru_u[:, :, :], ALU.mult, ALU.mult).then_inc(
                    sem("lru_sq_ready"), 1)
                yield from pause(2)
                dve.wait_ge(sem("lru_root"), 1)
                link(dve.tensor_tensor(lru_b[:, :, :].rearrange("p (n b) t -> p n (b t)", n=NB),
                                       lru_b[:, :, :].rearrange("p (n b) t -> p n (b t)", n=NB), wide(1), ALU.mult))
                yield
                dve.wait_ge(sem("lru_a_ready"), LB)
                for b in range(LB):
                    link.mark(dve.tensor_tensor_scan(lru_u[:, b, :], half(0)(b), lru_b[:, b, :], 0.0, ALU.mult, ALU.add))
                    if b % 2:
                        yield
                link.sync()
                dve.tensor_tensor(lru_g[:, :, :], lru_g[:, :, :], lru_u[:, :, :], ALU.mult).then_inc(sem("lru_y_ready"), 1)
                yield
                dve.wait_ge(sem("rope_landed"), 16)
                dve.wait_ge(acc_free_act, Q_IN + 8 + 2)
                dve.wait_ge(acc_free_dve, Q_IN + 8 + 2)
                dve.wait_ge(sem("lru_y_ready"), 1)
                for b in range(NB):
                    qk = Pin[:, b, C_Q:C_V].rearrange("p (h u e) -> p h u e", u=2, e=P // 2)
                    t1, t2 = qk[:, :, 0, :], qk[:, :, 1, :]
                    c, s = (rope[:, b, j:j + 1, :].to_broadcast([P, KT, P // 2]) for j in range(2))
                    for k, (dst, t, w) in enumerate(((rt[0], t1, c), (rt[1], t2, s), (rt[2], t1, s), (rt[3], t2, c))):
                        link.mark(dve.tensor_tensor(dst[:, :, :], t, w, ALU.mult))
                        if k == 1:
                            yield
                    link.sync()
                    yield
                    link.mark(dve.tensor_tensor(t1, rt[0][:, :, :], rt[1][:, :, :], ALU.subtract))
                    link(dve.tensor_tensor(t2, rt[2][:, :, :], rt[3][:, :, :], ALU.add))
                    dve.sem_inc(sem("rope_ready"), 1)
                    yield

            linear_among(S_IN, Q_IN, W_IN_HEAD, W_IN_TILES, to_pin, lru())
            dve.wait_ge(sem("lru_yh_ready"), 1)
            dve.tensor_tensor(UL[:, 0:LB, :], lru_g[:, :, :], UH[:, 0:LB, :].bitcast(F32), ALU.subtract).then_inc(
                sem("y1_ready"), LB)
            dve.wait_ge(sem("y1_ready"), LB)

            o = COL["zeta"][0]
            dve.tensor_tensor(ret_kz[:, :, :], Pin[:, 0, C_Q + 1024:C_V].rearrange("p (h e) -> p h e", e=P),
                              cols[:, o:o + HEADS].unsqueeze(2).to_broadcast([P, HEADS, P]), ALU.mult).then_inc(
                sem("ret_kz_ready"), 1)
            dve.wait_ge(sem("decay_landed"), 16)
            for j in range(4):
                dve.wait_ge(sem("ret_scores"), j + 1)
                for m in range(2):
                    h = 2 * j + m
                    ins = dve.tensor_tensor(ret_s[:, h, :, :], DB[j][:, m * T:(m + 1) * T].rearrange("p (n q) -> p n q", q=P),
                                            decay[:, h:h + 1, :].to_broadcast([P, NB, P]), ALU.mult)
                ins.then_inc(sem("ret_s_ready"), 1)
            dve.wait_ge(sem("ret_inner"), 1)
            for j in range(2):
                link.mark(dve.tensor_copy(ret_o[:, 0, 4 * j:4 * j + 4, :], bank[j][:, :].rearrange("p (h e) -> p h e", e=P)))
            dve.wait_ge(sem("ret_cross"), 1)
            o = COL["xi"][0]
            for j in range(2):
                link(dve.tensor_tensor(ret_o[:, 1, 4 * j:4 * j + 4, :], DB[2 + j][:, :].rearrange("p (h e) -> p h e", e=P),
                                       cols[:, o + 4 * j:o + 4 * j + 4].unsqueeze(2).to_broadcast([P, 4, P]), ALU.mult))
                link(dve.tensor_tensor(ret_o[:, 1, 4 * j:4 * j + 4, :], ret_o[:, 1, 4 * j:4 * j + 4, :],
                                       bank[2 + j][:, :].rearrange("p (h e) -> p h e", e=P), ALU.add))
            heads = ret_o[:, :, :, :].rearrange("p n h e -> p (n h) e")
            sq = ret_sq[:, :, :, :].rearrange("p n h e -> p (n h) e")
            nh = [P, NB * HEADS, P]
            link(dve.tensor_reduce(gn[0][:, :], heads, AX.X, ALU.add))
            link(dve.tensor_scalar(gn[0][:, :], gn[0][:, :], 1.0 / P, None, ALU.mult))
            link(dve.tensor_tensor(heads, heads, gn[0][:, :].unsqueeze(2).to_broadcast(nh), ALU.subtract))
            link(dve.tensor_tensor(sq, heads, heads, ALU.mult))
            link(dve.tensor_reduce(gn[0][:, :], sq, AX.X, ALU.add))
            dve.tensor_scalar(gn[0][:, :], gn[0][:, :], 1.0 / P, EPS, ALU.mult, ALU.add).then_inc(sem("gn_var"), 1)
            dve.wait_ge(sem("gn_root"), 1)
            link(dve.reciprocal(gn[2][:, :], gn[1][:, :]))
            link(dve.tensor_tensor(heads, heads, gn[2][:, :].unsqueeze(2).to_broadcast(nh), ALU.mult))
            dve.wait_ge(sem("ret_gate"), 1)
            dve.tensor_tensor(ret_o[:, :, :, :].rearrange("p n h e -> p n (h e)"),
                              ret_o[:, :, :, :].rearrange("p n h e -> p n (h e)"), Pin[:, :, C_G:C_G + 1024],
                              ALU.mult).then_inc(sem("ret_o_ready"), 1)
            for h in range(HEADS):
                dve.wait_ge(sem("ret_yh_ready"), h // 2 * 2 + 2)
                dve.scalar_tensor_tensor(UL[:, LB + h, :], bank[h // 2][:, (h % 2) * T:(h % 2 + 1) * T], col("gnw", h),
                                         UH[:, LB + h, :].bitcast(F32), ALU.mult, ALU.subtract).then_inc(
                    sem("y1_ready"), 1)
            linear(S_OUT, Q_OUT, OUT_TILES, add_to_x)
            dve.wait_ge(acc_free_dve, Q_FFN + 2)

            link.mark(dve.memset(cond[:, :, 4:P].bitcast(F32), 0.0))
            dve.wait_ge(sem("cond_hi"), 1)
            link.mark(dve.tensor_tensor(cond[:, :, 2:4], csil[:, :, :], cond[:, :, 0:2].bitcast(F32), ALU.subtract))
            link.sync()
            dve.sem_inc(sem("cond_ready"), 1)
            norm_turned(1, 1, lambda k: col("ln2", k))
            dve.sem_inc(sem("down_added"), 2)

            def up(i=None, nth=0):
                dve.wait_ge(acc_free_act, lin(Q_FFN + 2 + 2 * (nth + 1), i, 2))
                if i is not None:
                    dve.wait_ge(sem("ff_turned"), lin(nth, i, 1))
                for b in range(NB):
                    ins = dve.tensor_tensor(ff[:, b, :], ACC[1][b][:, :], ff_g[:, b, :], ALU.mult)
                ins.then_inc(sem("ff_ready"), 1)
                dve.sem_inc(acc_free_dve, 2)

            def turned(i=None, nth=0):
                for k in range(CK):
                    dve.wait_ge(sem("ffh_ready"), lin(CK * nth + k // 2 * 2 + 2, i, CK))
                    dve.tensor_tensor(FL[:, k, :], bank[2 + k // 2][:, (k % 2) * T:(k % 2 + 1) * T],
                                      FH[:, k, :].bitcast(F32), ALU.subtract).then_inc(sem("ffT_ready"), 1)

            def add_down(n, j, i=None, per=0):
                dve.wait_ge(split_used, lin(n + 1, i, per))
                for b in range(NB):
                    x = X[:, b, j * CW:(j + 1) * CW]
                    ins = dve.tensor_tensor(x, DB[2 * (j % 2) + b][:, :], x, ALU.add)
                ins.then_inc(sem("down_added"), 1)

            def step(kinds, n, i=None, tile=0):
                m = dict.fromkeys(kinds, 0)
                for p, kind in enumerate(kinds):
                    lo(n + LEAD + p, i, len(FF_STEP))
                    m[kind] += 1
                    if kind == "u" and m[kind] == CPT:
                        dve.wait_ge(split_used, lin(n + p + 1, i, len(FF_STEP)))
                        up(i, tile)
                    if kind == "d":
                        add_down(n + p, m[kind] - 1, i, len(FF_STEP))

            def modulation(i=None, nth=0):
                for t in range(ADA_STEP):
                    dve.wait_ge(sem("ada_cols"), lin(ADA_STEP * nth + t + 1, i, ADA_STEP))
                    w = CW // P
                    m = modt[:, bass.ds(lin(w * (ADA_STEP * nth + t), i, w * ADA_STEP), w), :]
                    dve.tensor_tensor(m, ACC[0][t][:, 0:2 * w].rearrange("p (j r) -> p j r", r=2), m, ALU.add).then_inc(
                        sem("mod_ready"), 1)

            step(FF_FIRST, S_FFN)
            turned()
            modulation()
            with dve.Fori(0, FT - 1) as i:
                step(FF_STEP, S_STEP, i, tile=1)
                modulation(i, 1)
                turned(i, 1)
            step(FF_LAST, S_LAST)
            modulation(nth=FT)
            dve.wait_ge(sem("down_added"), 2 + FT * OUT_TILES)

            dve.wait_ge(sem("mod_ready"), ADA_TILES)
            for r in range(2):
                link(dve.scalar_tensor_tensor(sc_mix[:, r, :], modt[:, KT:2 * KT, r], 1.0, col("nmix", 0, KT), ALU.add,
                                              ALU.mult))
            link(dve.scalar_tensor_tensor(sc_ffn[:, :], modt[:, 4 * KT:5 * KT, 0], 1.0, col("nffn", 0, KT), ALU.add,
                                          ALU.mult))

            norm_rows(2)
            dve.wait_ge(sem("xn_ready"), 2 * 3)
            dve.wait_ge(sem("fnw_landed"), 16)
            for b in range(NB):
                link.mark(dve.tensor_tensor(X[:, b, :], XN[:, b, :], fnw[:, :], ALU.mult))
            link.sync()
            dve.sem_inc(sem("x2_ready"), 1)

            def conv(S, dst, taps, padded, base):
                for j in range(4):
                    dve.wait_ge(sem(padded), base + (4 if S.lat else j + 1))
                    for tap in range(3):
                        for b in (2 * j, 2 * j + 1):
                            w, x = col("qkconv", tap * 2 * MB + taps + b), S.pad[:, b, tap:tap + T]
                            if tap == 0:
                                link.mark(dve.tensor_scalar(dst(b), x, w, None, ALU.mult))
                            else:
                                link.mark(dve.scalar_tensor_tensor(dst(b), x, w, dst(b), ALU.mult, ALU.add))
                        link.sync()
                    yield

            def edges(S):
                for t in (0, T + 1):
                    link.mark(dve.memset(S.pad[:, :, t:t + 1], 0.0))
                link.sync()

            def gates(s):
                dve.wait_ge(sem("gate_ps"), s + 1)
                dve.tensor_copy(g_row[s][0:NG, :], DB[2][0:NG, 0:T]).then_inc(sem("g_row_ready"), 1)

            def gate_rows(S):
                dve.wait_ge(sem("gate_rows_ps"), S.s + 1)
                for typ, dst in ((0, S.A), (1, S.lf)):
                    for d in range(2):
                        link.mark(dve.tensor_scalar(dst[:, d, :], DB[2 + typ][0:MH, d * T:(d + 1) * T],
                                                    col("bgate", 2 * d + typ, rows=MH), None, ALU.add))
                link.sync()
                dve.sem_inc(sem("gate_rows_kept"), 1)
                dve.scalar_tensor_tensor(S.b, S.lf, -1.0, S.lf, ALU.mult, ALU.max).then_inc(sem("fg_abs"), 1)
                link(dve.memset(S.M, 0.0))
                yield
                dve.wait_ge(sem("fg_log"), S.s + 1)
                link(dve.scalar_tensor_tensor(S.lf, S.lf, 0.0, S.b, ALU.min, ALU.subtract))
                for d in range(2):
                    for n in range(NB):
                        link.mark(dve.tensor_tensor_scan(scan_ap(S.b, d, n), scan_ap(S.lf, d, n), scan_ap(S.M, d, n), 0.0,
                                                         ALU.add, ALU.add))
                link.sync()
                link(dve.tensor_tensor(S.A, S.A, S.b, ALU.subtract))
                yield
                for step, d, n in S.steps:
                    m0 = NB * S.s + step
                    link(dve.tensor_tensor_scan(scan_ap(S.M, d, n), scan_ap(S.A, d, n), scan_ap(S.A, d, n),
                                                m_st[0:MH, d, m0:m0 + 1], ALU.max, ALU.max))
                    last = last_of(S.M, d, n)
                    link.mark(dve.tensor_tensor(m_st[0:MH, d, m0 + 1:m0 + 2], last_of(S.b, d, n), last, ALU.add))
                    link.mark(dve.tensor_scalar(n_ml[0:MH, d, n:n + 1], last, -1.0, None, ALU.mult))
                    link(dve.tensor_tensor(dcy[0:MH, d, n:n + 1], m_st[0:MH, d, m0:m0 + 1], last, ALU.subtract))
                    if d == 1:
                        yield
                if S.lat:
                    link(dve.tensor_tensor(S.ex, S.b, S.M, ALU.add))
                dve.sem_inc(sem("row_max"), 1)
                if S.lat:
                    link(dve.tensor_scalar(S.b, S.M, -1.0, None, ALU.mult))

            def rows_done(S):
                dve.wait_ge(sem("rows_exp"), S.s + 1)
                dve.sem_inc(sem("rows_ready"), 1)

            def columns(S):
                dve.wait_ge(sem("cols_ps"), S.s + 1)
                for k in range(5) if S.lat else (1, 4):
                    w = 2 * NB * MH
                    link.mark(dve.tensor_copy(co[:, k, :, :, :].rearrange("p d n h -> p (d n h)"), DB[2][:, k * w:(k + 1) * w]))
                link.sync()
                dve.sem_inc(sem("co_ready"), 1)

            def ones(S):
                link.mark(dve.memset(S.v1[:, :, :, MD:VA], 1.0))
                for n in range(NB):
                    link.mark(dve.tensor_copy(S.v1[:, n, :, 0:MD], S.v(n).rearrange("p (h e) -> p h e", e=MD)))
                link.sync()

            upd = [0]

            def updates(S, steps):
                u0 = upd[0]
                todo = [(d, n, h) for _, d, n in steps for h in range(MH)]

                def weigh(q):
                    if q < len(todo):
                        d, n, h = todo[q]
                        dve.tensor_scalar(vw[:, h % 2, :], S.v1[:, n, h, :], co[:, 1, d, n, h:h + 1], None, ALU.mult).then_inc(
                            sem("vw_ready"), 1)

                if u0:
                    dve.wait_ge(sem("state_ps"), u0)
                weigh(0)
                weigh(1)
                for q, (d, n, h) in enumerate(todo):
                    dve.wait_ge(sem("state_ps"), u0 + q + 1)
                    if u0 + q >= 2 * MH:
                        dve.wait_ge(sem("state_ready"), u0 + q + 1 - 2 * MH)
                    for kt in range(MKT):
                        s = st[:, d, h, kt, :]
                        ins = dve.scalar_tensor_tensor(s, s, co[:, 4, d, n, h:h + 1], ALLB[2 * h + kt][:, 0:VA], ALU.mult,
                                                       ALU.add)
                    ins.then_inc(sem("state_ready"), 1)
                    weigh(q + 2)
                upd[0] += len(todo)
                dve.wait_ge(sem("state_ready"), upd[0])

            def gate_weights(s):
                dve.wait_ge(sem("wg_hi"), s + 1)
                dve.tensor_tensor(wg_l[s][:, :, :], wg[:, :, :], wg_h[s][:, :, :].bitcast(F32), ALU.subtract).then_inc(
                    sem("wg_ready"), 1)

            dve.wait_ge(sem("ctx_landed"), 16)
            norm_turned(3, 2, lambda k: sc_mix[:, 1, k:k + 1], lambda k: modt[:, k, 1:2])
            gate_weights(0)
            to_kv = to(lambda t: kv[:, 1, bass.ds(t * CW, CW)], CW)
            C = streams[0]

            def context():
                edges(C)
                link.mark(dve.memset(m_st[0:MH, :, :], 0.0))
                link.mark(dve.memset(st[:, :, :, :, :], 0.0))
                yield
                gates(0)
                yield from pause(2)
                yield from gate_rows(C)
                yield from pause(2)
                rows_done(C)
                yield
                yield from conv(C, C.kT, MB, "k_pad_ready", 0)
                dve.sem_inc(sem("k_conv"), 1)

            linear_among(S_CTX, Q_CTX, 0, CTX_TILES, to_kv, context())
            dve.wait_ge(acc_free_act, Q_IN2 + 2)
            dve.wait_ge(acc_free_dve, Q_IN2 + 2)
            ones(C)
            dve.wait_ge(sem("k_pad_ready"), 4)
            dve.wait_ge(sem("k_turned"), 4)
            norm_rows(4)
            columns(C)
            updates(C, C.steps)
            dve.sem_inc(sem("ctx_done"), 1)

            norm_turned(4, 3, lambda k: sc_mix[:, 0, k:k + 1], lambda k: modt[:, k, 0:1], normed=True)
            gate_weights(1)
            def to_p2(par, t):
                dve.tensor_copy(P2[:, 1, W2_ORDER[t] * CW:(W2_ORDER[t] + 1) * CW], ACC[par][1][:, :]).then_inc(acc_free_dve, 1)

            linear(S_IN2, Q_IN2, W2_HEAD, to(lambda t: P2[:, 1, bass.ds(t * CW, CW)], CW))
            L = streams[1]

            def mixers():
                yield
                gates(1)
                dve.wait_ge(sem("sgu_gelu"), 1)
                dve.wait_ge(sem("sgu_n_landed"), 16)
                for b in range(NB):
                    v = P2[:, b, O_V:O_P]
                    link(dve.tensor_tensor_reduce(sgu_sq[:, :], v, v, 1.0, 0.0, ALU.mult, ALU.add, ss[:, b:b + 1]))
                dve.tensor_scalar(ms[:, :], ss[:, :], 1.0 / D_SGU, EPS, ALU.mult, ALU.add).then_inc(sem("sgu_ms"), 1)
                yield from pause(2)
                dve.wait_ge(sem("sgu_root"), 1)
                link(dve.reciprocal(rinv[:, :], rms[:, :]))
                for b in range(NB):
                    v = P2[:, b, O_V:O_P]
                    ins = dve.scalar_tensor_tensor(v, v, rinv[:, b:b + 1], sgu_n[:, :], ALU.mult, ALU.mult)
                ins.then_inc(sem("sgu_v_ready"), 1)
                yield from pause(2)
                dve.wait_ge(sem("sgu_ps"), 1)
                for n in range(NB):
                    for h in range(SH):
                        u = P2[:, n, O_U + h * P:O_U + (h + 1) * P]
                        ins = dve.scalar_tensor_tensor(u, DB[n][:, h * P:(h + 1) * P], col("sgub", h), u, ALU.add, ALU.mult)
                ins.then_inc(sem("sgu_y_ready"), 1)
                yield from pause(4)
                dve.wait_ge(sem("sgu_turned"), 2)
                dve.wait_ge(sem("pool_ps"), len(PW))
                yield from gate_rows(L)
                yield
                dve.wait_ge(sem("pool_y_ps"), len(PW))
                edges(L)
                qT = lat_half(O_Q)
                yield from conv(L, qT, 0, "q_pad_ready", 0)
                dve.sem_inc(sem("q_conv"), 1)
                yield
                yield from conv(L, L.kT, MB, "k_pad_ready", 4)
                dve.sem_inc(sem("k_conv"), 1)
                yield from pause(3)
                dve.wait_ge(acc_free_act, Q_IN2 + 9 + 2)
                dve.wait_ge(acc_free_dve, Q_IN2 + 9 + 2)
                ones(L)
                dve.sem_inc(sem("v1_ready"), 1)
                rows_done(L)
                yield from pause(2)
                dve.wait_ge(sem("ml_scores"), 1)
                for j in range(2):
                    link.mark(dve.tensor_scalar(sc_t[:, 2 * j:2 * j + 2, :, :].rearrange("p h n t -> p (h n t)"), DB[j][:, :],
                                                float(MD) ** -0.5, None, ALU.mult))
                link.sync()
                dve.sem_inc(sem("sc_t_ready"), 1)
                yield
                columns(L)

            linear_among(S_IN2, Q_IN2, W2_HEAD, W2_TILES, to_p2, mixers())
            x = 0
            for step, d, n in L.steps:
                def weights(h):
                    dve.wait_ge(sem("w_exp"), x + h + 1)
                    dve.tensor_tensor(wb[:, h % 2, :], wb[:, h % 2, :], sc_t[:, h, n, :], ALU.mult).then_inc(sem("w_ready"), 1)
                weights(0)
                for h in range(MH):
                    if h + 1 < MH:
                        weights(h + 1)
                    dve.wait_ge(sem("inter_ready"), x + h + 1)
                    t = ml_t[:, h % 2, :]
                    link(dve.tensor_tensor(t, t, ACC[h % 2][0][:, 0:VA], ALU.add))
                    link(dve.scalar_tensor_tensor(den[:, 0:1], t[:, MD:VA], -1.0, t[:, MD:VA], ALU.mult, ALU.max))
                    link(dve.tensor_scalar(den[:, 0:1], den[:, 0:1], co[:, 3, d, n, h:h + 1], None, ALU.max))
                    link(dve.reciprocal(den[:, 1:2], den[:, 0:1]))
                    y = P2[:, n, O_K + h * MD:O_K + (h + 1) * MD]
                    if step == 0:
                        ins = dve.tensor_scalar(y, t[:, 0:MD], den[:, 1:2], None, ALU.mult)
                    else:
                        ins = dve.scalar_tensor_tensor(y, t[:, 0:MD], den[:, 1:2], y, ALU.mult, ALU.add)
                    ins.then_inc(sem("h_ready"), 1)
                x += MH
                dve.wait_ge(sem("h_ready"), x)
                if step == 0:
                    updates(L, [(step, d, n)])
            nh = [P, MH, MD]
            for n in range(NB):
                y = P2[:, n, O_K:O_K + D_ML]
                sq = P2[:, n, O_Q:O_Q + D_ML]
                link(dve.tensor_tensor(sq, y, y, ALU.mult))
                link(dve.tensor_reduce(l_ms[2][:, n * MH:(n + 1) * MH], sq.rearrange("p (h e) -> p h e", e=MD), AX.X, ALU.add))
            dve.tensor_scalar(l_ms[0][:, :], l_ms[2][:, :], 1.0 / MD, EPS, ALU.mult, ALU.add).then_inc(sem("ml_ms"), 1)
            dve.wait_ge(sem("ml_root"), 1)
            link(dve.reciprocal(l_ms[2][:, :], l_ms[1][:, :]))
            dve.wait_ge(sem("ml_gate"), 1)
            for n in range(NB):
                y = P2[:, n, O_K:O_K + D_ML]
                yh = y.rearrange("p (h e) -> p h e", e=MD)
                link(dve.tensor_tensor(yh, yh, l_ms[2][:, n * MH:(n + 1) * MH].unsqueeze(2).to_broadcast(nh), ALU.mult))
                link(dve.tensor_tensor(y, y, P2[:, n, O_O:O_O + D_ML], ALU.mult))
            dve.sem_inc(sem("ml_y_ready"), 1)
            for g in range(len(PW)):
                dve.wait_ge(sem("yh2_ready"), g + 1)
                dve.tensor_tensor(UL[:, 12 + g, :], pool_y[:, g, :], UH[:, 12 + g, :].bitcast(F32), ALU.subtract).then_inc(
                    sem("y2_ready"), 1)
            for k in range(4):
                dve.wait_ge(sem("yh2_ready"), 4 + k + 1)
                dve.tensor_tensor(UL[:, k, :], sgu_t[:, k, :], UH[:, k, :].bitcast(F32), ALU.subtract).then_inc(
                    sem("y2_ready"), 1)
            for b in range(MB):
                dve.wait_ge(sem("yh2_ready"), 8 + b // 2 * 2 + 2)
                dve.scalar_tensor_tensor(UL[:, 4 + b, :], DB[b // 2][:, (b % 2) * T:(b % 2 + 1) * T], col("mlnorm", b),
                                         UH[:, 4 + b, :].bitcast(F32), ALU.mult, ALU.subtract).then_inc(sem("y2_ready"), 1)

            def add_gated(par, t):
                for b in range(NB):
                    ins = dve.tensor_tensor(g_tmp[:, b, :], ACC[par][b][:, :], gb1[:, bass.ds(t * CW, CW)], ALU.mult)
                ins.then_inc(sem("gated"), 1)
                dve.wait_ge(sem("gated"), t + 1)
                for b in range(NB):
                    x = X[:, b, bass.ds(t * CW, CW)]
                    ins = dve.tensor_tensor(x, g_tmp[:, b, :], x, ALU.add)
                ins.then_inc(acc_free_dve, 1)

            dve.wait_ge(sem("spread_ready"), 8)
            linear(S_OUT2, Q_OUT2, OUT_TILES, add_gated)
            dve.wait_ge(acc_free_dve, Q_WQ + 2)
            norm_turned(5, 4, lambda k: sc_ffn[:, k:k + 1], lambda k: modt[:, 3 * KT + k, 0:1])

            def to_q(par, t):
                if t >= 2:
                    dve.wait_ge(sem("pq_turned"), 2 * (t - 1))
                dve.tensor_copy(q_tok[:, t % 2, 1, :], ACC[par][1][:, :]).then_inc(acc_free_dve, 1)

            def top16(values, keep, pos):
                for r in range(2):
                    w = slice(8 * r, 8 * r + 8)
                    for v, k in zip(values, keep):
                        link.mark(dve.max(k[:, w], v))
                    link.sync()
                    for v, k, p in zip(values, keep, pos):
                        link.mark(dve.max_index(p[:, w], k[:, w], v))
                    if r == 0:
                        for v, k in zip(values, keep):
                            link.mark(dve.match_replace(v, k[:, w], v, LOWEST))
                    link.sync()
                    yield

            def choose(b, g):
                lists = range(2 * GH)
                dve.wait_ge(sem("key_s_ready"), NB * g + b + 1)
                yield from top16([key_s[b][:, 2 * GH * g + hp, :] for hp in lists], [top_v[:, hp, :] for hp in lists],
                                 [top_i[:, hp, :] for hp in lists])
                link.mark(dve.tensor_copy(top_f[:, :, :], top_i[:, :, :]))
                both = top_v[:, :, :].rearrange("p (h s) k -> p h s k", s=2)
                full = [P, GH, TOPK, TOPK]
                link(dve.tensor_tensor(cand[:, :, :, :], both[:, :, 0, :].unsqueeze(3).to_broadcast(full),
                                       both[:, :, 1, :].unsqueeze(2).to_broadcast(full), ALU.add))
                yield from top16([cand[:, h, :, :].rearrange("p a b -> p (a b)") for h in range(GH)],
                                 [best_v[:, h, :] for h in range(GH)], [best_i[:, h, :] for h in range(GH)])
                ranks = best_i[:, :, :].rearrange("p h k -> p (h k)")
                of = top_f[:, :, :].rearrange("p (h s) k -> p h s k", s=2)
                hots = hot[:, :, :, :].rearrange("p h j k -> p (h j) k")
                o = COL["iota"][0]
                for s in range(2):
                    op, by = (ALU.logical_shift_right, 4) if s == 0 else (ALU.bitwise_and, TOPK - 1)
                    link(dve.tensor_scalar(pick_i[:, :], ranks, by, None, op))
                    link(dve.tensor_copy(pick_f[:, :], pick_i[:, :]))
                    link(dve.tensor_tensor(hots, cols[:, o:o + TOPK].unsqueeze(1).to_broadcast([P, GSTEP, TOPK]),
                                           pick_f[:, :].unsqueeze(2).to_broadcast([P, GSTEP, TOPK]), ALU.is_equal))
                    link(dve.tensor_tensor(hot[:, :, :, :], hot[:, :, :, :], of[:, :, s, :].unsqueeze(2).to_broadcast(full),
                                           ALU.mult))
                    link(dve.tensor_reduce(exp_f[s][:, :], hots, AX.X, ALU.add))
                    yield
                link(dve.scalar_tensor_tensor(pick_f[:, :], exp_f[0][:, :], float(NKEY), exp_f[1][:, :], ALU.mult, ALU.add))
                mine = slice(GSTEP * g, GSTEP * (g + 1))
                dve.tensor_copy(idx[:, b, mine], pick_f[:, :]).then_inc(sem("idx_ready"), 1)
                w = gate_w[:, b, mine].rearrange("p (h k) -> p h k", k=TOPK)
                link(dve.tensor_tensor(w, best_v[:, :, :], best_v[:, :, 0:1].to_broadcast([P, GH, TOPK]), ALU.subtract))

            def choices(which):
                for b, g in which:
                    yield from choose(b, g)

            def early():
                dve.wait_ge(sem("spread_ready"), 16)
                for b in range(NB):
                    link(dve.tensor_tensor(XN2[:, b, :], XN2[:, b, :], sc_row[:, :], ALU.mult))
                    yield
                    link(dve.tensor_tensor(XN2[:, b, :], XN2[:, b, :], sh_row[:, :], ALU.add))
                    yield
                yield from pause(5)
                yield from choices(((0, 0), (0, 1)))

            linear_among(S_WQ, Q_WQ, 0, OUT_TILES, to_q, early())

            def landed(g0, s, i=None):
                dve.wait_ge(sem(f"row_landed{s % GATH}"), lin(16 * ((g0 + s) // GATH + 1), i, 16 * GSTEP // GATH))

            dve.sem_inc(sem("row_used"), GATH)
            pieces = choices([(0, g) for g in range(2, GROUPS)] + [(1, g) for g in range(GROUPS)])
            for s in range(SLOTS):
                landed(0, s)
                r = rows_g[:, s % GATH, :]
                dve.tensor_tensor_reduce(r, r, XN2[:, 0, :], 1.0, 0.0, ALU.mult, ALU.add, dots[:, 0, s:s + 1]).then_inc(
                    sem("row_used"), 1)
                if s % 3 == 2:
                    next(pieces, None)
            for _ in pieces:
                pass
            with dve.Fori(0, SLOTS // GSTEP) as i:
                for s in range(GSTEP):
                    landed(SLOTS, s, i)
                    r = rows_g[:, s % GATH, :]
                    dve.tensor_tensor_reduce(r, r, XN2[:, 1, :], 1.0, 0.0, ALU.mult, ALU.add,
                                             step_dots[:, s:s + 1]).then_inc(sem("row_used"), 1)
                dve.wait_ge(sem("row_used"), lin(GATH + SLOTS + GSTEP, i, GSTEP))
                dve.tensor_copy(dots[:, 1, bass.ds(i * GSTEP, GSTEP)], step_dots[:, :]).then_inc(sem("dots_kept"), 1)
                dve.wait_ge(sem("dots_kept"), lin(1, i, 1))
            dve.wait_ge(sem("dots_kept"), SLOTS // GSTEP)
            dve.wait_ge(sem("slots_ready"), 1)
            w = gate_w[:, :, :].rearrange("p b (h k) -> p (b h) k", k=TOPK)
            link(dve.tensor_reduce(soft[:, :], w, AX.X, ALU.add))
            link(dve.reciprocal(soft[:, :], soft[:, :]))
            link(dve.tensor_tensor(w, w, soft[:, :].unsqueeze(2).to_broadcast([P, NB * PH, TOPK]), ALU.mult))
            dve.wait_ge(sem("slots_ready"), 2)
            link(dve.tensor_tensor(gate_w[:, :, :], gate_w[:, :, :], dots[:, :, :], ALU.mult))
            for b in range(NB):
                g0 = (NB + b) * SLOTS
                link(dve.memset(v_sum[:, :, :], 0.0))
                with dve.Fori(0, SLOTS // GSTEP) as i:
                    for s in range(GSTEP):
                        landed(g0, s, i)
                        dve.wait_ge(sem("row_used"), lin(GATH + g0 + s - 1, i, GSTEP))
                        v = v_sum[:, s % 2, :]
                        dve.scalar_tensor_tensor(v, rows_g[:, s % GATH, :], gate_w[:, b, bass.ds(lin(s, i, GSTEP), 1)], v,
                                                 ALU.mult, ALU.add).then_inc(sem("row_used"), 1)
                dve.wait_ge(sem("row_used"), GATH + g0 + SLOTS)
                v = v_sum[:, 0, :]
                link(dve.tensor_tensor(v, v, v_sum[:, 1, :], ALU.add))
                link(dve.tensor_tensor(v, v, gb2[:, :], ALU.mult))
                x = X[:, b, :]
                link(dve.tensor_tensor(x, x, v, ALU.add))
                link(dve.tensor_tensor_reduce(v_sum[:, 1, :], x, x, 1.0, 0.0, ALU.mult, ALU.add, ss[:, b:b + 1]))
                dve.tensor_scalar(ms[:, b:b + 1], ss[:, b:b + 1], 1.0 / D, EPS, ALU.mult, ALU.add).then_inc(sem("fin_ms"), 1)
                dve.wait_ge(sem("fin_root"), b + 1)
                link(dve.reciprocal(rinv[:, b:b + 1], rms[:, b:b + 1]))
                dve.wait_ge(sem("nfin_landed"), 16)
                dve.scalar_tensor_tensor(x, x, rinv[:, b:b + 1], nfin[:, :], ALU.mult, ALU.mult).then_inc(
                    sem("out_ready"), 1)


def tables():
    f = np.float32
    pos, half = np.arange(T, dtype=f), P // 2
    freq = (f(10000.0) ** (-np.arange(0, P, 2, dtype=f) / f(P))).astype(f)
    ang = pos[:, None] * freq[None, :]
    rope = np.stack([np.cos(ang), np.sin(ang)], 1).astype(f).reshape(NB, P, 2, half).transpose(1, 0, 2, 3)
    lg = np.log1p(-np.exp2(-5.0 - np.arange(HEADS, dtype=np.float64)))
    k = np.arange(P)
    diff = k[None, :] - k[:, None]
    decay = np.where(diff[:, None, :] >= 0, np.exp(lg[None, :, None] * np.maximum(diff, 0)[:, None, :]), 0.0) * P ** -0.5
    xi = np.exp(lg[None, :] * (k[:, None] + 1))
    zeta = np.exp(lg[None, :] * (P - 1 - k[:, None])) * P ** -0.5
    rows = T // GRID_W
    pool = np.zeros((P, len(PW), NB, T))
    for g, w in enumerate(PW):
        def box(n):
            i = np.arange(n)
            lo, hi = np.clip(i - w // 2, 0, n), np.clip(i - w // 2 + w, 0, n)
            return ((i[None, :] >= lo[:, None]) & (i[None, :] < hi[:, None])).astype(np.float64)
        m = np.kron(box(rows), box(GRID_W))
        m = m / m.sum(1, keepdims=True) - np.eye(T)
        pool[:, g] = m.T.reshape(NB, P, T).transpose(1, 0, 2)
    mask = np.stack([np.where(diff >= 0, 0.0, -1e30), np.where(diff <= 0, 0.0, -1e30)], 1)
    sel = np.zeros((P, 2))
    sel[[0, 2], 0] = sel[[1, 3], 1] = 1.0
    out = {"rope": rope, "decay": decay, "pool_t": pool, "mask": mask, "ident": np.eye(P), "xi": xi, "zeta": zeta, "sel": sel,
           "iota": np.tile(np.arange(TOPK), (P, 1))}
    return {n: np.ascontiguousarray(v, dtype=f) for n, v in out.items()}


def chunks(w, rows_first=False):
    k, n = w.shape
    c = w.reshape(k // (CK * P), CK, P, n // CW, CW)
    c = c.transpose(0, 3, 2, 1, 4) if rows_first else c.transpose(3, 0, 2, 1, 4)
    return c.reshape(c.shape[0], c.shape[1], P, CK * CW)


def layout(v):
    t = tables()
    one = {n: np.asarray(x) for n, x in v.items()}
    first = {n: x[0] for n, x in one.items() if n not in ("x", "final_norm_w", "c_ctx_2", "ctx_2", "c_2", "norm_final_2")}
    stream = np.empty((NCH, P, CK * CW), np.float32)

    def put(at, c):
        c = c.reshape(-1, P, CK * CW)
        stream[at:at + len(c)] = c

    w2 = first["w_in_2"]
    put(S_IN, chunks(first["w_in"]))
    put(S_OUT, chunks(first["w_out"]))
    gate, up, down = chunks(first["w_ffn_gate"]), chunks(first["w_ffn_up"]), chunks(first["w_ffn_down"], True)
    ada = chunks(first["ada_w_2"])
    at = S_FFN
    for i in range(FT + 1):
        rest = {"g": list(gate[i]), "u": list(up[i])} if i < FT else {}
        rest["a"] = list(ada[ADA_STEP * i:ADA_STEP * (i + 1)].reshape(-1, P, CK * CW))
        rest["d"] = list(down[i - 1]) if i else []
        for kind in FF_FIRST if i == 0 else FF_STEP if i < FT else FF_LAST:
            stream[at] = rest[kind].pop(0)
            at += 1
    put(S_CTX, chunks(w2[:, O_K:O_G]))
    put(S_IN2, chunks(w2[:, :O_G])[list(W2_ORDER)])
    put(S_OUT2, chunks(first["w_out_2"]))
    put(S_WQ, chunks(first["peer_wq_2"]))

    def down_cols(x):
        return np.ascontiguousarray(x.reshape(-1, P).T)

    parts = {"ln1": down_cols(first["ln1_w"]), "ln2": down_cols(first["ln2_w"]), "ba": down_cols(first["gate_a_b"]),
             "bx": down_cols(first["gate_x_b"]), "conv": down_cols(first["conv_w"]), "convb": down_cols(first["conv_b"]),
             "lam": down_cols(first["lru_lambda"]), "gnw": down_cols(first["ret_gn_w"]), "nmix": down_cols(first["norm_mix_2"]),
             "nffn": down_cols(first["norm_ffn_2"]), "ada_b": down_cols(first["ada_b_2"]),
             "qkconv": down_cols(first["qk_conv_2"]), "mlnorm": down_cols(first["mlstm_norm_2"]),
             "pscale": down_cols(first["pool_scale_2"]), "c": down_cols(one["c_2"]), "cctx": down_cols(one["c_ctx_2"]),
             "sgub": down_cols(first["sgu_b_2"]), "xi": t["xi"], "zeta": t["zeta"], "sel": t["sel"], "iota": t["iota"]}
    cols = np.zeros((P, NCOL), np.float32)
    for name, x in parts.items():
        o, w = COL[name]
        cols[:, o:o + w] = x
    o, w = COL["bgate"]
    cols[0:MH, o:o + w] = first["b_gate_2"].reshape(4, MH).T

    def c(x):
        return np.ascontiguousarray(x)

    return {
        "x": one["x"], "ctx": one["ctx_2"], "wstream": stream, "cols": cols, "ident": t["ident"],
        "wa": c(first["gate_a_w"].transpose(1, 0, 2)), "wx": c(first["gate_x_w"].transpose(1, 0, 2)),
        "decay": t["decay"], "rope": t["rope"], "pool_t": t["pool_t"], "mask": t["mask"],
        "sgu_w": c(first["sgu_w_2"].transpose(2, 0, 1)), "pool_w": c(first["pool_w_2"].transpose(1, 0, 2)),
        "keys": c(first["peer_keys_2"].transpose(2, 0, 1)),
        "wg": c(w2[:, O_G:].reshape(KT, P, NG).transpose(1, 0, 2)),
        "fnw": one["final_norm_w"], "nfin": one["norm_final_2"], "sgu_n": first["sgu_norm_2"],
        "u_tab": first["peer_u_2"], "v_tab": first["peer_v_2"],
    }


def kernel(**inputs):
    import concourse.bacc as bacc
    from concourse.bass_utils import run_bass_kernel_spmd

    nc = bacc.Bacc("TRN2", target_bir_lowering=False, num_devices=1)
    arrays = {f"in_{n}_dram": np.ascontiguousarray(x) for n, x in layout(inputs).items()}
    args = {n[3:-5]: nc.dram_tensor(n, x.shape, mybir.dt.from_np(x.dtype), kind="ExternalInput").ap()
            for n, x in arrays.items()}
    out = nc.dram_tensor("out_dram", (1, T, D), F32, kind="ExternalOutput").ap()
    build(nc, args, out)
    return run_bass_kernel_spmd(nc, [arrays], core_ids=[0]).results[0]["out_dram"]
```
